# Optimizing a Trainium2 kernel written in Bass

```python
import jax, jax.numpy as jnp
from jax import lax
import numpy as np

D_MODEL = 1024
BATCH = 1
SEQ = 512
DEPTH = 1

CHUNK = 64
Q_BLOCK = 128
EPS = 1e-6

D_MIX = D_MODEL
SB_WIDTH = D_MIX // 2
SB_HEADS = 8
SB_HEAD_DIM = SB_WIDTH // SB_HEADS
GLA_WIDTH = D_MIX - SB_WIDTH
GLA_HEADS = 4
GLA_DV = GLA_WIDTH // GLA_HEADS
GLA_DK = GLA_DV // 2
GLA_KEY_WIDTH = GLA_HEADS * GLA_DK
GLA_GATE_RANK = 16
GLA_GATE_TAU = 16.0

IN_SIZES = (SB_WIDTH, SB_WIDTH, SB_WIDTH,
            GLA_KEY_WIDTH, GLA_KEY_WIDTH, GLA_WIDTH,
            GLA_GATE_RANK,
            GLA_WIDTH)
D_IN_PROJ = SB_WIDTH * 3 + GLA_KEY_WIDTH * 2 + GLA_WIDTH + GLA_GATE_RANK + GLA_WIDTH

PEER_HEADS = 8
PEER_N_KEYS = 128
PEER_N_EXPERTS = PEER_N_KEYS * PEER_N_KEYS
PEER_QUERY_DIM = 256
PEER_HALF = PEER_QUERY_DIM // 2
PEER_TOPK = 16
PEER_TOKEN_BLOCK = 128

kernel_name = "hybrid_sb_gla_peer_adaln_block"

def _rms(x):
    x32 = x.astype(jnp.float32)
    return (x32 * lax.rsqrt(jnp.mean(x32 * x32, axis=-1, keepdims=True) + EPS)).astype(x.dtype)

def _split_cols(t, sizes):
    outs, start = [], 0
    for s in sizes:
        outs.append(t[..., start:start + s])
        start += s
    return outs

def _heads(t, n_heads):
    b, s, _ = t.shape
    return t.reshape(b, s, n_heads, -1).transpose(0, 2, 1, 3)

def _merge_heads(t):
    b, n, s, d = t.shape
    return t.transpose(0, 2, 1, 3).reshape(b, s, n * d)

def stick_breaking_attention(q, k, v):
    b, h, s, dh = q.shape
    scale = dh ** -0.5
    n_blocks = s // Q_BLOCK
    key_pos = jnp.arange(s)

    def block(i):
        start = i * Q_BLOCK
        qb = lax.dynamic_slice_in_dim(q, start, Q_BLOCK, axis=2)
        z = jnp.einsum('bhtd,bhsd->bhts', qb, k).astype(jnp.float32) * scale
        q_pos = start + jnp.arange(Q_BLOCK)
        causal = key_pos[None, :] < q_pos[:, None]
        log_beta = jax.nn.log_sigmoid(z)
        log_keep = jnp.where(causal, jax.nn.log_sigmoid(-z), 0.0)
        suffix = lax.cumsum(log_keep, axis=3, reverse=True) - log_keep
        w = jnp.where(causal, jnp.exp(log_beta + suffix), 0.0)
        return jnp.einsum('bhts,bhsd->bhtd', w.astype(v.dtype), v)

    out = lax.map(block, jnp.arange(n_blocks))
    return out.transpose(1, 2, 0, 3, 4).reshape(b, h, s, dh)

def gla_chunked(q, k, v, log_a):
    b, h, s, dk = q.shape
    dv = v.shape[-1]
    n_chunks = s // CHUNK

    def to_chunks(t):
        return t.reshape(b, h, n_chunks, CHUNK, t.shape[-1]).transpose(2, 0, 1, 3, 4)

    qc, kc, vc, gc = (to_chunks(t) for t in (q * (dk ** -0.5), k, v, log_a))
    tri = jnp.tril(jnp.ones((CHUNK, CHUNK), dtype=bool))

    def step(state, inp):
        qi, ki, vi, gi = inp
        bcum = jnp.cumsum(gi.astype(jnp.float32), axis=2)
        b_last = bcum[:, :, -1:, :]
        diff = bcum[:, :, :, None, :] - bcum[:, :, None, :, :]
        decay = jnp.exp(jnp.where(tri[:, :, None], diff, -jnp.inf))
        scores = jnp.einsum('bhtd,bhsd,bhtsd->bhts', qi.astype(jnp.float32), ki.astype(jnp.float32), decay)
        o_intra = jnp.einsum('bhts,bhsv->bhtv', scores, vi.astype(jnp.float32))
        o_inter = jnp.einsum('bhtd,bhdv->bhtv', qi.astype(jnp.float32) * jnp.exp(bcum), state)
        k_dec = ki.astype(jnp.float32) * jnp.exp(b_last - bcum)
        new_state = state * jnp.exp(b_last[:, :, 0, :])[..., None] + jnp.einsum('bhsd,bhsv->bhdv', k_dec, vi.astype(jnp.float32))
        return new_state, o_intra + o_inter

    s0 = jnp.zeros((b, h, dk, dv), jnp.float32)
    _, out = lax.scan(step, s0, (qc, kc, vc, gc))
    return out.transpose(1, 2, 0, 3, 4).reshape(b, h, s, dv).astype(v.dtype)

def _head_rms(t, gain, n_heads):
    b, s, w = t.shape
    return _rms(t.reshape(b, s, n_heads, w // n_heads)).reshape(b, s, w) * gain

def peer_layer(h, w_q, keys_a, keys_b, expert_u, expert_v):
    t_tot, d = h.shape
    q = (h @ w_q).reshape(t_tot, PEER_HEADS, PEER_QUERY_DIM)
    q1, q2 = q[..., :PEER_HALF], q[..., PEER_HALF:]
    s1 = jnp.einsum('thd,hkd->thk', q1, keys_a)
    s2 = jnp.einsum('thd,hkd->thk', q2, keys_b)
    v1, i1 = lax.top_k(s1, PEER_TOPK)
    v2, i2 = lax.top_k(s2, PEER_TOPK)
    cand_s = (v1[..., :, None] + v2[..., None, :]).reshape(t_tot, PEER_HEADS, PEER_TOPK * PEER_TOPK)
    cand_i = (i1[..., :, None] * PEER_N_KEYS + i2[..., None, :]).reshape(t_tot, PEER_HEADS, PEER_TOPK * PEER_TOPK)
    top_s, pos = lax.top_k(cand_s, PEER_TOPK)
    idx = jnp.take_along_axis(cand_i, pos, axis=-1)
    gates = jax.nn.softmax(top_s.astype(jnp.float32), axis=-1).astype(h.dtype)

    n_blocks = t_tot // PEER_TOKEN_BLOCK

    def block(args):
        hb, ib, gb = args
        u = expert_u[ib]
        act = jax.nn.gelu(jnp.einsum('td,thkd->thk', hb, u), approximate=False)
        vv = expert_v[ib]
        return jnp.einsum('thk,thkd->td', gb * act, vv)

    out = lax.map(block, (h.reshape(n_blocks, PEER_TOKEN_BLOCK, d),
                          idx.reshape(n_blocks, PEER_TOKEN_BLOCK, PEER_HEADS, PEER_TOPK),
                          gates.reshape(n_blocks, PEER_TOKEN_BLOCK, PEER_HEADS, PEER_TOPK)))
    return out.reshape(t_tot, d)

def setup_inputs(seed: int = 0) -> dict:
    key = jax.random.key(seed)
    ks = jax.random.split(key, 16)
    d = D_MODEL
    nrm = jax.random.normal
    return {
        "x": nrm(ks[0], (BATCH, SEQ, d), jnp.float32),
        "c": nrm(ks[1], (BATCH, d), jnp.float32),
        "w_ada": nrm(ks[2], (DEPTH, d, 6 * d), jnp.float32) * (0.5 * d ** -0.5),
        "b_ada": nrm(ks[3], (DEPTH, 6 * d), jnp.float32) * 0.05,
        "w_in": nrm(ks[4], (DEPTH, d, D_IN_PROJ), jnp.float32) * d ** -0.5,
        "w_gla_gate_up": nrm(ks[5], (DEPTH, GLA_GATE_RANK, GLA_KEY_WIDTH), jnp.float32) * GLA_GATE_RANK ** -0.5,
        "b_gla_gate": nrm(ks[6], (DEPTH, GLA_KEY_WIDTH), jnp.float32) * 0.1,
        "g_sb_norm": 1.0 + 0.02 * nrm(ks[7], (DEPTH, SB_WIDTH), jnp.float32),
        "g_gla_norm": 1.0 + 0.02 * nrm(ks[8], (DEPTH, GLA_WIDTH), jnp.float32),
        "w_out": nrm(ks[9], (DEPTH, D_MIX, d), jnp.float32) * D_MIX ** -0.5,
        "w_peer_q": nrm(ks[10], (DEPTH, d, PEER_HEADS * PEER_QUERY_DIM), jnp.float32) * d ** -0.5,
        "peer_keys_a": nrm(ks[11], (DEPTH, PEER_HEADS, PEER_N_KEYS, PEER_HALF), jnp.float32) * PEER_HALF ** -0.5,
        "peer_keys_b": nrm(ks[12], (DEPTH, PEER_HEADS, PEER_N_KEYS, PEER_HALF), jnp.float32) * PEER_HALF ** -0.5,
        "peer_u": nrm(ks[13], (DEPTH, PEER_N_EXPERTS, d), jnp.float32) * d ** -0.5,
        "peer_v": nrm(ks[14], (DEPTH, PEER_N_EXPERTS, d), jnp.float32) * PEER_HEADS ** -0.5,
        "g_final": 1.0 + 0.02 * nrm(ks[15], (d,), jnp.float32),
    }

def reference(x, c, w_ada, b_ada, w_in, w_gla_gate_up, b_gla_gate, g_sb_norm, g_gla_norm,
              w_out, w_peer_q, peer_keys_a, peer_keys_b, peer_u, peer_v, g_final):
    b, s, d = x.shape
    c_act = jax.nn.silu(c)
    for l in range(DEPTH):
        mod = (c_act @ w_ada[l] + b_ada[l])[:, None, :]
        shift1, scale1, gate1, shift2, scale2, gate2 = _split_cols(mod, (d,) * 6)

        h = _rms(x) * (1.0 + scale1) + shift1
        proj = h @ w_in[l]
        sb_q, sb_k, sb_v, g_q, g_k, g_v, g_lr, g_r = _split_cols(proj, IN_SIZES)

        sb_out = stick_breaking_attention(_heads(sb_q, SB_HEADS), _heads(sb_k, SB_HEADS), _heads(sb_v, SB_HEADS))
        sb_out = _head_rms(_merge_heads(sb_out), g_sb_norm[l], SB_HEADS)

        log_a = jax.nn.log_sigmoid((g_lr @ w_gla_gate_up[l] + b_gla_gate[l]).astype(jnp.float32)) / GLA_GATE_TAU
        gla_out = gla_chunked(_heads(g_q, GLA_HEADS), _heads(g_k, GLA_HEADS), _heads(g_v, GLA_HEADS),
                              _heads(log_a, GLA_HEADS))
        gla_out = _head_rms(_merge_heads(gla_out), g_gla_norm[l], GLA_HEADS) * jax.nn.silu(g_r)

        mixed = jnp.concatenate([sb_out, gla_out], axis=-1) @ w_out[l]
        x = x + gate1 * mixed

        h2 = _rms(x) * (1.0 + scale2) + shift2
        y = peer_layer(h2.reshape(b * s, d), w_peer_q[l], peer_keys_a[l], peer_keys_b[l], peer_u[l], peer_v[l])
        x = x + gate2 * y.reshape(b, s, d)
    return _rms(x) * g_final


_drawn_inputs = setup_inputs


def setup_inputs(seed=0):
    import zlib

    import numpy as np

    out = dict(_drawn_inputs(seed))
    spreads = {}
    factors = {'b_gla_gate': 6.65,
     'g_sb_norm': 125.22,
     'g_gla_norm': 196.848,
     'g_final': 23.561,
     'w_peer_q': 8.0,
     'peer_keys_a': 8.0,
     'peer_keys_b': 8.0,
     'peer_u': 8.0,
     'peer_v': 8.0}
    for name, (base, spread) in spreads.items():
        noise = np.random.default_rng([zlib.crc32(name.encode()), seed]).standard_normal(out[name].shape)
        drawn = base * np.exp(spread * noise) if base else spread * noise
        out[name] = __import__('jax').numpy.asarray(drawn.astype(out[name].dtype))
    for name, factor in factors.items():
        out[name] = (out[name] * factor).astype(out[name].dtype)
    return out
```

```python
from contextlib import ExitStack

import concourse.bass as bass
from concourse import mybir
from concourse.bass import ds

F32 = mybir.dt.float32
F32R = mybir.dt.float32r
U32 = mybir.dt.uint32
I32 = mybir.dt.int32
ALU = mybir.AluOpType
ACT = mybir.ActivationFunctionType
AX = mybir.AxisListType

P = 128
D, T = 1024, 512
KD = D // P
TB = T // P
EPS = 1e-6
SB_HEADS, SB_DH = 8, 64
GLA_HEADS, GLA_DK, GLA_DV, GLA_CHUNK, GLA_RANK, GLA_TAU = 4, 64, 128, 64, 16, 16.0
GLA_PAIRS = GLA_HEADS // 2
N_CHUNKS = T // GLA_CHUNK
PEER_HEADS, N_KEYS, TOPK = 8, 128, 16
SBQ, SBK, GLQ, GLK, GLR, N_PROJ = 0, 4, 8, 10, 12, 16
NEG = -3.0e38
PAIR_ROWS = [(a, TOPK // (a + 1)) for a in range(TOPK)]
PAIR_START = [sum(n for _, n in PAIR_ROWS[:a]) for a in range(TOPK)]
N_PAIRS = sum(n for _, n in PAIR_ROWS)
G_TOK = 64
G_TILES = T // G_TOK
GROUP = 8
N_GROUPS = N_KEYS // GROUP


def turns(eng, n, body):
    body(0)
    with eng.Fori(1, n) as i:
        body(i)


def wait_count(eng, sem, count):
    if not isinstance(count, int) or count > 0:
        eng.wait_ge(sem, count)


def mixer_front(nc, io, keep):
    with ExitStack() as ctx:
        sb = lambda n, s, d=F32: ctx.enter_context(nc.sbuf_tensor(n, s, d))
        pb = lambda n, s: ctx.enter_context(nc.psum_tensor(n, s, F32))
        sem = lambda n: ctx.enter_context(nc.semaphore(n))
        SLOTS, COLS = 3, 512
        N_COLS = 6 * D // COLS
        xT, hT, mod = keep["xT"], keep["hT"], keep["mod"]
        cT = sb("cT", [P, KD])
        c_act = sb("c_act", [P, KD])
        w_ada = [sb(f"w_ada{n}", [P, KD, COLS]) for n in range(SLOTS)]
        b_row = sb("b_row", [1, 6 * D])
        mod_row = sb("mod_row", [1, 6 * D])
        sq = sb("sq_x", [P, KD, T])
        scaled = sb("scaled_x", [P, 2, T])
        root = sb("root_x", [P, T])
        rstd = sb("rstd_x", [P, T])
        ps_row = [pb(f"ps_row{n}", [1, COLS]) for n in range(SLOTS)]
        ps_mod = pb("ps_mod", [P, 6 * KD])
        ps_sum = pb("ps_sum_x", [P, T])
        small_in, x_in = sem("small_in"), sem("x_in")
        w_in = [sem(f"w_ada_in{n}") for n in range(SLOTS)]
        row_done = [sem(f"row_done{n}") for n in range(SLOTS)]
        row_kept = [sem(f"row_kept{n}") for n in range(SLOTS)]
        consts, silu_done, mod_done, mod_kept = sem("consts"), sem("silu_done"), sem("mod_done"), sem("mod_kept")
        sq_done, sum_done, root_done, rstd_done = sem("sq_done"), sem("sum_done"), sem("root_done"), sem("rstd_done")
        scaled_done, h_done, eps_set = sem("scaled_done"), sem("h_done"), sem("eps_set")
        block = ctx.enter_context(nc.Block())

        @block.sync
        def _(sp):
            sp.dma_start(cT[:], io["cT"]).then_inc(small_in, 16)
            sp.dma_start(b_row[:], io["b_ada"]).then_inc(small_in, 16)
            sp.dma_start(keep["gains"][:], io["gains"]).then_inc(small_in, 16)
            sp.dma_start(xT[:], io["xT"]).then_inc(x_in, 16)
            def turn(i):
                for n in range(SLOTS):
                    wait_count(sp, row_done[n], i)
                    sp.dma_start(w_ada[n][:], io["w_ada"][ds(i * SLOTS + n, 1)].rearrange("o p k c -> (o p) k c")).then_inc(w_in[n], 16)

            turns(sp, N_COLS // SLOTS, turn)

        @block.gpsimd
        def _(pool):
            pool.memset(keep["ones"][:], 1.0).then_inc(consts, 1)
            pool.memset(keep["pair_ones"][:], 0.0).then_inc(consts, 1)
            pool.memset(keep["neg_ones"][:], -1.0).then_inc(consts, 1)
            pool.wait_ge(consts, 3)
            for e in range(2):
                pool.memset(keep["pair_ones"][64 * e:64 * e + 64, 64 * e:64 * e + 64], 1.0).then_inc(consts, 1)
                pool.wait_ge(consts, 4 + e)
            pool.affine_select(out=keep["ident"][:], in_=keep["ones"][:], compare_op=ALU.is_equal, fill=0.0, base=0,
                               pattern=[[-1, P]], channel_multiplier=1).then_inc(consts, 1)
            pool.affine_select(out=keep["neg_tri"][:], in_=keep["neg_ones"][:], compare_op=ALU.is_ge, fill=0.0, base=0,
                               pattern=[[-1, P]], channel_multiplier=1).then_inc(consts, 1)
            pool.iota(keep["iota"][:], pattern=[[1, P]], base=0, channel_multiplier=0,
                      allow_small_or_imprecise_dtypes=True).then_inc(consts, 1)
            pool.memset(keep["eps"][:], EPS).then_inc(consts, 1)

        @block.scalar
        def _(act):
            act.wait_ge(small_in, 48)
            act.activation(c_act[:], cT[:], ACT.Silu).then_inc(silu_done, 1)
            act.wait_ge(x_in, 16)
            for k in range(KD):
                act.activation(sq[:, k], xT[:, k], ACT.Square).then_inc(sq_done, 1)
            act.wait_ge(sum_done, 1)
            act.wait_ge(consts, 9)
            act.activation(root[:], ps_sum[:], ACT.Sqrt, bias=keep["eps"][:], scale=1.0 / D).then_inc(root_done, 1)

        @block.tensor
        def _(pe):
            pe.wait_ge(consts, 1)
            for k in range(KD):
                pe.wait_ge(sq_done, k + 1)
                last = pe.matmul(ps_sum[:], keep["ones"][:], sq[:, k], start=(k == 0), stop=(k == KD - 1))
            last.then_inc(sum_done, 1)
            pe.wait_ge(silu_done, 1)
            def turn(i):
                for n in range(SLOTS):
                    pe.wait_ge(w_in[n], i * 16 + 16)
                    wait_count(pe, row_kept[n], i)
                    for k in range(KD):
                        last = pe.matmul(ps_row[n][:], c_act[:, k:k + 1], w_ada[n][:, k], start=(k == 0), stop=(k == KD - 1))
                    last.then_inc(row_done[n], 1)

            turns(pe, N_COLS // SLOTS, turn)
            for n in range(SLOTS):
                pe.wait_ge(row_kept[n], N_COLS // SLOTS)
            for j in range(6 * KD):
                last = pe.matmul(ps_mod[:, j:j + 1], mod_row[0:1, j * P:(j + 1) * P], keep["ones"][0:1, 0:1], start=True, stop=True)
            last.then_inc(mod_done, 1)

        @block.vector
        def _(dve):
            dve.wait_ge(root_done, 1)
            dve.reciprocal(rstd[:], root[:]).then_inc(rstd_done, 1)
            with dve.Fori(0, N_COLS // SLOTS) as i:
                for n in range(SLOTS):
                    dve.wait_ge(row_done[n], i + 1)
                    dve.tensor_tensor(mod_row[:, ds((i * SLOTS + n) * COLS, COLS)], ps_row[n][:],
                                      b_row[:, ds((i * SLOTS + n) * COLS, COLS)], ALU.add).then_inc(row_kept[n], 1)
            dve.wait_ge(mod_done, 1)
            dve.tensor_copy(mod[:], ps_mod[:]).then_inc(mod_kept, 1)
            dve.wait_ge(mod_kept, 1)
            for part in (1, 4):
                cols = mod[:, part * KD:(part + 1) * KD]
                dve.tensor_scalar(cols, cols, 1.0, None, ALU.add).then_inc(mod_kept, 1)
            dve.wait_ge(mod_kept, 3)
            dve.wait_ge(rstd_done, 1)
            for k in range(KD):
                if k >= 2:
                    dve.wait_ge(h_done, k - 1)
                dve.tensor_tensor(scaled[:, k % 2], xT[:, k], rstd[:], ALU.mult).then_inc(scaled_done, 1)
                dve.wait_ge(scaled_done, k + 1)
                dve.tensor_scalar(hT[:, k], scaled[:, k % 2], mod[:, KD + k:KD + k + 1], mod[:, k:k + 1],
                                  ALU.mult, ALU.add).then_inc(h_done, 1)


def projections(nc, io, keep, t16, v8, lrT):
    with ExitStack() as ctx:
        sb = lambda n, s, d=F32: ctx.enter_context(nc.sbuf_tensor(n, s, d))
        pb = lambda n, s: ctx.enter_context(nc.psum_tensor(n, s, F32))
        sem = lambda n: ctx.enter_context(nc.semaphore(n))
        hT = keep["hT"]
        SLOTS = 4
        w = [sb(f"w_proj{n}", [P, KD, P]) for n in range(SLOTS)]
        wv = sb("w_values", [P, 2, KD, T])
        wl = sb("w_lr", [P, KD, GLA_RANK])
        ps = [pb(f"ps_proj{n}", [P, T]) for n in range(SLOTS)]
        ps_v = [pb(f"ps_val{n}", [P, T]) for n in range(3)]
        ps_l = pb("ps_lr", [GLA_RANK, T])
        w_in = [sem(f"w_proj_in{n}") for n in range(SLOTS)]
        prod = [sem(f"proj_done{n}") for n in range(SLOTS)]
        kept = [sem(f"proj_kept{n}") for n in range(SLOTS)]
        wv_in, wl_in, v_done, v_kept, l_done = sem("wv_in"), sem("wl_in"), sem("v_done"), sem("v_kept"), sem("l_done")
        block = ctx.enter_context(nc.Block())

        @block.sync
        def _(sp):
            def turn(i):
                for n in range(SLOTS):
                    wait_count(sp, prod[n], i)
                    sp.dma_start(w[n][:], io["w_proj"][ds(i * SLOTS + n, 1)].rearrange("o p k c -> (o p) k c")).then_inc(w_in[n], 16)

            turns(sp, N_PROJ // SLOTS, turn)

        @block.gpsimd
        def _(pool):
            pool.dma_start(wl[:], io["w_lr"]).then_inc(wl_in, 16)
            pool.dma_start(wv[:], io["w_values"]).then_inc(wv_in, 16)

        @block.tensor
        def _(pe):
            def turn(i):
                for n in range(SLOTS):
                    pe.wait_ge(w_in[n], i * 16 + 16)
                    wait_count(pe, kept[n], i)
                    for k in range(KD):
                        last = pe.matmul(ps[n][:], w[n][:, k], hT[:, k], start=(k == 0), stop=(k == KD - 1))
                    last.then_inc(prod[n], 1)

            turns(pe, N_PROJ // SLOTS, turn)
            pe.wait_ge(wl_in, 16)
            for k in range(KD):
                last = pe.matmul(ps_l[:], wl[:, k], hT[:, k], start=(k == 0), stop=(k == KD - 1))
            last.then_inc(l_done, 1)
            pe.wait_ge(wv_in, 16)
            for g in range(2):
                for b in range(TB):
                    n = g * TB + b
                    if n >= 3:
                        pe.wait_ge(v_kept, n - 2)
                    for k in range(KD):
                        last = pe.matmul(ps_v[n % 3][:], hT[:, k, b * P:(b + 1) * P], wv[:, g, k], start=(k == 0), stop=(k == KD - 1))
                    last.then_inc(v_done, 1)

        @block.scalar
        def _(act):
            with act.Fori(0, N_PROJ // SLOTS) as i:
                for n in range(SLOTS):
                    act.wait_ge(prod[n], i + 1)
                    act.copy(t16[:, ds(i * SLOTS + n, 1)], ps[n][:].rearrange("p (o t) -> p o t", o=1)).then_inc(kept[n], 1)
            act.wait_ge(l_done, 1)
            act.copy(lrT[:], ps_l[:]).then_inc(l_done, 1)

        @block.vector
        def _(dve):
            for n in range(SLOTS):
                dve.wait_ge(kept[n], 1)
                dve.tensor_scalar(t16[:, SBQ + n], t16[:, SBQ + n], SB_DH ** -0.5, None, ALU.mult)
            for n in range(2 * TB):
                dve.wait_ge(v_done, n + 1)
                dve.tensor_copy(v8[:, n // TB, n % TB], ps_v[n % 3][:]).then_inc(v_kept, 1)


def stick_breaking(nc, keep, t16, v8, catT):
    with ExitStack() as ctx:
        sb = lambda n, s, d=F32: ctx.enter_context(nc.sbuf_tensor(n, s, d))
        pb = lambda n, s: ctx.enter_context(nc.psum_tensor(n, s, F32))
        sem = lambda n: ctx.enter_context(nc.semaphore(n))
        NU, ZB = SB_HEADS * TB, 6
        mag = sb("z_mag", [P, 2, T])
        ez = sb("z_exp", [P, 2, T])
        lz = sb("z_log", [P, 2, T])
        soft = sb("softplus", [P, 2, TB, T])
        w = sb("sb_weights", [P, 2, TB, T])
        ps_z = [pb(f"ps_z{n}", [P, T]) for n in range(ZB)]
        ps_o = [pb(f"ps_o{n}", [P, T]) for n in range(2)]
        z_done, mag_done, ez_done, lz_done = sem("z_done"), sem("mag_done"), sem("ez_done"), sem("lz_done")
        soft_done, soft_masked, suffix_done = sem("soft_done"), sem("soft_masked"), sem("suffix_done")
        w_done, w_masked, o_done, o_kept = sem("w_done"), sem("w_masked"), sem("o_done"), sem("o_kept")
        block = ctx.enter_context(nc.Block())
        place = lambda u: (u // TB, TB - 1 - u % TB)
        LAG_SUM, LAG_OUT = 2, 6

        @block.tensor
        def _(pe):
            def scores(u):
                h, s = place(u)
                r, c = 64 * (h % 2), h // 2
                if u >= ZB:
                    pe.wait_ge(w_done, u - ZB + 1)
                pe.matmul(ps_z[u % ZB][:, s * P:T], t16[r:r + 64, SBK + c, s * P:(s + 1) * P], t16[r:r + 64, SBQ + c, s * P:T],
                          start=True, stop=True).then_inc(z_done, 1)

            def outputs(h):
                pe.wait_ge(w_masked, TB * h + TB)
                if h >= 4 and h % 2 == 0:
                    pe.wait_ge(o_kept, h // 2 - 1)
                for s in range(TB):
                    last = pe.matmul(ps_o[h // 2 % 2][64 * (h % 2):64 * (h % 2) + 64, s * P:T], v8[:, 0, s, h * 64:h * 64 + 64],
                                     w[:, h % 2, s, s * P:T], start=(s == 0), stop=(s == TB - 1))
                last.then_inc(o_done, 1)

            for u in range(NU + LAG_OUT):
                if u < NU:
                    scores(u)
                if LAG_SUM <= u < NU + LAG_SUM:
                    v = u - LAG_SUM
                    h, s = place(v)
                    pe.wait_ge(soft_masked, v + 1)
                    for s2 in range(s, TB):
                        last = pe.matmul(ps_z[v % ZB][:, s2 * P:T], keep["neg_tri" if s2 == s else "neg_ones"][:],
                                         soft[:, h % 2, s2, s2 * P:T], start=False, stop=(s2 == TB - 1), skip_group_check=True)
                    last.then_inc(suffix_done, 1)
                if u >= LAG_OUT and (u - LAG_OUT) % TB == TB - 1:
                    outputs((u - LAG_OUT) // TB)

        @block.scalar
        def _(act):
            def weights(u):
                h, s = place(u)
                act.wait_ge(suffix_done, u + 1)
                if h >= 2:
                    act.wait_ge(o_done, h - 1)
                act.activation(w[:, h % 2, s, s * P:T], ps_z[u % ZB][:, s * P:T], ACT.Exp).then_inc(w_done, 1)

            act.preload_act_table_set("natural_log_exp_and_others")
            for u in range(NU + 3):
                if u < NU:
                    h, s = place(u)
                    n = T - s * P
                    act.wait_ge(z_done, u + 1)
                    if u >= 2:
                        act.wait_ge(ez_done, u - 1)
                    act.activation(mag[:, u % 2, 0:n], ps_z[u % ZB][:, s * P:T], ACT.Abs).then_inc(mag_done, 1)
                    act.wait_ge(mag_done, u + 1)
                    if u >= 2:
                        act.wait_ge(lz_done, u - 1)
                    act.activation(ez[:, u % 2, 0:n], mag[:, u % 2, 0:n], ACT.Exp, scale=-1.0).then_inc(ez_done, 1)
                    act.wait_ge(ez_done, u + 1)
                    if u >= 2:
                        act.wait_ge(soft_done, u - 1)
                    act.activation(lz[:, u % 2, 0:n], ez[:, u % 2, 0:n], ACT.Ln, bias=1.0).then_inc(lz_done, 1)
                if u >= 3:
                    weights(u - 3)

        @block.vector
        def _(dve):
            def keep_outputs(p):
                dve.wait_ge(o_done, 2 * p + 2)
                dve.tensor_copy(catT[:, p], ps_o[p % 2][:]).then_inc(o_kept, 1)

            for u in range(NU):
                h, s = place(u)
                n = T - s * P
                dve.wait_ge(lz_done, u + 1)
                if h >= 2 and s == TB - 1:
                    dve.wait_ge(suffix_done, TB * (h - 1))
                dve.scalar_tensor_tensor(soft[:, h % 2, s, s * P:T], ps_z[u % ZB][:, s * P:T], 0.0, lz[:, u % 2, 0:n],
                                         ALU.max, ALU.add).then_inc(soft_done, 1)
                if h >= 3 and h % 2 == 1 and s == 0:
                    keep_outputs((h - 3) // 2)
            keep_outputs(SB_HEADS // 2 - 1)

        @block.gpsimd
        def _(pool):
            def mask(tile, h, s, done):
                diag = tile[:, h % 2, s, s * P:(s + 1) * P]
                pool.affine_select(out=diag, in_=diag, compare_op=ALU.is_gt, fill=0.0, base=0, pattern=[[1, P]],
                                   channel_multiplier=-1).then_inc(done, 1)

            for u in range(NU + 3):
                if u < NU:
                    pool.wait_ge(soft_done, u + 1)
                    mask(soft, *place(u), soft_masked)
                if u >= 3:
                    pool.wait_ge(w_done, u - 2)
                    mask(w, *place(u - 3), w_masked)


def gated_linear(nc, io, keep, t16, v8, lrT, catT):
    with ExitStack() as ctx:
        sb = lambda n, s, d=F32: ctx.enter_context(nc.sbuf_tensor(n, s, d))
        pb = lambda n, s: ctx.enter_context(nc.psum_tensor(n, s, F32))
        sem = lambda n: ctx.enter_context(nc.semaphore(n))
        C, NC = GLA_CHUNK, N_CHUNKS
        up = sb("gate_up", [GLA_RANK, GLA_PAIRS * P])
        b_gate = sb("b_gate", [P, GLA_PAIRS])
        restart = sb("restart", [P, T])
        causal = sb("gla_causal", [P, C])
        x = sb("gate_x", [P, GLA_PAIRS, T])
        mag = sb("gate_mag", [P, GLA_PAIRS, T])
        la = x
        bc = sb("b_cum16", [P, GLA_PAIRS, T])
        dm = sb("b_mid16", [P, GLA_PAIRS, T])
        dl = sb("b_last16", [P, GLA_PAIRS, T])
        e_q = sb("e_q", [P, GLA_PAIRS, T])
        e_k = dm
        e_b = sb("e_b", [P, GLA_PAIRS, T])
        e_l = dl
        carry = sb("chunk_decay", [P, GLA_PAIRS, NC])
        q_in = sb("q_intra", [P, GLA_PAIRS, T])
        q_st = sb("q_state", [P, GLA_PAIRS, T])
        k_in = sb("k_intra", [P, GLA_HEADS, T])
        k_dec = sb("k_decayed", [P, GLA_PAIRS, T])
        kt = sb("k_decayed_t", [P, GLA_PAIRS, NC, P])
        sc = sb("gla_scores", [P, GLA_HEADS, TB, P])
        st = sb("gla_state", [P, GLA_HEADS, 2, GLA_DV])
        ps_g = [pb(f"ps_gate{n}", [P, T]) for n in range(2)]
        ps_u = [pb(f"ps_upd{n}", [P, T]) for n in range(2)]
        ps_o = [pb(f"ps_gla_o{h}", [P, T]) for h in range(GLA_HEADS)]
        small_in, zeros, gate_done, x_done, link = sem("gla_small_in"), sem("gla_zeros"), sem("gate_done"), sem("x_done"), sem("gla_act_link")
        log_done, chain, exps, ops = sem("log_done"), sem("gla_dve_chain"), sem("exps"), sem("gla_operands")
        t_done, kt_done, s_done, sc_done = sem("kt_ps"), sem("kt_done"), sem("sc_ps"), sem("sc_done")
        u_done, st_done, inter, o_done = sem("upd_done"), sem("state_done"), sem("inter_done"), sem("gla_o_done")
        block = ctx.enter_context(nc.Block())
        upd_bank = lambda p, c: (ps_u, ps_g)[c % 2][p]

        @block.sync
        def _(sp):
            sp.dma_start(up[:], io["gate_up"]).then_inc(small_in, 16)
            sp.dma_start(b_gate[:], io["b_gate"]).then_inc(small_in, 16)

        @block.gpsimd
        def _(pool):
            for tile in (k_in, kt, sc, st):
                pool.memset(tile[:], 0.0).then_inc(zeros, 1)
            pool.memset(restart[:], 1.0).then_inc(zeros, 1)
            pool.memset(causal[:], 1.0).then_inc(zeros, 1)
            pool.wait_ge(zeros, 6)
            pool.memset(restart[:].rearrange("p (c t) -> p c t", c=NC)[:, :, 0:1], 0.0).then_inc(zeros, 1)
            for o in range(2):
                pool.wait_ge(zeros, 7 + o)
                half = causal[64 * o:64 * o + 64, :]
                pool.affine_select(out=half, in_=half, compare_op=ALU.is_ge, fill=0.0, base=0, pattern=[[1, C]],
                                   channel_multiplier=-1).then_inc(zeros, 1)

        @block.scalar
        def _(act):
            act.wait_ge(small_in, 32)
            for p in range(GLA_PAIRS):
                act.wait_ge(gate_done, p + 1)
                act.activation(x[:, p], ps_g[p][:], ACT.Identity, bias=b_gate[:, p:p + 1]).then_inc(x_done, 1)
            act.wait_ge(x_done, GLA_PAIRS)
            act.activation(mag[:], x[:], ACT.Abs).then_inc(link, 1)
            act.wait_ge(link, 1)
            act.activation(mag[:], mag[:], ACT.Exp, scale=-1.0).then_inc(link, 1)
            act.wait_ge(link, 2)
            act.activation(mag[:], mag[:], ACT.Ln, bias=1.0).then_inc(log_done, 1)
            act.wait_ge(chain, 2 + 3 * GLA_PAIRS)
            act.activation(e_q[:], dm[:], ACT.Exp, scale=1.0 / GLA_TAU).then_inc(exps, 1)
            act.wait_ge(exps, 1)
            act.activation(e_k[:], dm[:], ACT.Exp, scale=-1.0 / GLA_TAU).then_inc(exps, 1)
            act.activation(e_b[:], bc[:], ACT.Exp, scale=1.0 / GLA_TAU).then_inc(exps, 1)
            act.activation(e_l[:], dl[:], ACT.Exp, scale=1.0 / GLA_TAU).then_inc(exps, 1)
            last_row = bc[:].rearrange("p a (c t) -> p a c t", c=NC)[:, :, :, C - 1]
            act.activation(carry[:], last_row, ACT.Exp, scale=1.0 / GLA_TAU).then_inc(exps, 1)

        @block.vector
        def _(dve):
            done = [0]

            def link_next(ins):
                done[0] += 1
                ins.then_inc(chain, 1)
                dve.wait_ge(chain, done[0])

            dve.wait_ge(x_done, GLA_PAIRS)
            dve.wait_ge(log_done, 1)
            link_next(dve.tensor_scalar(la[:], x[:], 0.0, None, ALU.min))
            link_next(dve.tensor_tensor(la[:], la[:], mag[:], ALU.subtract))
            dve.wait_ge(zeros, 9)
            for p in range(GLA_PAIRS):
                link_next(dve.tensor_tensor_scan(bc[:, p], restart[:], la[:, p], 0.0, ALU.mult, ALU.add))
            view = lambda tile, p: tile[:, p].rearrange("p (c t) -> p c t", c=NC)
            for p in range(GLA_PAIRS):
                b = view(bc, p)
                mid = b[:, :, C // 2 - 1:C // 2].broadcast_to([P, NC, C])
                end = b[:, :, C - 1:C].broadcast_to([P, NC, C])
                link_next(dve.tensor_tensor(view(dm, p), b, mid, ALU.subtract))
                link_next(dve.tensor_tensor(view(dl, p), end, b, ALU.subtract))
            dve.wait_ge(exps, 5)
            scale = GLA_DK ** -0.5
            for p in range(GLA_PAIRS):
                dve.tensor_tensor(k_dec[:, p], t16[:, GLK + p], e_l[:, p], ALU.mult).then_inc(ops, 1)
                dve.scalar_tensor_tensor(q_in[:, p], t16[:, GLQ + p], scale, e_q[:, p], ALU.mult, ALU.mult).then_inc(ops, 1)
                dve.scalar_tensor_tensor(q_st[:, p], t16[:, GLQ + p], scale, e_b[:, p], ALU.mult, ALU.mult).then_inc(ops, 1)
                for e in range(2):
                    r = slice(64 * e, 64 * e + 64)
                    dve.tensor_tensor(k_in[r, 2 * p + e], t16[r, GLK + p], e_k[r, p], ALU.mult).then_inc(ops, 1)
            for p in range(GLA_PAIRS):
                dve.wait_ge(t_done, p + 1)
                for o in range(2):
                    r = slice(64 * o, 64 * o + 64)
                    src = ps_g[p][:].rearrange("p (b d) -> p b d", b=TB)
                    dst = kt[:, p].rearrange("p (b o) d -> p b o d", o=2)
                    dve.tensor_copy(dst[r, :, o, :], src[r]).then_inc(kt_done, 1)
            for h in range(GLA_HEADS):
                dve.wait_ge(s_done, h + 1)
                for o in range(2):
                    r = slice(64 * o, 64 * o + 64)
                    src = ps_o[h][:].rearrange("p (b t) -> p b t", b=TB)
                    m = causal[r].rearrange("p (o t) -> p o t", o=1).broadcast_to([64, TB, C])
                    dve.tensor_tensor(sc[r, h, :, o * C:(o + 1) * C], src[r, :, o * C:(o + 1) * C], m, ALU.mult).then_inc(sc_done, 1)
            for c in range(NC - 1):
                dve.wait_ge(u_done, 2 * c + 2)
                if c >= 2:
                    dve.wait_ge(inter, c - 1)
                if c >= 1:
                    dve.wait_ge(st_done, GLA_HEADS * c)
                for h in range(GLA_HEADS):
                    p, e = h // 2, h % 2
                    r = slice(64 * e, 64 * e + 64)
                    new, old = st[r, h, (c + 1) % 2], st[r, h, c % 2]
                    u = upd_bank(p, c)[r, e * P:(e + 1) * P]
                    if c == 0:
                        dve.tensor_copy(new, u).then_inc(st_done, 1)
                    else:
                        dve.scalar_tensor_tensor(new, old, carry[r, p, c:c + 1], u, ALU.mult, ALU.add).then_inc(st_done, 1)
            for h in range(GLA_HEADS):
                dve.wait_ge(o_done, 1)
                dve.tensor_copy(catT[:, TB + h], ps_o[h][:])

        @block.tensor
        def _(pe):
            pe.wait_ge(small_in, 32)
            for p in range(GLA_PAIRS):
                pe.matmul(ps_g[p][:], up[:, p * P:(p + 1) * P], lrT[:], start=True, stop=True).then_inc(gate_done, 1)
            pe.wait_ge(ops, 5 * GLA_PAIRS)
            for p in range(GLA_PAIRS):
                for b in range(TB):
                    last = pe.transpose(ps_g[p][:, b * P:(b + 1) * P], k_dec[:, p, b * P:(b + 1) * P], keep["ident"][:])
                last.then_inc(t_done, 1)
            for h in range(GLA_HEADS):
                for b in range(TB):
                    last = pe.matmul(ps_o[h][:, b * P:(b + 1) * P], k_in[:, h, b * P:(b + 1) * P],
                                     q_in[:, h // 2, b * P:(b + 1) * P], start=True, stop=True)
                last.then_inc(s_done, 1)
            pe.wait_ge(kt_done, 2 * GLA_PAIRS)
            pe.wait_ge(sc_done, 2 * GLA_HEADS)

            def update(c):
                if c >= 2:
                    pe.wait_ge(st_done, GLA_HEADS * (c - 1))
                for p in range(GLA_PAIRS):
                    pe.matmul(upd_bank(p, c)[:, 0:2 * P], kt[:, p, c], v8[:, 1, c // 2, p * 256:(p + 1) * 256],
                              start=True, stop=True).then_inc(u_done, 1)

            update(0)
            for c in range(NC):
                if c + 1 < NC - 1:
                    update(c + 1)
                if c % 2 == 0:
                    for h in range(GLA_HEADS):
                        pe.matmul(ps_o[h][:, c * C:(c + 2) * C], v8[:, 1, c // 2, h * P:(h + 1) * P], sc[:, h, c // 2],
                                  start=True, stop=False, skip_group_check=True)
                if c >= 1:
                    pe.wait_ge(st_done, GLA_HEADS * c)
                    for h in range(GLA_HEADS):
                        last = pe.matmul(ps_o[h][:, c * C:(c + 1) * C], st[:, h, c % 2], q_st[:, h // 2, c * C:(c + 1) * C],
                                         start=False, stop=(c % 2 == 1), skip_group_check=True)
                    last.then_inc(inter, 1)
            pe.wait_ge(inter, NC - 1)
            pe.nop().then_inc(o_done, 1)


def mixer_back(nc, io, keep, t16, catT):
    with ExitStack() as ctx:
        sb = lambda n, s, d=F32: ctx.enter_context(nc.sbuf_tensor(n, s, d))
        pb = lambda n, s: ctx.enter_context(nc.psum_tensor(n, s, F32))
        sem = lambda n: ctx.enter_context(nc.semaphore(n))
        xT, mod, gains = keep["xT"], keep["mod"], keep["gains"]
        h2 = keep["hT"]
        h_hi, h_lo = keep["h_hi"], keep["h_lo"]
        sq = sb("sq_heads", [P, 2, T])
        root = sb("root_heads", [P, 2, T])
        rstd = sb("rstd_heads", [P, 2, T])
        sig = sb("sig_r", [P, 4, T])
        sw = sb("swish_r", [P, 4, T])
        w = sb("w_out_all", [P, KD, KD, P])
        scaled = sb("scaled_2", [P, 2, T])
        ps_s = [pb(f"ps_hs{n}", [P, T]) for n in range(2)]
        ps_p = [pb(f"ps_mix{n}", [P, T]) for n in range(3)]
        ps_x = pb("ps_sum_2", [P, T])
        w_in, sq_done, sum_done, root_done, rstd_done = sem("w_out_in"), sem("hsq"), sem("hsum"), sem("hroot"), sem("hrstd")
        silu_done, cat_done, mix_done, x_done, link = sem("silu_r"), sem("cat_done"), sem("mix_done"), sem("x1_done"), sem("mb_link")
        sq2_done, sum2_done, root2_done, sc_done, h_done, hi_done = (
            sem("sq2"), sem("sum2"), sem("root2"), sem("scaled2"), sem("h2_done"), sem("hi_done"))
        lo_done = sem("lo_done")
        block = ctx.enter_context(nc.Block())

        @block.sync
        def _(sp):
            sp.dma_start(w[:], io["w_out"]).then_inc(w_in, 16)

        @block.scalar
        def _(act):
            act.activation(sig[:], t16[:, GLR:GLR + 4], ACT.Sigmoid).then_inc(silu_done, 1)
            for c in range(KD + 1):
                if c < KD:
                    if c >= 2:
                        act.wait_ge(sum_done, c - 1)
                    act.activation(sq[:, c % 2], catT[:, c], ACT.Square).then_inc(sq_done, 1)
                if c >= 1:
                    n = c - 1
                    act.wait_ge(sum_done, n + 1)
                    if n >= 2:
                        act.wait_ge(rstd_done, n - 1)
                    act.activation(root[:, n % 2], ps_s[n % 2][:], ACT.Sqrt, bias=keep["eps"][:],
                                   scale=1.0 / (SB_DH if n < 4 else GLA_DV)).then_inc(root_done, 1)
            for n in range(KD):
                act.wait_ge(x_done, n + 1)
                if n >= 2:
                    act.wait_ge(sum2_done, n - 1)
                else:
                    act.wait_ge(sum_done, KD)
                act.activation(sq[:, n % 2], xT[:, n], ACT.Square).then_inc(sq2_done, 1)
            act.wait_ge(sum2_done, KD)
            act.activation(root[:, 0], ps_x[:], ACT.Sqrt, bias=keep["eps"][:], scale=1.0 / D).then_inc(root2_done, 1)
            for k in range(KD):
                act.wait_ge(h_done, k + 1)
                act.copy(h_hi[:, k], h2[:, k]).then_inc(hi_done, 1)

        @block.tensor
        def _(pe):
            for c in range(KD):
                pe.wait_ge(sq_done, c + 1)
                if c >= 2:
                    pe.wait_ge(root_done, c - 1)
                pe.matmul(ps_s[c % 2][:], keep["pair_ones" if c < 4 else "ones"][:], sq[:, c % 2], start=True, stop=True).then_inc(sum_done, 1)
            pe.wait_ge(w_in, 16)
            pe.wait_ge(cat_done, KD)
            for n in range(KD + 1):
                if n < KD:
                    if n >= 3:
                        pe.wait_ge(x_done, n - 2)
                    for k in range(KD):
                        last = pe.matmul(ps_p[n % 3][:], w[:, n, k], catT[:, k], start=(k == 0), stop=(k == KD - 1))
                    last.then_inc(mix_done, 1)
                if n >= 1:
                    pe.wait_ge(sq2_done, n)
                    pe.matmul(ps_x[:], keep["ones"][:], sq[:, (n - 1) % 2], start=(n == 1), stop=(n == KD),
                              skip_group_check=True).then_inc(sum2_done, 1)

        @block.vector
        def _(dve):
            dve.wait_ge(silu_done, 1)
            dve.tensor_tensor(sw[:], sig[:], t16[:, GLR:GLR + 4], ALU.mult).then_inc(link, 1)
            for c in range(KD):
                dve.wait_ge(root_done, c + 1)
                if c >= 2:
                    dve.wait_ge(cat_done, c - 1)
                dve.reciprocal(rstd[:, c % 2], root[:, c % 2]).then_inc(rstd_done, 1)
                dve.wait_ge(rstd_done, c + 1)
                dve.scalar_tensor_tensor(catT[:, c], catT[:, c], gains[:, c:c + 1], rstd[:, c % 2], ALU.mult, ALU.mult)\
                   .then_inc(link if c >= 4 else cat_done, 1)
                if c >= 4:
                    dve.wait_ge(link, c - 2)
                    dve.tensor_tensor(catT[:, c], catT[:, c], sw[:, c - 4], ALU.mult).then_inc(cat_done, 1)
            for n in range(KD):
                dve.wait_ge(mix_done, n + 1)
                dve.scalar_tensor_tensor(xT[:, n], ps_p[n % 3][:], mod[:, 2 * KD + n:2 * KD + n + 1], xT[:, n],
                                         ALU.mult, ALU.add).then_inc(x_done, 1)
            dve.wait_ge(root2_done, 1)
            dve.reciprocal(rstd[:, 0], root[:, 0]).then_inc(rstd_done, 1)
            dve.wait_ge(rstd_done, KD + 1)
            dve.wait_ge(x_done, KD)
            for k in range(KD):
                if k >= 2:
                    dve.wait_ge(h_done, k - 1)
                dve.tensor_tensor(scaled[:, k % 2], xT[:, k], rstd[:, 0], ALU.mult).then_inc(sc_done, 1)
                dve.wait_ge(sc_done, k + 1)
                dve.tensor_scalar(h2[:, k], scaled[:, k % 2], mod[:, 4 * KD + k:4 * KD + k + 1], mod[:, 3 * KD + k:3 * KD + k + 1],
                                  ALU.mult, ALU.add).then_inc(h_done, 1)
                if k >= 1:
                    dve.wait_ge(hi_done, k)
                    dve.tensor_tensor(h_lo[:, k - 1], h2[:, k - 1], h_hi[:, k - 1].bitcast(F32), ALU.subtract).then_inc(lo_done, 1)
            dve.wait_ge(hi_done, KD)
            dve.tensor_tensor(h_lo[:, KD - 1], h2[:, KD - 1], h_hi[:, KD - 1].bitcast(F32), ALU.subtract).then_inc(lo_done, 1)


def retrieval(nc, io, keep, picks):
    with ExitStack() as ctx:
        sb = lambda n, s, d=F32: ctx.enter_context(nc.sbuf_tensor(n, s, d))
        pb = lambda n, s: ctx.enter_context(nc.psum_tensor(n, s, F32))
        sem = lambda n: ctx.enter_context(nc.semaphore(n))
        hT = keep["hT"]
        expert, gate = picks
        w = [sb(f"w_query{s}", [P, KD, P]) for s in range(2)]
        keys = [sb(f"keys{s}", [P, N_KEYS]) for s in range(2)]
        q = [sb(f"query{s}", [P, T]) for s in range(2)]
        iota50 = sb("iota_pairs", [P, N_PAIRS])
        turn = sb("turn", [P, 1])
        scores = sb("scores", [P, 2, TB, N_KEYS])
        rest = sb("rest", [P, 2, TB, N_KEYS])
        top = sb("top_keys", [P, 2, TB, TOPK])
        idx = sb("top_idx", [P, 2, TB, TOPK], U32)
        num = sb("top_num", [P, 2, TB, TOPK])
        cand = sb("cand", [P, TB, N_PAIRS])
        cnum = sb("cand_num", [P, TB, N_PAIRS])
        crest = sb("cand_rest", [P, TB, N_PAIRS])
        ctop = sb("cand_top", [P, TB, TOPK])
        cpos = sb("cand_pos", [P, TB, TOPK], U32)
        cposf = sb("cand_posf", [P, TB, TOPK])
        hit = sb("hit", [P, TOPK, N_PAIRS])
        ex = sb("gate_exp", [P, TB, TOPK])
        tot = sb("gate_sum", [P, TB, 1])
        picked = sb("picked", [P, TB, TOPK])
        ps_q = [pb(f"ps_q{s}", [P, T]) for s in range(2)]
        ps_s = [pb(f"ps_s{s}", [P, T]) for s in range(2)]
        iota_done = sem("iota50_done")
        w_in, k_in = [sem(f"wq_in{s}") for s in range(2)], [sem(f"keys_in{s}") for s in range(2)]
        q_done, q_kept, s_done, s_used = sem("q_done"), sem("q_kept"), sem("s_done"), sem("s_used")
        s_copied, s_read = sem("s_copied"), sem("s_read")
        chain, e_in, e_done = sem("topk_chain"), sem("exp_in"), sem("exp_done")
        block = ctx.enter_context(nc.Block())

        @block.gpsimd
        def _(pool):
            pool.iota(iota50[:], pattern=[[1, N_PAIRS]], base=0, channel_multiplier=0,
                      allow_small_or_imprecise_dtypes=True).then_inc(iota_done, 1)

        @block.sync
        def _(sp):
            def turn(h):
                for s in range(2):
                    wait_count(sp, q_done, h * 2)
                    sp.dma_start(w[s][:], io["w_q"][ds(h * 2 + s, 1)].rearrange("o p k c -> (o p) k c")).then_inc(w_in[s], 16)
                for s in range(2):
                    wait_count(sp, s_done, h)
                    sp.dma_start(keys[s][:], io[("keys_a", "keys_b")[s]][ds(h, 1)].rearrange("o p k -> (o p) k")).then_inc(k_in[s], 16)

            turns(sp, PEER_HEADS, turn)

        @block.tensor
        def _(pe):
            def turn(h):
                for s in range(2):
                    pe.wait_ge(w_in[s], h * 16 + 16)
                    wait_count(pe, q_kept, h * 2)
                    for k in range(KD):
                        last = pe.matmul(ps_q[s][:], w[s][:, k], hT[:, k], start=(k == 0), stop=(k == KD - 1))
                    last.then_inc(q_done, 1)
                wait_count(pe, s_used, h)
                pe.wait_ge(q_kept, h * 2 + 2)
                for s in range(2):
                    pe.wait_ge(k_in[s], h * 16 + 16)
                    for b in range(TB):
                        last = pe.matmul(ps_s[s][:, b * P:(b + 1) * P], q[s][:, b * P:(b + 1) * P], keys[s][:], start=True, stop=True)
                last.then_inc(s_done, 1)

            turns(pe, PEER_HEADS, turn)

        @block.scalar
        def _(act):
            def turn(h):
                for s in range(2):
                    act.wait_ge(q_done, h * 2 + s + 1)
                    wait_count(act, s_done, h)
                    act.copy(q[s][:], ps_q[s][:]).then_inc(q_kept, 1)
                act.wait_ge(s_done, h + 1)
                wait_count(act, s_read, h)
                for s in range(2):
                    last = act.copy(scores[:, s], ps_s[s][:].rearrange("p (b k) -> p b k", b=TB))
                    last.then_inc(s_copied, 1)
                act.wait_ge(s_copied, h * 2 + 2)
                act.sem_inc(s_used, 1)
                act.wait_ge(e_in, h + 1)
                act.activation(ex[:], ex[:], ACT.Exp).then_inc(e_done, 1)

            turns(act, PEER_HEADS, turn)

        @block.vector
        def _(dve):
            dve.wait_ge(iota_done, 1)
            with dve.Fori(0, PEER_HEADS) as h:
                steps = [0]

                def stage(instructions):
                    for ins in instructions:
                        ins.then_inc(chain, 1)
                        steps[0] += 1
                    dve.wait_ge(chain, steps[0])

                score = lambda s, b: scores[:, s, b]
                both = [(s, b) for s in range(2) for b in range(TB)]
                dve.wait_ge(s_used, h + 1)
                dve.memset(turn[:], 0.0)
                dve.sem_clear(chain)
                stage(dve.max(top[:, s, b, 0:8], score(s, b)) for s, b in both)
                stage([f for s, b in both for f in (
                    dve.match_replace(rest[:, s, b], top[:, s, b, 0:8], score(s, b), NEG),
                    dve.max_index(idx[:, s, b, 0:8], top[:, s, b, 0:8], score(s, b)))])
                stage(dve.max(top[:, s, b, 8:16], rest[:, s, b]) for s, b in both)
                stage(dve.max_index(idx[:, s, b, 8:16], top[:, s, b, 8:16], rest[:, s, b]) for s, b in both)
                dve.sem_inc(s_read, 1)
                stage([dve.tensor_copy(num[:], idx[:])])
                stage([dve.tensor_scalar(num[:, 0], num[:, 0], float(N_KEYS), None, ALU.mult)])

                def pair_sums(out, of):
                    for a in range(8):
                        n = PAIR_ROWS[a][1]
                        yield dve.tensor_tensor(out[:, :, PAIR_START[a]:PAIR_START[a] + n],
                                                of[:, 0, :, a:a + 1].broadcast_to([P, TB, n]), of[:, 1, :, 0:n], ALU.add)
                    yield dve.tensor_tensor(out[:, :, PAIR_START[8]:N_PAIRS], of[:, 0, :, 8:16],
                                            of[:, 1, :, 0:1].broadcast_to([P, TB, 8]), ALU.add)

                stage([*pair_sums(cand, top), *pair_sums(cnum, num)])
                stage(dve.max(ctop[:, b, 0:8], cand[:, b]) for b in range(TB))
                stage([f for b in range(TB) for f in (
                    dve.match_replace(crest[:, b], ctop[:, b, 0:8], cand[:, b], NEG),
                    dve.max_index(cpos[:, b, 0:8], ctop[:, b, 0:8], cand[:, b]))])
                stage(dve.max(ctop[:, b, 8:16], crest[:, b]) for b in range(TB))
                stage(dve.max_index(cpos[:, b, 8:16], ctop[:, b, 8:16], crest[:, b]) for b in range(TB))
                stage([dve.tensor_tensor(ex[:], ctop[:], ctop[:, :, 0:1].broadcast_to([P, TB, TOPK]), ALU.subtract),
                       dve.tensor_copy(cposf[:], cpos[:])])
                dve.sem_inc(e_in, 1)
                for b in range(TB):
                    stage([dve.tensor_tensor(hit[:], cposf[:, b].rearrange("p (k o) -> p k o", o=1).broadcast_to([P, TOPK, N_PAIRS]),
                                             iota50[:].rearrange("p (o n) -> p o n", o=1).broadcast_to([P, TOPK, N_PAIRS]), ALU.is_equal)])
                    stage([dve.tensor_tensor(hit[:], hit[:], cnum[:, b].rearrange("p (o n) -> p o n", o=1).broadcast_to([P, TOPK, N_PAIRS]), ALU.mult)])
                    stage([dve.tensor_reduce(picked[:, b], hit[:], AX.X, ALU.add)])
                dve.wait_ge(e_done, h + 1)
                stage([dve.tensor_reduce(tot[:], ex[:], AX.X, ALU.add)])
                stage([dve.reciprocal(tot[:], tot[:])])
                stage([dve.tensor_tensor(gate[:, :, ds(h * TOPK, TOPK)], ex[:], tot[:].broadcast_to([P, TB, TOPK]), ALU.mult),
                       dve.tensor_copy(expert[:, :, ds(h * TOPK, TOPK)], picked[:])])


def dense_gates(nc, io, keep, picks, g_dram):
    with ExitStack() as ctx:
        sb = lambda n, s, d=F32: ctx.enter_context(nc.sbuf_tensor(n, s, d))
        pb = lambda n, s: ctx.enter_context(nc.psum_tensor(n, s, F32))
        sem = lambda n: ctx.enter_context(nc.semaphore(n))
        expert, gate = picks
        whole = sb("whole", [P, TB, P], I32)
        part = sb("part", [P, 2, TB, P], I32)
        ij = sb("ij", [P, 2, TB, P])
        cols = sb("pick_cols", [P, 3, T])
        EB, PB, PER = 8, 4, 4
        hot_i = [sb(f"hot_i{n}", [P, P]) for n in range(EB)]
        hot_j = [sb(f"hot_j{n}", [P, P]) for n in range(EB)]
        tile = [sb(f"g_tile{n}", [P, P, G_TOK]) for n in range(2)]
        ps_c = [pb(f"ps_cols{n}", [P, T]) for n in range(3)]
        ps_g = [pb(f"ps_g{n}", [P, PER, P]) for n in range(PB)]
        chain, t_done, c_done = sem("pick_chain"), sem("pick_t"), sem("pick_cols_done")
        hot, used, g_done, g_kept = sem("hot"), sem("hot_used"), sem("g_done"), sem("g_kept")
        stored = [sem(f"g_stored{n}") for n in range(2)]
        block = ctx.enter_context(nc.Block())
        BANKS = G_TOK // PER

        @block.vector
        def _(dve):
            done = [0]

            def link(ins):
                done[0] += 1
                ins.then_inc(chain, 1)
                dve.wait_ge(chain, done[0])

            link(dve.tensor_copy(whole[:], expert[:]))
            link(dve.tensor_scalar(part[:, 0], whole[:], 7, None, ALU.logical_shift_right))
            link(dve.tensor_scalar(part[:, 1], whole[:], N_KEYS - 1, None, ALU.bitwise_and))
            link(dve.tensor_copy(ij[:], part[:]))
            dve.wait_ge(t_done, 1)
            for n in range(3):
                dve.tensor_copy(cols[:, n], ps_c[n][:]).then_inc(c_done, 1)
            dve.wait_ge(c_done, 3)
            def turn(r):
                for n in range(EB):
                    wait_count(dve, used, r * EB)
                    t = r * EB + n
                    dve.tensor_scalar(hot_j[n][:], keep["iota"][:], cols[:, 1, ds(t, 1)], None, ALU.is_equal).then_inc(hot, 1)
                    dve.tensor_scalar(hot_i[n][:], keep["iota"][:], cols[:, 0, ds(t, 1)], cols[:, 2, ds(t, 1)],
                                      ALU.is_equal, ALU.mult).then_inc(hot, 1)

            turns(dve, T // EB, turn)

        @block.tensor
        def _(pe):
            pe.wait_ge(chain, 4)
            for n in range(3):
                for b in range(TB):
                    src = gate[:, b] if n == 2 else ij[:, n, b]
                    last = pe.transpose(ps_c[n][:, b * P:(b + 1) * P], src, keep["ident"][:])
            last.then_inc(t_done, 1)
            def turn(r):
                for m in range(PB):
                    wait_count(pe, g_kept, r * PB)
                    for o in range(PER):
                        n = (m * PER + o) % EB
                        pe.wait_ge(hot, (r * PB * PER + m * PER + o) * 2 + 2)
                        pe.matmul(ps_g[m][:, o], hot_j[n][:], hot_i[n][:], start=True, stop=True).then_inc(used, 1)
                    pe.sem_inc(g_done, 1)

            turns(pe, T // (PB * PER), turn)

        @block.scalar
        def _(act):
            def turn(r):
                for n in range(2):
                    wait_count(act, stored[n], r * 16)
                    for f in range(BANKS):
                        m = f % PB
                        act.wait_ge(used, (((r * 2 + n) * BANKS + f) + 1) * PER)
                        act.copy(tile[n][:, :, f * PER:(f + 1) * PER], ps_g[m][:].rearrange("p t i -> p i t")).then_inc(g_kept, 1)

            turns(act, G_TILES // 2, turn)

        @block.sync
        def _(sp):
            with sp.Fori(0, G_TILES // 2) as r:
                for n in range(2):
                    sp.wait_ge(g_kept, ((r * 2 + n) + 1) * BANKS)
                    sp.dma_start(g_dram[ds(r * 2 + n, 1)].rearrange("o p i t -> (o p) (i t)"),
                                 tile[n][:].rearrange("p i t -> p (i t)")).then_inc(stored[n], 16)
            for n in range(2):
                sp.wait_ge(stored[n], G_TILES // 2 * 16)


def experts(nc, io, keep, g_dram, yT):
    with ExitStack() as ctx:
        sb = lambda n, s, d=F32: ctx.enter_context(nc.sbuf_tensor(n, s, d))
        pb = lambda n, s: ctx.enter_context(nc.psum_tensor(n, s, F32))
        sem = lambda n: ctx.enter_context(nc.semaphore(n))
        h_hi, h_lo = keep["h_hi"], keep["h_lo"]
        HALF = GROUP // 2
        UR, US, VR, VS = 2, 2, 4, 4
        HC = D // 2
        u_raw = [sb(f"u_raw{n}", [P, KD, P]) for n in range(UR)]
        u_hi = [sb(f"u_hi{n}", [P, KD, P], F32R) for n in range(US)]
        u_lo = [sb(f"u_lo{n}", [P, KD, P], F32R) for n in range(US)]
        v_raw = [sb(f"v_raw{n}", [P, HC]) for n in range(VR)]
        v_hi = [sb(f"v_hi{n}", [P, HC], F32R) for n in range(VS)]
        v_lo = [sb(f"v_lo{n}", [P, HC], F32R) for n in range(VS)]
        gates = [sb(f"gates{n}", [P, G_TILES, HALF, G_TOK]) for n in range(2)]
        wt = [sb(f"act{n}", [P, T]) for n in range(HALF)]
        w_hi = [sb(f"w_hi{n}", [P, T], F32R) for n in range(GROUP)]
        w_lo = [sb(f"w_lo{n}", [P, T], F32R) for n in range(GROUP)]
        ps_a = [pb(f"ps_a{n}", [P, T]) for n in range(HALF)]
        ps_y = [pb(f"ps_y{n}", [P, T]) for n in range(4)]
        u_in = [sem(f"u_in{n}") for n in range(UR)]
        v_in = [sem(f"v_in{n}") for n in range(VR)]
        g_in = [sem(f"g_in{n}") for n in range(2)]
        uhi, ulo, vhi, vlo = sem("u_hi_done"), sem("u_lo_done"), sem("v_hi_done"), sem("v_lo_done")
        u_mul, v_mul, act_done, w_done, whi, wlo = sem("u_mul"), sem("v_mul"), sem("act_done"), sem("w_gated"), sem("w_hi_done"), sem("w_lo_done")
        y_kept, y_zero = sem("y_kept"), sem("y_zero")
        block = ctx.enter_context(nc.Block())

        def group_loop(eng, body):
            body(0, first=True)
            with eng.Fori(1, N_GROUPS - 1) as g:
                body(g)
            body(N_GROUPS - 1, last=True)

        def order(lift_u, lift_v, first_step, second_step, add_y, loop):
            g = 0
            for n in range(GROUP):
                lift_u(g, n)
                if n >= 1:
                    first_step(g, n - 1)
                if n >= 2:
                    second_step(g, n - 2)

            def body(g, first=False, last=False):
                lift_v(g, 0, 0)
                lift_v(g, 0, 1)
                first_step(g, GROUP - 1)
                second_step(g, GROUP - 2)
                lift_v(g, 0, 2)
                second_step(g, GROUP - 1)
                for n in range(3, GROUP):
                    lift_v(g, 0, n)
                if last:
                    add_y(g, 0)
                    for n in range(GROUP):
                        lift_v(g, 1, n)
                    add_y(g, 1)
                    return
                g1 = g + 1
                lift_u(g1, 0)
                lift_u(g1, 1)
                add_y(g, 0)
                first_step(g1, 0)
                lift_u(g1, 2)
                first_step(g1, 1)
                lift_u(g1, 3)
                first_step(g1, 2)
                lift_v(g, 1, 0)
                lift_v(g, 1, 1)
                first_step(g1, 3)
                lift_v(g, 1, 2)
                for n in range(3, GROUP):
                    lift_v(g, 1, n)
                    if n <= 6:
                        second_step(g1, n - 3)
                lift_u(g1, 4)
                lift_u(g1, 5)
                add_y(g, 1)
                first_step(g1, 4)
                lift_u(g1, 6)
                first_step(g1, 5)
                second_step(g1, 4)
                lift_u(g1, 7)
                first_step(g1, 6)
                second_step(g1, 5)

            loop(body)

        @block.sync
        def _(sp):
            def load_u(g, n):
                wait_count(sp, ulo, g * GROUP + n - UR + 1)
                sp.dma_start(u_raw[n % UR][:], io["u"][ds(g * GROUP + n, 1)].rearrange("o p k e -> (o p) k e")).then_inc(u_in[n % UR], 16)

            def load_g(g, half):
                wait_count(sp, w_done, g * GROUP + half * HALF - HALF)
                src = g_dram[:].rearrange("a p (q i) t -> q p a i t", i=HALF)[ds(g * 2 + half, 1)]
                sp.dma_start(gates[half][:], src.rearrange("o p a i t -> (o p) a i t")).then_inc(g_in[half], 16)

            def load_v(g, half, n, first=False):
                wait_count(sp, vlo, g * 2 * GROUP + half * GROUP + n - VR + 1)
                sp.dma_start(v_raw[n % VR][:], io["v"][ds(g * GROUP + n, 1)].rearrange("o p d -> (o p) d")[:, half * HC:(half + 1) * HC])\
                  .then_inc(v_in[n % VR], 16)

            for n in range(GROUP):
                if n % HALF == 0:
                    load_g(0, n // HALF)
                load_u(0, n)

            def group(g, first=False, last=False):
                for half in range(2):
                    for n in range(GROUP):
                        load_v(g, half, n, first)
                    if not last:
                        load_g(g + 1, half)
                        for n in range(half * HALF, half * HALF + HALF):
                            load_u(g + 1, n)

            group_loop(sp, group)

        @block.scalar
        def _(act):
            def split_u(g, n):
                act.wait_ge(u_in[n % UR], (g * (GROUP // UR) + n // UR + 1) * 16)
                wait_count(act, u_mul, g * GROUP + n - US + 1)
                wait_count(act, ulo, g * GROUP + n - US + 1)
                act.copy(u_hi[n % US][:], u_raw[n % UR][:]).then_inc(uhi, 1)

            def split_v(g, half, n):
                at = g * 2 * GROUP + half * GROUP + n
                act.wait_ge(v_in[n % VR], (g * (2 * GROUP // VR) + half * (GROUP // VR) + n // VR + 1) * 16)
                wait_count(act, v_mul, at - VS + 1)
                wait_count(act, vlo, at - VS + 1)
                act.copy(v_hi[n % VS][:], v_raw[n % VR][:]).then_inc(vhi, 1)

            def gelu(g, n):
                act.wait_ge(u_mul, g * GROUP + n + 1)
                wait_count(act, wlo, g * GROUP + n - HALF + 1)
                act.activation(wt[n % HALF][:], ps_a[n % HALF][:], ACT.Gelu).then_inc(act_done, 1)

            def w_high(g, n):
                act.wait_ge(w_done, g * GROUP + n + 1)
                if not (isinstance(g, int) and g == 0):
                    act.wait_ge(v_mul, g * 2 * GROUP - GROUP + n + 1)
                act.copy(w_hi[n][:], wt[n % HALF][:]).then_inc(whi, 1)

            order(split_u, split_v, gelu, w_high, lambda g, half: None, lambda body: group_loop(act, body))

        @block.vector
        def _(dve):
            def split_u(g, n):
                dve.wait_ge(uhi, g * GROUP + n + 1)
                wait_count(dve, u_mul, g * GROUP + n - US + 1)
                dve.tensor_tensor(u_lo[n % US][:], u_raw[n % UR][:], u_hi[n % US][:].bitcast(F32), ALU.subtract).then_inc(ulo, 1)

            def split_v(g, half, n):
                at = g * 2 * GROUP + half * GROUP + n
                dve.wait_ge(vhi, at + 1)
                wait_count(dve, v_mul, at - VS + 1)
                dve.tensor_tensor(v_lo[n % VS][:], v_raw[n % VR][:], v_hi[n % VS][:].bitcast(F32), ALU.subtract).then_inc(vlo, 1)

            def weigh(g, n):
                dve.wait_ge(act_done, g * GROUP + n + 1)
                dve.wait_ge(g_in[n // HALF], g * 16 + 16)
                w = wt[n % HALF][:].rearrange("p (a t) -> p a t", a=G_TILES)
                dve.tensor_tensor(w, w, gates[n // HALF][:, :, n % HALF], ALU.mult).then_inc(w_done, 1)

            def w_low(g, n):
                dve.wait_ge(whi, g * GROUP + n + 1)
                dve.tensor_tensor(w_lo[n][:], wt[n % HALF][:], w_hi[n][:].bitcast(F32), ALU.subtract).then_inc(wlo, 1)

            def add_y(g, half):
                dve.wait_ge(v_mul, g * 2 * GROUP + half * GROUP + GROUP)
                for c in range(4):
                    y = yT[:, half * 4 + c]
                    if isinstance(g, int) and g == 0:
                        dve.tensor_copy(y, ps_y[c][:]).then_inc(y_kept, 1)
                    else:
                        dve.tensor_tensor(y, y, ps_y[c][:], ALU.add).then_inc(y_kept, 1)

            def add_y_after(g, half):
                if not (isinstance(g, int) and g == 0):
                    dve.wait_ge(y_kept, g * 8 + half * 4 - 4)
                add_y(g, half)

            order(split_u, split_v, weigh, w_low, add_y_after, lambda body: group_loop(dve, body))

        @block.tensor
        def _(pe):
            def u_products(g, n):
                pe.wait_ge(ulo, g * GROUP + n + 1)
                wait_count(pe, act_done, g * GROUP + n - HALF + 1)
                for k in range(KD):
                    hi, lo = u_hi[n % US][:, k], u_lo[n % US][:, k]
                    pe.matmul(ps_a[n % HALF][:], hi, h_hi[:, k], start=(k == 0), stop=False)
                    pe.matmul(ps_a[n % HALF][:], hi, h_lo[:, k], start=False, stop=False)
                    last = pe.matmul(ps_a[n % HALF][:], lo, h_hi[:, k], start=False, stop=(k == KD - 1))
                last.then_inc(u_mul, 1)

            def v_products(g, half, n, first):
                at = g * 2 * GROUP + half * GROUP + n
                pe.wait_ge(vlo, at + 1)
                pe.wait_ge(wlo, g * GROUP + n + 1)
                if n == 0 and not (first and half == 0):
                    pe.wait_ge(y_kept, g * 8 + half * 4)
                for c in range(4):
                    hi, lo = v_hi[n % VS][:, c * P:(c + 1) * P], v_lo[n % VS][:, c * P:(c + 1) * P]
                    pe.matmul(ps_y[c][:], hi, w_hi[n][:], start=(n == 0), stop=False)
                    pe.matmul(ps_y[c][:], hi, w_lo[n][:], start=False, stop=False)
                    last = pe.matmul(ps_y[c][:], lo, w_hi[n][:], start=False, stop=(n == GROUP - 1))
                last.then_inc(v_mul, 1)

            for n in range(GROUP):
                u_products(0, n)

            def group(g, first=False, last=False):
                for half in range(2):
                    for n in range(GROUP):
                        v_products(g, half, n, first)
                    if not last:
                        for n in range(half * HALF, half * HALF + HALF):
                            u_products(g + 1, n)

            group_loop(pe, group)


def finish(nc, io, keep, yT):
    with ExitStack() as ctx:
        sb = lambda n, s, d=F32: ctx.enter_context(nc.sbuf_tensor(n, s, d))
        sem = lambda n: ctx.enter_context(nc.semaphore(n))
        xT, mod = keep["xT"], keep["mod"]
        sq = sb("sq_y", [P, KD, T])
        g_fin = sb("g_final", [P, KD])
        root = sb("root_y", [P, T])
        rstd = sb("rstd_y", [P, T])
        ps = ctx.enter_context(nc.psum_tensor("ps_sum_y", [P, T], F32))
        g_in, x_done, sq_done, sum_done, root_done, rstd_done, o_done, stored = (
            sem("gf_in"), sem("x2_done"), sem("sq_y_done"), sem("sum_y_done"), sem("root_y_done"), sem("rstd_y_done"), sem("out_done"), sem("stored"))
        block = ctx.enter_context(nc.Block())

        @block.sync
        def _(sp):
            sp.dma_start(g_fin[:], io["g_final"]).then_inc(g_in, 16)
            for k in range(KD):
                sp.wait_ge(o_done, k + 1)
                sp.dma_start(io["out"][:, k], yT[:, k]).then_inc(stored, 16)
            sp.wait_ge(stored, 16 * KD)

        @block.vector
        def _(dve):
            for k in range(KD):
                dve.scalar_tensor_tensor(xT[:, k], yT[:, k], mod[:, 5 * KD + k:5 * KD + k + 1], xT[:, k], ALU.mult, ALU.add)\
                   .then_inc(x_done, 1)
            dve.wait_ge(root_done, 1)
            dve.reciprocal(rstd[:], root[:]).then_inc(rstd_done, 1)
            dve.wait_ge(rstd_done, 1)
            dve.wait_ge(g_in, 16)
            dve.wait_ge(x_done, KD)
            for k in range(KD):
                dve.scalar_tensor_tensor(yT[:, k], xT[:, k], g_fin[:, k:k + 1], rstd[:], ALU.mult, ALU.mult).then_inc(o_done, 1)

        @block.scalar
        def _(act):
            for k in range(KD):
                act.wait_ge(x_done, k + 1)
                act.activation(sq[:, k], xT[:, k], ACT.Square).then_inc(sq_done, 1)
            act.wait_ge(sum_done, 1)
            act.activation(root[:], ps[:], ACT.Sqrt, bias=keep["eps"][:], scale=1.0 / D).then_inc(root_done, 1)

        @block.tensor
        def _(pe):
            for k in range(KD):
                pe.wait_ge(sq_done, k + 1)
                last = pe.matmul(ps[:], keep["ones"][:], sq[:, k], start=(k == 0), stop=(k == KD - 1))
            last.then_inc(sum_done, 1)


def program(nc, io, until=99, probe=None):
    with ExitStack() as top:
        sb = lambda n, s, d=F32: top.enter_context(nc.sbuf_tensor(n, s, d))
        keep = {
            "xT": sb("xT", [P, KD, T]), "mod": sb("mod", [P, 6 * KD]), "gains": sb("gains", [P, KD]),
            "ones": sb("ones", [P, P]), "neg_ones": sb("neg_ones", [P, P]), "pair_ones": sb("pair_ones", [P, P]),
            "ident": sb("ident", [P, P]), "neg_tri": sb("neg_tri", [P, P]), "iota": sb("iota", [P, P]), "eps": sb("eps", [P, 1]),
            "h_hi": sb("h_hi", [P, KD, T], F32R), "h_lo": sb("h_lo", [P, KD, T], F32R),
        }
        g_dram = nc.dram_tensor("gate_tiles", [G_TILES, P, N_KEYS, G_TOK], F32, kind="Internal").ap()
        with ExitStack() as front:
            fsb = lambda n, s, d=F32: front.enter_context(nc.sbuf_tensor(n, s, d))
            keep["hT"] = fsb("hT", [P, KD, T])
            mixer_front(nc, io, keep)
            if until >= 2:
                with ExitStack() as mix:
                    msb = lambda n, s: mix.enter_context(nc.sbuf_tensor(n, s, F32))
                    t16, v8, lrT, catT = (msb("t16", [P, N_PROJ, T]), msb("v8", [P, 2, TB, T]), msb("lrT", [GLA_RANK, T]),
                                          msb("catT", [P, KD, T]))
                    projections(nc, io, keep, t16, v8, lrT)
                    stick_breaking(nc, keep, t16, v8, catT)
                    gated_linear(nc, io, keep, t16, v8, lrT, catT)
                    if probe == "cat":
                        dump(nc, io["out"], catT)
                        return
                    mixer_back(nc, io, keep, t16, catT)
            if probe == "h2":
                dump(nc, io["out"], keep["hT"])
                return
            picks = (fsb("expert", [P, TB, P]), fsb("gate", [P, TB, P]))
            retrieval(nc, io, keep, picks)
            if probe == "picks":
                dump(nc, io["out"][:, 0], picks[0][:].rearrange("p a b -> p (a b)"), whole=False)
                dump(nc, io["out"][:, 1], picks[1][:].rearrange("p a b -> p (a b)"), whole=False)
                return
            dense_gates(nc, io, keep, picks, g_dram)
        with ExitStack() as back:
            yT = back.enter_context(nc.sbuf_tensor("yT", [P, KD, T], F32))
            experts(nc, io, keep, g_dram, yT)
            finish(nc, io, keep, yT)


def dump(nc, out, tile, whole=True):
    with ExitStack() as ctx:
        s = ctx.enter_context(nc.semaphore("dump"))
        block = ctx.enter_context(nc.Block())

        @block.sync
        def _(sp):
            sp.dma_start(out, tile[:] if whole else tile).then_inc(s, 16)
            sp.wait_ge(s, 16)


def kernel(**inputs):
    import numpy as np
    import concourse.bacc as bacc
    from concourse.bass_utils import run_bass_kernel_spmd

    nc = bacc.Bacc("TRN2", target_bir_lowering=False, num_devices=1)
    arrays = laid_out(np, inputs)
    io = {n: nc.dram_tensor(f"in_{n}", a.shape, mybir.dt.from_np(a.dtype), kind="ExternalInput").ap() for n, a in arrays.items()}
    io["out"] = nc.dram_tensor("out_0", (P, KD, T), F32, kind="ExternalOutput").ap()
    program(nc, io)
    r = run_bass_kernel_spmd(nc, [{f"in_{n}": a for n, a in arrays.items()}], core_ids=[0])
    out = r.results[0]["out_0"]
    return np.ascontiguousarray(out.transpose(2, 1, 0)).reshape(1, T, D)


def laid_out(np, inputs):
    get = lambda n: np.asarray(inputs[n])
    chunks = lambda w, n: w.reshape(KD, P, w.shape[1] // n, n).transpose(2, 1, 0, 3)
    cols = lambda v: v.reshape(-1, P).T
    w_in = get("w_in")[0]
    at = np.cumsum([0, 512, 512, 512, 256, 256, 512, GLA_RANK, 512])
    part = [w_in[:, a:b] for a, b in zip(at[:-1], at[1:])]
    sq, sk, sv, gq, gk, gv, lr, gr = part
    arrays = {
        "xT": get("x")[0].T.reshape(KD, P, T).transpose(1, 0, 2),
        "cT": cols(get("c")[0]),
        "w_ada": chunks(get("w_ada")[0], 512),
        "b_ada": get("b_ada"),
        "gains": np.concatenate([cols(get("g_sb_norm")[0]), cols(get("g_gla_norm")[0])], axis=1),
        "w_proj": chunks(np.concatenate([sq, sk, gq, gk, gr], axis=1), P),
        "w_lr": chunks(lr, GLA_RANK)[0],
        "w_values": chunks(np.concatenate([sv, gv], axis=1), T).transpose(1, 0, 2, 3),
        "gate_up": get("w_gla_gate_up")[0],
        "b_gate": cols(get("b_gla_gate")[0]),
        "w_out": chunks(get("w_out")[0], P).transpose(1, 0, 2, 3),
        "w_q": chunks(get("w_peer_q")[0], P),
        "keys_a": get("peer_keys_a")[0].transpose(0, 2, 1),
        "keys_b": get("peer_keys_b")[0].transpose(0, 2, 1),
        "u": get("peer_u")[0].reshape(N_KEYS, P, KD, P).transpose(0, 3, 2, 1),
        "v": get("peer_v")[0].reshape(N_KEYS, P, D),
        "g_final": cols(get("g_final")),
    }
    return {n: np.ascontiguousarray(a) for n, a in arrays.items()}
```

```python
from contextlib import ExitStack

import concourse.bass as bass
from concourse import mybir
from concourse.bass import ds

F32 = mybir.dt.float32
F32R = mybir.dt.float32r
U32 = mybir.dt.uint32
I32 = mybir.dt.int32
ALU = mybir.AluOpType
ACT = mybir.ActivationFunctionType
AX = mybir.AxisListType

P = 128
D, T = 1024, 512
KD = D // P
TB = T // P
EPS = 1e-6
SB_HEADS, SB_DH = 8, 64
GLA_HEADS, GLA_DK, GLA_DV, GLA_CHUNK, GLA_RANK, GLA_TAU = 4, 64, 128, 64, 16, 16.0
GLA_PAIRS = GLA_HEADS // 2
N_CHUNKS = T // GLA_CHUNK
PEER_HEADS, N_KEYS, TOPK = 8, 128, 16
SBQ, SBK, GLQ, GLK, GLR, N_PROJ = 0, 4, 8, 10, 12, 16
NEG = -3.0e38
PAIR_ROWS = [(a, TOPK // (a + 1)) for a in range(TOPK)]
PAIR_START = [sum(n for _, n in PAIR_ROWS[:a]) for a in range(TOPK)]
N_PAIRS = sum(n for _, n in PAIR_ROWS)
G_TOK = 32
G_TILES = T // G_TOK
FILL = 4
FILLED = FILL * (PEER_HEADS + G_TILES // 2)
GROUP = 8
N_GROUPS = N_KEYS // GROUP


def turns(eng, n, body):
    body(0)
    with eng.Fori(1, n) as i:
        body(i)


def wait_count(eng, sem, count):
    if not isinstance(count, int) or count > 0:
        eng.wait_ge(sem, count)


def front_stage(nc, io, keep, t16, v8, gx):
    with ExitStack() as ctx:
        sb = lambda n, s, d=F32: ctx.enter_context(nc.sbuf_tensor(n, s, d))
        pb = lambda n, s: ctx.enter_context(nc.psum_tensor(n, s, F32))
        sem = lambda n: ctx.enter_context(nc.semaphore(n))
        xT, mod, h_hi, h_lo = keep["xT"], keep["mod"], keep["h_hi"], keep["h_lo"]
        COLS = 512
        N_ADA, EARLY, TURNS, PAIR = 6 * D // COLS, 2 * D // COLS, N_PROJ // 2, 2
        PER = COLS // P
        assert N_ADA - EARLY == TURNS
        cT = sb("cT", [P, KD])
        c_act = sb("c_act", [P, KD])
        b_cols = sb("b_cols", [P, 6 * KD])
        w_ada = [sb(f"w_ada{n}", [P, KD, COLS]) for n in range(3)]
        ada = [sb(f"ada_sum{n}", [P, COLS]) for n in range(2)]
        sq = sb("sq_x", [P, 2, T])
        rstd = sb("rstd_x", [P, T])
        scaled = sq
        full = sb("full_h", [P, 2, T])
        w = [sb(f"w_proj{n}", [P, KD, P]) for n in range(PAIR)]
        w_hi = [sb(f"w_proj_hi{n}", [P, KD, P], F32R) for n in range(PAIR)]
        w_lo = [sb(f"w_proj_lo{n}", [P, KD, P], F32R) for n in range(PAIR)]
        wv = [sb(f"w_val{n}", [P, T]) for n in range(2)]
        wv_hi = [sb(f"w_val_hi{n}", [P, T], F32R) for n in range(2)]
        wv_lo = [sb(f"w_val_lo{n}", [P, T], F32R) for n in range(2)]
        wl = sb("w_lr", [P, KD, GLA_RANK])
        wl_hi = sb("w_lr_hi", [P, KD, GLA_RANK], F32R)
        wl_lo = sb("w_lr_lo", [P, KD, GLA_RANK], F32R)
        lrT = sb("lrT", [GLA_RANK, T])
        up = sb("gate_up", [GLA_RANK, GLA_PAIRS * P])
        b_gate = sb("b_gate", [P, GLA_PAIRS])
        ps_sum = pb("ps_sum_x", [P, T])
        ps_mod = pb("ps_mod", [P, 6 * KD])
        ps = [pb(f"ps_proj{n}", [P, T]) for n in range(PAIR)]
        ps_v = [pb(f"ps_val{n}", [P, T]) for n in range(TB)]
        small_in, x_in, late_in = sem("small_in"), sem("x_in"), sem("late_in")
        ada_in = [sem(f"ada_in{n}") for n in range(3)]
        w_in = [sem(f"w_proj_in{n}") for n in range(PAIR)]
        wv_in = [sem(f"wv_in{n}") for n in range(2)]
        consts, silu_done, sq_done, sum_done = sem("consts"), sem("silu_done"), sem("sq_done"), sem("sum_done")
        ln_done, rstd_done, chain, ada_read = sem("ln_done"), sem("rstd_done"), sem("ada_chain"), sem("ada_read")
        mod_done, mod_kept = sem("mod_done"), sem("mod_kept")
        scaled_done, full_done, hhi, hlo = sem("scaled_done"), sem("full_done"), sem("h_hi_done"), sem("h_lo_done")
        whi, wlo, prod, kept = sem("w_hi_done"), sem("w_lo_done"), sem("proj_done"), sem("proj_kept")
        lhi, llo, l_done, l_kept, g_done = sem("lr_hi"), sem("lr_lo"), sem("lr_done"), sem("lr_kept"), sem("gate_done")
        vhi, vlo, v_mul, v_kept = sem("wv_hi_done"), sem("wv_lo_done"), sem("v_mul"), sem("v_kept")
        block = ctx.enter_context(nc.Block())
        N_VAL = 2 * KD

        def projection_turns(eng, turn):
            with eng.Fori(0, (TURNS - 1) // 2) as i:
                turn(i, 0)
                turn(i, 1)
            turn((TURNS - 1) // 2, 0)

        @block.sync
        def _(sp):
            def load_ada(m, slot):
                sp.dma_start(w_ada[slot][:], io["w_ada"][ds(m, 1)].rearrange("o p k c -> (o p) k c")).then_inc(ada_in[slot], 16)

            def load_w(i, n):
                wait_count(sp, wlo, i * PAIR + n - PAIR + 1)
                sp.dma_start(w[n][:], io["w_proj"][ds(i * PAIR + n, 1)].rearrange("o p k c -> (o p) k c")).then_inc(w_in[n], 16)

            sp.dma_start(cT[:], io["cT"]).then_inc(small_in, 16)
            sp.dma_start(b_cols[:], io["b_ada"]).then_inc(small_in, 16)
            load_ada(0, 0)
            sp.dma_start(xT[:], io["xT"]).then_inc(x_in, 16)
            for m in range(1, 3):
                load_ada(m, m)
            sp.wait_ge(ada_read, 1)
            load_ada(3, 0)
            for n in range(PAIR):
                load_w(0, n)
            sp.dma_start(keep["gains"][:], io["gains"]).then_inc(late_in, 16)
            sp.dma_start(wl[:], io["w_lr"]).then_inc(late_in, 16)
            sp.dma_start(up[:], io["gate_up"]).then_inc(late_in, 16)
            sp.dma_start(b_gate[:], io["b_gate"]).then_inc(late_in, 16)

            def late_ada(i, e):
                m = EARLY + 2 * i + e
                sp.wait_ge(ada_read, m - 1)
                load_ada(m, 1 + e)

            def turn(i, e):
                late_ada(i, e)
                for n in range(PAIR):
                    load_w(2 * i + e + 1, n)

            projection_turns(sp, turn)
            late_ada((TURNS - 1) // 2, 1)
            for v in range(N_VAL):
                if v >= 2:
                    sp.wait_ge(vlo, v - 1)
                sp.dma_start(wv[v % 2][:], io["w_values"][v]).then_inc(wv_in[v % 2], 16)

        @block.gpsimd
        def _(pool):
            pool.memset(keep["ones"][:], 1.0).then_inc(consts, 1)
            pool.memset(keep["pair_ones"][:], 0.0).then_inc(consts, 1)
            pool.memset(keep["neg_ones"][:], -1.0).then_inc(consts, 1)
            pool.wait_ge(consts, 3)
            for e in range(2):
                pool.memset(keep["pair_ones"][64 * e:64 * e + 64, 64 * e:64 * e + 64], 1.0).then_inc(consts, 1)
                pool.wait_ge(consts, 4 + e)
            pool.affine_select(out=keep["ident"][:], in_=keep["ones"][:], compare_op=ALU.is_equal, fill=0.0, base=0,
                               pattern=[[-1, P]], channel_multiplier=1).then_inc(consts, 1)
            pool.affine_select(out=keep["neg_tri"][:], in_=keep["neg_ones"][:], compare_op=ALU.is_ge, fill=0.0, base=0,
                               pattern=[[-1, P]], channel_multiplier=1).then_inc(consts, 1)
            pool.iota(keep["iota"][:], pattern=[[1, P]], base=0, channel_multiplier=0,
                      allow_small_or_imprecise_dtypes=True).then_inc(consts, 1)
            pool.memset(keep["eps"][:], EPS).then_inc(consts, 1)

            def low(j, n):
                pool.wait_ge(whi, j * PAIR + n + 1)
                wait_count(pool, prod, j * PAIR + n - PAIR + 1)
                pool.tensor_tensor(w_lo[n][:], w[n][:], w_hi[n][:].bitcast(F32), ALU.subtract).then_inc(wlo, 1)

            def turn(i, e):
                for n in range(PAIR):
                    low(2 * i + e + 1, n)

            for n in range(PAIR):
                low(0, n)
            projection_turns(pool, turn)

        @block.scalar
        def _(act):
            def high(i, n):
                act.wait_ge(w_in[n], i * 16 + 16)
                wait_count(act, prod, i * PAIR + n - PAIR + 1)
                wait_count(act, wlo, i * PAIR + n - PAIR + 1)
                act.copy(w_hi[n][:], w[n][:]).then_inc(whi, 1)

            def keep_chunk(i, n):
                act.wait_ge(prod, i * PAIR + n + 1)
                act.copy(t16[:, ds(i * PAIR + n, 1)], ps[n][:].rearrange("p (o t) -> p o t", o=1)).then_inc(kept, 1)

            act.wait_ge(small_in, 32)
            act.activation(c_act[:], cT[:], ACT.Silu).then_inc(silu_done, 1)
            act.wait_ge(x_in, 16)
            for k in range(KD):
                if k >= 2:
                    act.wait_ge(sum_done, k - 1)
                act.activation(sq[:, k % 2], xT[:, k], ACT.Square).then_inc(sq_done, 1)
            act.wait_ge(sum_done, KD)
            act.wait_ge(consts, 9)
            act.activation(rstd[:], ps_sum[:], ACT.Ln, bias=keep["eps"][:], scale=1.0 / D).then_inc(ln_done, 1)
            act.wait_ge(ln_done, 1)
            act.activation(rstd[:], rstd[:], ACT.Exp, scale=-0.5).then_inc(rstd_done, 1)
            for n in range(PAIR):
                high(0, n)
            act.wait_ge(mod_kept, 2)
            for k in range(KD):
                shift = mod[:, k:k + 1]
                act.wait_ge(scaled_done, k + 1)
                act.activation(h_hi[:, k], scaled[:, k % 2], ACT.Identity, bias=shift).then_inc(hhi, 1)
                if k >= 2:
                    act.wait_ge(hlo, k - 1)
                act.activation(full[:, k % 2], scaled[:, k % 2], ACT.Identity, bias=shift).then_inc(full_done, 1)

            def turn(i, e):
                for n in range(PAIR):
                    keep_chunk(2 * i + e, n)
                    high(2 * i + e + 1, n)

            projection_turns(act, turn)
            for n in range(PAIR):
                keep_chunk(TURNS - 1, n)
            act.wait_ge(kept, N_PROJ)
            act.activation(t16[:, GLR:GLR + 4], t16[:, GLR:GLR + 4], ACT.Silu)
            act.wait_ge(late_in, 64)
            act.copy(wl_hi[:], wl[:]).then_inc(lhi, 1)
            for v in range(N_VAL):
                act.wait_ge(wv_in[v % 2], 16 * (v // 2 + 1))
                if v >= 2:
                    act.wait_ge(v_mul, v - 1)
                    act.wait_ge(vlo, v - 1)
                act.copy(wv_hi[v % 2][:], wv[v % 2][:]).then_inc(vhi, 1)
                if v == 1:
                    act.wait_ge(l_done, 1)
                    act.copy(lrT[:], ps_sum[0:GLA_RANK, :]).then_inc(l_kept, 1)
                if v == 3:
                    for p in range(GLA_PAIRS):
                        act.wait_ge(g_done, p + 1)
                        act.activation(gx[:, p], ps[p][:], ACT.Identity, bias=b_gate[:, p:p + 1])

        def keep_values(dve, g):
            dve.wait_ge(v_mul, (g + 1) * KD)
            for b in range(TB):
                dve.tensor_copy(v8[:, g, b], ps_v[b][:]).then_inc(v_kept, 1)

        @block.vector
        def _(dve):
            def sum_rows(m, slot, uses, at):
                dve.wait_ge(ada_in[slot], uses * 16)
                wait_count(dve, mod_done, m - 1)
                for k in range(KD):
                    col = c_act[:, k:k + 1]
                    if k == 0:
                        last = dve.tensor_scalar(ada[at][:], w_ada[slot][:, 0], col, None, ALU.mult)
                    else:
                        dve.wait_ge(chain, m * KD + k)
                        last = dve.scalar_tensor_tensor(ada[at][:], w_ada[slot][:, k], col, ada[at][:], ALU.mult, ALU.add)
                    last.then_inc(chain, 1)
                dve.wait_ge(chain, m * KD + KD)
                dve.sem_inc(ada_read, 1)

            dve.wait_ge(silu_done, 1)
            for m in range(EARLY):
                sum_rows(m, m % 3, m // 3 + 1, m % 2)
            n_early = EARLY * PER
            dve.wait_ge(mod_done, EARLY)
            dve.tensor_tensor(mod[:, 0:n_early], ps_mod[:, 0:n_early], b_cols[:, 0:n_early], ALU.add).then_inc(mod_kept, 1)
            dve.wait_ge(mod_kept, 1)
            dve.tensor_scalar(mod[:, KD:2 * KD], mod[:, KD:2 * KD], 1.0, None, ALU.add).then_inc(mod_kept, 1)
            dve.wait_ge(mod_kept, 2)
            dve.wait_ge(rstd_done, 1)
            for k in range(KD + 1):
                if k < KD:
                    if k >= 2:
                        dve.wait_ge(full_done, k - 1)
                    dve.scalar_tensor_tensor(scaled[:, k % 2], xT[:, k], mod[:, KD + k:KD + k + 1], rstd[:], ALU.mult, ALU.mult)\
                       .then_inc(scaled_done, 1)
                if k >= 1:
                    dve.wait_ge(full_done, k)
                    dve.tensor_tensor(h_lo[:, k - 1], full[:, (k - 1) % 2], h_hi[:, k - 1].bitcast(F32), ALU.subtract).then_inc(hlo, 1)

            def turn(i, e):
                sum_rows(EARLY + 2 * i + e, 1 + e, i + 2, e)

            projection_turns(dve, turn)
            turn((TURNS - 1) // 2, 1)
            dve.wait_ge(kept, N_PROJ)
            for n in range(SBK - SBQ):
                dve.tensor_scalar(t16[:, SBQ + n], t16[:, SBQ + n], SB_DH ** -0.5, None, ALU.mult)
            dve.wait_ge(lhi, 1)
            dve.tensor_tensor(wl_lo[:], wl[:], wl_hi[:].bitcast(F32), ALU.subtract).then_inc(llo, 1)
            for v in range(N_VAL):
                dve.wait_ge(vhi, v + 1)
                if v >= 2:
                    dve.wait_ge(v_mul, v - 1)
                dve.tensor_tensor(wv_lo[v % 2][:], wv[v % 2][:], wv_hi[v % 2][:].bitcast(F32), ALU.subtract).then_inc(vlo, 1)
                if v == KD + 1:
                    keep_values(dve, 0)
            dve.wait_ge(mod_done, N_ADA)
            dve.tensor_tensor(mod[:, n_early:], ps_mod[:, n_early:], b_cols[:, n_early:], ALU.add).then_inc(mod_kept, 1)
            dve.wait_ge(mod_kept, 3)
            dve.tensor_scalar(mod[:, 4 * KD:5 * KD], mod[:, 4 * KD:5 * KD], 1.0, None, ALU.add)
            keep_values(dve, 1)

        @block.tensor
        def _(pe):
            def mod_columns(m, at):
                pe.wait_ge(chain, m * KD + KD)
                for c in range(PER):
                    col = m * PER + c
                    last = pe.matmul(ps_mod[:, ds(col, 1)], ada[at][:, c * P:(c + 1) * P], keep["ones"][:, 0:1], start=True, stop=True)
                last.then_inc(mod_done, 1)

            def three_passes(n, k):
                hi, lo = w_hi[n][:, k], w_lo[n][:, k]
                pe.matmul(ps[n][:], hi, h_hi[:, k], start=(k == 0), stop=False)
                pe.matmul(ps[n][:], hi, h_lo[:, k], start=False, stop=False)
                return pe.matmul(ps[n][:], lo, h_hi[:, k], start=False, stop=(k == KD - 1))

            def product(i, n):
                pe.wait_ge(wlo, i * PAIR + n + 1)
                wait_count(pe, kept, i * PAIR + n - PAIR + 1)
                for k in range(KD):
                    last = three_passes(n, k)
                last.then_inc(prod, 1)

            pe.wait_ge(consts, 1)
            for k in range(KD):
                pe.wait_ge(sq_done, k + 1)
                pe.matmul(ps_sum[:], keep["ones"][:], sq[:, k % 2], start=(k == 0), stop=(k == KD - 1)).then_inc(sum_done, 1)
            for m in range(EARLY):
                mod_columns(m, m % 2)
            for n in range(PAIR):
                pe.wait_ge(wlo, n + 1)
            for k in range(KD):
                pe.wait_ge(hlo, k + 1)
                for n in range(PAIR):
                    last = three_passes(n, k)
                    if k == KD - 1:
                        last.then_inc(prod, 1)
            pe.wait_ge(mod_kept, 1)

            def turn(i, e):
                mod_columns(EARLY + 2 * i + e, e)
                for n in range(PAIR):
                    product(2 * i + e + 1, n)

            projection_turns(pe, turn)
            mod_columns(N_ADA - 1, 1)
            pe.wait_ge(llo, 1)
            for k in range(KD):
                for a, b in ((wl_hi, h_hi), (wl_hi, h_lo), (wl_lo, h_hi)):
                    last = pe.matmul(ps_sum[0:GLA_RANK, :], a[:, k], b[:, k], start=(k == 0 and b is h_hi and a is wl_hi),
                                     stop=(k == KD - 1 and a is wl_lo))
            last.then_inc(l_done, 1)
            for v in range(N_VAL):
                g, k = v // KD, v % KD
                pe.wait_ge(vlo, v + 1)
                for b in range(TB):
                    t = slice(b * P, (b + 1) * P)
                    if v == KD:
                        pe.wait_ge(v_kept, b + 1)
                    pe.matmul(ps_v[b][:], h_hi[:, k, t], wv_hi[v % 2][:], start=(k == 0), stop=False)
                    pe.matmul(ps_v[b][:], h_hi[:, k, t], wv_lo[v % 2][:], start=False, stop=False)
                    last = pe.matmul(ps_v[b][:], h_lo[:, k, t], wv_hi[v % 2][:], start=False, stop=(k == KD - 1))
                last.then_inc(v_mul, 1)
                if v == 2:
                    pe.wait_ge(l_kept, 1)
                    pe.wait_ge(kept, N_PROJ)
                    for p in range(GLA_PAIRS):
                        pe.matmul(ps[p][:], up[:, p * P:(p + 1) * P], lrT[:], start=True, stop=True).then_inc(g_done, 1)


def stick_breaking(nc, io, keep, t16, v8, catT):
    with ExitStack() as ctx:
        sb = lambda n, s, d=F32: ctx.enter_context(nc.sbuf_tensor(n, s, d))
        pb = lambda n, s: ctx.enter_context(nc.psum_tensor(n, s, F32))
        sem = lambda n: ctx.enter_context(nc.semaphore(n))
        NU, ZB = SB_HEADS * TB, 6
        mag = sb("z_mag", [P, 2, T])
        ez = sb("z_exp", [P, 2, T])
        lz = sb("z_log", [P, 2, T])
        soft = sb("softplus", [P, 2, TB, T])
        w = sb("sb_weights", [P, 2, TB, T])
        ps_z = [pb(f"ps_z{n}", [P, T]) for n in range(ZB)]
        ps_o = [pb(f"ps_o{n}", [P, T]) for n in range(2)]
        z_done, mag_done, ez_done, lz_done = sem("z_done"), sem("mag_done"), sem("ez_done"), sem("lz_done")
        soft_done, soft_masked, suffix_done = sem("soft_done"), sem("soft_masked"), sem("suffix_done")
        w_done, w_masked, o_done, o_kept = sem("w_done"), sem("w_masked"), sem("o_done"), sem("o_kept")
        block = ctx.enter_context(nc.Block())
        place = lambda u: (u // TB, TB - 1 - u % TB)
        LAG_SUM, LAG_OUT = 2, 6

        @block.sync
        def _(sp):
            sp.dma_start(keep["w_out"][:], io["w_out"]).then_inc(keep["w_out_in"], 16)

        @block.tensor
        def _(pe):
            def scores(u):
                h, s = place(u)
                r, c = 64 * (h % 2), h // 2
                if u >= ZB:
                    pe.wait_ge(w_done, u - ZB + 1)
                pe.matmul(ps_z[u % ZB][:, s * P:T], t16[r:r + 64, SBK + c, s * P:(s + 1) * P], t16[r:r + 64, SBQ + c, s * P:T],
                          start=True, stop=True).then_inc(z_done, 1)

            def outputs(h):
                pe.wait_ge(w_masked, TB * h + TB)
                if h >= 4 and h % 2 == 0:
                    pe.wait_ge(o_kept, h // 2 - 1)
                for s in range(TB):
                    last = pe.matmul(ps_o[h // 2 % 2][64 * (h % 2):64 * (h % 2) + 64, s * P:T], v8[:, 0, s, h * 64:h * 64 + 64],
                                     w[:, h % 2, s, s * P:T], start=(s == 0), stop=(s == TB - 1))
                last.then_inc(o_done, 1)

            for u in range(NU + LAG_OUT):
                if u < NU:
                    scores(u)
                if LAG_SUM <= u < NU + LAG_SUM:
                    v = u - LAG_SUM
                    h, s = place(v)
                    pe.wait_ge(soft_masked, v + 1)
                    for s2 in range(s, TB):
                        last = pe.matmul(ps_z[v % ZB][:, s2 * P:T], keep["neg_tri" if s2 == s else "neg_ones"][:],
                                         soft[:, h % 2, s2, s2 * P:T], start=False, stop=(s2 == TB - 1), skip_group_check=True)
                    last.then_inc(suffix_done, 1)
                if u >= LAG_OUT and (u - LAG_OUT) % TB == TB - 1:
                    outputs((u - LAG_OUT) // TB)

        @block.scalar
        def _(act):
            def weights(u):
                h, s = place(u)
                act.wait_ge(suffix_done, u + 1)
                if h >= 2:
                    act.wait_ge(o_done, h - 1)
                act.activation(w[:, h % 2, s, s * P:T], ps_z[u % ZB][:, s * P:T], ACT.Exp).then_inc(w_done, 1)

            act.preload_act_table_set("natural_log_exp_and_others")
            for u in range(NU + 3):
                if u < NU:
                    h, s = place(u)
                    n = T - s * P
                    act.wait_ge(z_done, u + 1)
                    if u >= 2:
                        act.wait_ge(ez_done, u - 1)
                    act.activation(mag[:, u % 2, 0:n], ps_z[u % ZB][:, s * P:T], ACT.Abs).then_inc(mag_done, 1)
                    act.wait_ge(mag_done, u + 1)
                    if u >= 2:
                        act.wait_ge(lz_done, u - 1)
                    act.activation(ez[:, u % 2, 0:n], mag[:, u % 2, 0:n], ACT.Exp, scale=-1.0).then_inc(ez_done, 1)
                    act.wait_ge(ez_done, u + 1)
                    if u >= 2:
                        act.wait_ge(soft_done, u - 1)
                    act.activation(lz[:, u % 2, 0:n], ez[:, u % 2, 0:n], ACT.Ln, bias=1.0).then_inc(lz_done, 1)
                if u >= 3:
                    weights(u - 3)

        @block.vector
        def _(dve):
            def keep_outputs(p):
                dve.wait_ge(o_done, 2 * p + 2)
                dve.tensor_copy(catT[:, p], ps_o[p % 2][:]).then_inc(o_kept, 1)

            for u in range(NU):
                h, s = place(u)
                n = T - s * P
                dve.wait_ge(lz_done, u + 1)
                if h >= 2 and s == TB - 1:
                    dve.wait_ge(suffix_done, TB * (h - 1))
                dve.scalar_tensor_tensor(soft[:, h % 2, s, s * P:T], ps_z[u % ZB][:, s * P:T], 0.0, lz[:, u % 2, 0:n],
                                         ALU.max, ALU.add).then_inc(soft_done, 1)
                if h >= 3 and h % 2 == 1 and s == 0:
                    keep_outputs((h - 3) // 2)
            keep_outputs(SB_HEADS // 2 - 1)

        @block.gpsimd
        def _(pool):
            def mask(tile, h, s, done):
                diag = tile[:, h % 2, s, s * P:(s + 1) * P]
                pool.affine_select(out=diag, in_=diag, compare_op=ALU.is_gt, fill=0.0, base=0, pattern=[[1, P]],
                                   channel_multiplier=-1).then_inc(done, 1)

            for u in range(NU + 3):
                if u < NU:
                    pool.wait_ge(soft_done, u + 1)
                    mask(soft, *place(u), soft_masked)
                if u >= 3:
                    pool.wait_ge(w_done, u - 2)
                    mask(w, *place(u - 3), w_masked)


def gated_linear(nc, io, keep, t16, v8, x, catT):
    with ExitStack() as ctx:
        sb = lambda n, s, d=F32: ctx.enter_context(nc.sbuf_tensor(n, s, d))
        pb = lambda n, s: ctx.enter_context(nc.psum_tensor(n, s, F32))
        sem = lambda n: ctx.enter_context(nc.semaphore(n))
        C, NC = GLA_CHUNK, N_CHUNKS
        restart = sb("restart", [P, T])
        causal = sb("gla_causal", [P, C])
        mag = sb("gate_mag", [P, GLA_PAIRS, T])
        la = x
        bc = sb("b_cum16", [P, GLA_PAIRS, T])
        dm = sb("b_mid16", [P, GLA_PAIRS, T])
        dl = sb("b_last16", [P, GLA_PAIRS, T])
        e_q = sb("e_q", [P, GLA_PAIRS, T])
        e_k = dm
        e_b = sb("e_b", [P, GLA_PAIRS, T])
        e_l = dl
        carry = sb("chunk_decay", [P, GLA_PAIRS, NC])
        q_in = sb("q_intra", [P, GLA_PAIRS, T])
        q_st = sb("q_state", [P, GLA_PAIRS, T])
        k_in = sb("k_intra", [P, GLA_HEADS, T])
        k_dec = sb("k_decayed", [P, GLA_PAIRS, T])
        kt = sb("k_decayed_t", [P, GLA_PAIRS, NC, P])
        sc = sb("gla_scores", [P, GLA_HEADS, TB, P])
        st = sb("gla_state", [P, GLA_HEADS, 2, GLA_DV])
        sq = sb("sq_sb", [P, 2, T])
        rstd = sb("rstd_sb", [P, TB, T])
        ps_g = [pb(f"ps_gate{n}", [P, T]) for n in range(2)]
        ps_u = [pb(f"ps_upd{n}", [P, T]) for n in range(2)]
        ps_o = [pb(f"ps_gla_o{h}", [P, T]) for h in range(GLA_HEADS)]
        zeros, link = sem("gla_zeros"), sem("gla_act_link")
        log_done, chain, exps, ops = sem("log_done"), sem("gla_dve_chain"), sem("exps"), sem("gla_operands")
        t_done, kt_done, s_done, sc_done = sem("kt_ps"), sem("kt_done"), sem("sc_ps"), sem("sc_done")
        sq_done, sum_done, ln_done, rstd_done = sem("sq_sb_done"), sem("sum_sb_done"), sem("ln_sb_done"), sem("rstd_sb_done")
        u_done, st_done, inter, o_done = sem("upd_done"), sem("state_done"), sem("inter_done"), sem("gla_o_done")
        block = ctx.enter_context(nc.Block())
        upd_bank = lambda p, c: (ps_u, ps_g)[c % 2][p]

        @block.gpsimd
        def _(pool):
            for tile in (k_in, kt, sc, st):
                pool.memset(tile[:], 0.0).then_inc(zeros, 1)
            pool.memset(restart[:], 1.0).then_inc(zeros, 1)
            pool.memset(causal[:], 1.0).then_inc(zeros, 1)
            pool.wait_ge(zeros, 6)
            pool.memset(restart[:].rearrange("p (c t) -> p c t", c=NC)[:, :, 0:1], 0.0).then_inc(zeros, 1)
            for o in range(2):
                pool.wait_ge(zeros, 7 + o)
                half = causal[64 * o:64 * o + 64, :]
                pool.affine_select(out=half, in_=half, compare_op=ALU.is_ge, fill=0.0, base=0, pattern=[[1, C]],
                                   channel_multiplier=-1).then_inc(zeros, 1)

        @block.scalar
        def _(act):
            act.activation(mag[:], x[:], ACT.Abs).then_inc(link, 1)
            act.wait_ge(link, 1)
            act.activation(mag[:], mag[:], ACT.Exp, scale=-1.0).then_inc(link, 1)
            act.wait_ge(link, 2)
            act.activation(mag[:], mag[:], ACT.Ln, bias=1.0).then_inc(log_done, 1)
            for c in range(TB):
                if c >= 2:
                    act.wait_ge(sum_done, c - 1)
                act.activation(sq[:, c % 2], catT[:, c], ACT.Square).then_inc(sq_done, 1)
            for c in range(TB):
                act.wait_ge(sum_done, c + 1)
                act.activation(rstd[:, c], ps_o[c][:], ACT.Ln, bias=keep["eps"][:], scale=1.0 / SB_DH).then_inc(ln_done, 1)
            for c in range(TB):
                act.wait_ge(ln_done, c + 1)
                act.activation(rstd[:, c], rstd[:, c], ACT.Exp, scale=-0.5).then_inc(rstd_done, 1)
            act.wait_ge(chain, 2 + 3 * GLA_PAIRS)
            act.activation(e_q[:], dm[:], ACT.Exp, scale=1.0 / GLA_TAU).then_inc(exps, 1)
            act.wait_ge(exps, 1)
            act.activation(e_k[:], dm[:], ACT.Exp, scale=-1.0 / GLA_TAU).then_inc(exps, 1)
            act.activation(e_b[:], bc[:], ACT.Exp, scale=1.0 / GLA_TAU).then_inc(exps, 1)
            act.activation(e_l[:], dl[:], ACT.Exp, scale=1.0 / GLA_TAU).then_inc(exps, 1)
            last_row = bc[:].rearrange("p a (c t) -> p a c t", c=NC)[:, :, :, C - 1]
            act.activation(carry[:], last_row, ACT.Exp, scale=1.0 / GLA_TAU).then_inc(exps, 1)

        @block.vector
        def _(dve):
            done = [0]

            def link_next(ins):
                done[0] += 1
                ins.then_inc(chain, 1)
                dve.wait_ge(chain, done[0])

            dve.wait_ge(log_done, 1)
            link_next(dve.tensor_scalar(la[:], x[:], 0.0, None, ALU.min))
            link_next(dve.tensor_tensor(la[:], la[:], mag[:], ALU.subtract))
            dve.wait_ge(zeros, 9)
            for p in range(GLA_PAIRS):
                link_next(dve.tensor_tensor_scan(bc[:, p], restart[:], la[:, p], 0.0, ALU.mult, ALU.add))
            view = lambda tile, p: tile[:, p].rearrange("p (c t) -> p c t", c=NC)
            for p in range(GLA_PAIRS):
                b = view(bc, p)
                mid = b[:, :, C // 2 - 1:C // 2].broadcast_to([P, NC, C])
                end = b[:, :, C - 1:C].broadcast_to([P, NC, C])
                link_next(dve.tensor_tensor(view(dm, p), b, mid, ALU.subtract))
                link_next(dve.tensor_tensor(view(dl, p), end, b, ALU.subtract))
            dve.wait_ge(exps, 5)
            scale = GLA_DK ** -0.5
            for p in range(GLA_PAIRS):
                dve.tensor_tensor(k_dec[:, p], t16[:, GLK + p], e_l[:, p], ALU.mult).then_inc(ops, 1)
                dve.scalar_tensor_tensor(q_in[:, p], t16[:, GLQ + p], scale, e_q[:, p], ALU.mult, ALU.mult).then_inc(ops, 1)
                dve.scalar_tensor_tensor(q_st[:, p], t16[:, GLQ + p], scale, e_b[:, p], ALU.mult, ALU.mult).then_inc(ops, 1)
                for e in range(2):
                    r = slice(64 * e, 64 * e + 64)
                    dve.tensor_tensor(k_in[r, 2 * p + e], t16[r, GLK + p], e_k[r, p], ALU.mult).then_inc(ops, 1)
            for c in range(TB):
                dve.wait_ge(rstd_done, c + 1)
                dve.scalar_tensor_tensor(catT[:, c], catT[:, c], keep["gains"][:, c:c + 1], rstd[:, c], ALU.mult, ALU.mult)
            for p in range(GLA_PAIRS):
                dve.wait_ge(t_done, p + 1)
                for o in range(2):
                    r = slice(64 * o, 64 * o + 64)
                    src = ps_g[p][:].rearrange("p (b d) -> p b d", b=TB)
                    dst = kt[:, p].rearrange("p (b o) d -> p b o d", o=2)
                    dve.tensor_copy(dst[r, :, o, :], src[r]).then_inc(kt_done, 1)
            for h in range(GLA_HEADS):
                dve.wait_ge(s_done, h + 1)
                for o in range(2):
                    r = slice(64 * o, 64 * o + 64)
                    src = ps_o[h][:].rearrange("p (b t) -> p b t", b=TB)
                    m = causal[r].rearrange("p (o t) -> p o t", o=1).broadcast_to([64, TB, C])
                    dve.tensor_tensor(sc[r, h, :, o * C:(o + 1) * C], src[r, :, o * C:(o + 1) * C], m, ALU.mult).then_inc(sc_done, 1)
            for c in range(NC - 1):
                dve.wait_ge(u_done, 2 * c + 2)
                if c >= 2:
                    dve.wait_ge(inter, c - 1)
                if c >= 1:
                    dve.wait_ge(st_done, GLA_HEADS * c)
                for h in range(GLA_HEADS):
                    p, e = h // 2, h % 2
                    r = slice(64 * e, 64 * e + 64)
                    new, old = st[r, h, (c + 1) % 2], st[r, h, c % 2]
                    u = upd_bank(p, c)[r, e * P:(e + 1) * P]
                    if c == 0:
                        dve.tensor_copy(new, u).then_inc(st_done, 1)
                    else:
                        dve.scalar_tensor_tensor(new, old, carry[r, p, c:c + 1], u, ALU.mult, ALU.add).then_inc(st_done, 1)
            for h in range(GLA_HEADS):
                dve.wait_ge(o_done, 1)
                dve.tensor_copy(catT[:, TB + h], ps_o[h][:])

        @block.tensor
        def _(pe):
            for c in range(TB):
                pe.wait_ge(sq_done, c + 1)
                pe.matmul(ps_o[c][:], keep["pair_ones"][:], sq[:, c % 2], start=True, stop=True).then_inc(sum_done, 1)
            pe.wait_ge(ln_done, TB)
            pe.wait_ge(ops, 5 * GLA_PAIRS)
            for p in range(GLA_PAIRS):
                for b in range(TB):
                    last = pe.transpose(ps_g[p][:, b * P:(b + 1) * P], k_dec[:, p, b * P:(b + 1) * P], keep["ident"][:])
                last.then_inc(t_done, 1)
            for h in range(GLA_HEADS):
                for b in range(TB):
                    last = pe.matmul(ps_o[h][:, b * P:(b + 1) * P], k_in[:, h, b * P:(b + 1) * P],
                                     q_in[:, h // 2, b * P:(b + 1) * P], start=True, stop=True)
                last.then_inc(s_done, 1)
            pe.wait_ge(kt_done, 2 * GLA_PAIRS)
            pe.wait_ge(sc_done, 2 * GLA_HEADS)

            def update(c):
                if c >= 2:
                    pe.wait_ge(st_done, GLA_HEADS * (c - 1))
                for p in range(GLA_PAIRS):
                    pe.matmul(upd_bank(p, c)[:, 0:2 * P], kt[:, p, c], v8[:, 1, c // 2, p * 256:(p + 1) * 256],
                              start=True, stop=True).then_inc(u_done, 1)

            update(0)
            for c in range(NC):
                if c + 1 < NC - 1:
                    update(c + 1)
                if c % 2 == 0:
                    for h in range(GLA_HEADS):
                        pe.matmul(ps_o[h][:, c * C:(c + 2) * C], v8[:, 1, c // 2, h * P:(h + 1) * P], sc[:, h, c // 2],
                                  start=True, stop=False, skip_group_check=True)
                if c >= 1:
                    pe.wait_ge(st_done, GLA_HEADS * c)
                    for h in range(GLA_HEADS):
                        last = pe.matmul(ps_o[h][:, c * C:(c + 1) * C], st[:, h, c % 2], q_st[:, h // 2, c * C:(c + 1) * C],
                                         start=False, stop=(c % 2 == 1), skip_group_check=True)
                    last.then_inc(inter, 1)
            pe.wait_ge(inter, NC - 1)
            pe.nop().then_inc(o_done, 1)


def mixer_back(nc, io, keep, t16, v8, catT):
    with ExitStack() as ctx:
        sb = lambda n, s, d=F32: ctx.enter_context(nc.sbuf_tensor(n, s, d))
        pb = lambda n, s: ctx.enter_context(nc.psum_tensor(n, s, F32))
        sem = lambda n: ctx.enter_context(nc.semaphore(n))
        xT, mod, gains = keep["xT"], keep["mod"], keep["gains"]
        h_hi, h_lo = keep["h_hi"], keep["h_lo"]
        WS = 3
        NG = KD - TB
        cat_hi, cat_lo = sb("cat_hi", [P, KD, T], F32R), sb("cat_lo", [P, KD, T], F32R)
        w_hi = [sb(f"w_out_hi{n}", [P, KD, P], F32R) for n in range(WS)]
        w_lo = [sb(f"w_out_lo{n}", [P, KD, P], F32R) for n in range(WS)]
        sq, rstd = v8[:, 0], v8[:, 1]
        scaled, full = rstd[:, 2:4], sq[:, 2:4]
        ps_s = [pb(f"ps_hs{n}", [P, T]) for n in range(NG)]
        ps_p = [pb(f"ps_mix{n}", [P, T]) for n in range(3)]
        ps_x = pb("ps_sum_2", [P, T])
        sq_done, sum_done, ln_done, rstd_done = sem("hsq"), sem("hsum"), sem("hln"), sem("hrstd")
        normed, cat_done, chi, clo = sem("normed"), sem("cat_done"), sem("cat_hi_done"), sem("cat_lo_done")
        whi, wlo, mix_done, x_done = sem("w_out_hi_done"), sem("w_out_lo_done"), sem("mix_done"), sem("x1_done")
        sq2_done, sum2_done, ln2_done, rstd2_done = sem("sq2"), sem("sum2"), sem("ln2"), sem("rstd2")
        sc_done, f_done, hi_done, lo_done = sem("scaled2"), sem("full2"), sem("hi_done"), sem("lo_done")
        block = ctx.enter_context(nc.Block())

        @block.scalar
        def _(act):
            def w_high(n):
                if n == 0:
                    act.wait_ge(keep["w_out_in"], 16)
                if n >= WS:
                    act.wait_ge(mix_done, n - WS + 1)
                    act.wait_ge(wlo, n - WS + 1)
                act.copy(w_hi[n % WS][:], keep["w_out"][:, n]).then_inc(whi, 1)

            for c in range(NG):
                act.activation(sq[:, c], catT[:, TB + c], ACT.Square).then_inc(sq_done, 1)
                if c == 1:
                    w_high(0)
                    act.copy(cat_hi[:, 0:2], catT[:, 0:2]).then_inc(chi, 2)
            for c in range(NG):
                act.wait_ge(sum_done, c + 1)
                act.activation(rstd[:, c], ps_s[c][:], ACT.Ln, bias=keep["eps"][:], scale=1.0 / GLA_DV).then_inc(ln_done, 1)
                act.wait_ge(ln_done, c + 1)
                act.activation(rstd[:, c], rstd[:, c], ACT.Exp, scale=-0.5).then_inc(rstd_done, 1)
                if c == 0:
                    act.copy(cat_hi[:, 2:4], catT[:, 2:4]).then_inc(chi, 2)
            w_high(1)
            for c in range(NG):
                act.wait_ge(cat_done, c + 1)
                act.copy(cat_hi[:, TB + c], catT[:, TB + c]).then_inc(chi, 1)
            for n in range(KD):
                if n + 2 < KD:
                    w_high(n + 2)
                act.wait_ge(x_done, n + 1)
                if n >= 2:
                    act.wait_ge(sum2_done, n - 1)
                else:
                    act.wait_ge(sum_done, NG)
                act.activation(sq[:, n % 2], xT[:, n], ACT.Square).then_inc(sq2_done, 1)
            act.wait_ge(sum2_done, KD)
            act.activation(rstd[:, 0], ps_x[:], ACT.Ln, bias=keep["eps"][:], scale=1.0 / D).then_inc(ln2_done, 1)
            act.wait_ge(ln2_done, 1)
            act.activation(rstd[:, 0], rstd[:, 0], ACT.Exp, scale=-0.5).then_inc(rstd2_done, 1)
            for k in range(KD):
                shift = mod[:, 3 * KD + k:3 * KD + k + 1]
                act.wait_ge(sc_done, k + 1)
                act.activation(h_hi[:, k], scaled[:, k % 2], ACT.Identity, bias=shift).then_inc(hi_done, 1)
                if k >= 2:
                    act.wait_ge(lo_done, k - 1)
                act.activation(full[:, k % 2], scaled[:, k % 2], ACT.Identity, bias=shift).then_inc(f_done, 1)

        @block.gpsimd
        def _(pool):
            for n in range(KD):
                pool.wait_ge(whi, n + 1)
                if n >= WS:
                    pool.wait_ge(mix_done, n - WS + 1)
                pool.tensor_tensor(w_lo[n % WS][:], keep["w_out"][:, n], w_hi[n % WS][:].bitcast(F32), ALU.subtract).then_inc(wlo, 1)

        @block.tensor
        def _(pe):
            for c in range(NG):
                pe.wait_ge(sq_done, c + 1)
                pe.matmul(ps_s[c][:], keep["ones"][:], sq[:, c], start=True, stop=True).then_inc(sum_done, 1)
            for n in range(KD + 1):
                if n < KD:
                    pe.wait_ge(wlo, n + 1)
                    if n >= 3:
                        pe.wait_ge(x_done, n - 2)
                    for k in range(KD):
                        if n == 0:
                            pe.wait_ge(clo, k + 1)
                        hi, lo = w_hi[n % WS][:, k], w_lo[n % WS][:, k]
                        pe.matmul(ps_p[n % 3][:], hi, cat_hi[:, k], start=(k == 0), stop=False)
                        pe.matmul(ps_p[n % 3][:], hi, cat_lo[:, k], start=False, stop=False)
                        last = pe.matmul(ps_p[n % 3][:], lo, cat_hi[:, k], start=False, stop=(k == KD - 1))
                    last.then_inc(mix_done, 1)
                if n >= 1:
                    pe.wait_ge(sq2_done, n)
                    pe.matmul(ps_x[:], keep["ones"][:], sq[:, (n - 1) % 2], start=(n == 1), stop=(n == KD),
                              skip_group_check=True).then_inc(sum2_done, 1)

        @block.vector
        def _(dve):
            def cat_low(c0, c1):
                dve.wait_ge(chi, c1)
                dve.tensor_tensor(cat_lo[:, c0:c1], catT[:, c0:c1], cat_hi[:, c0:c1].bitcast(F32), ALU.subtract).then_inc(clo, c1 - c0)

            cat_low(0, 2)
            cat_low(2, 4)
            for c in range(NG):
                dve.wait_ge(rstd_done, c + 1)
                at = TB + c
                dve.scalar_tensor_tensor(catT[:, at], catT[:, at], gains[:, at:at + 1], rstd[:, c], ALU.mult, ALU.mult).then_inc(normed, 1)
                dve.wait_ge(normed, c + 1)
                dve.tensor_tensor(catT[:, at], catT[:, at], t16[:, GLR + c], ALU.mult).then_inc(cat_done, 1)
                if c >= 1:
                    cat_low(at - 1, at)
            cat_low(KD - 1, KD)
            for n in range(KD):
                dve.wait_ge(mix_done, n + 1)
                dve.scalar_tensor_tensor(xT[:, n], ps_p[n % 3][:], mod[:, 2 * KD + n:2 * KD + n + 1], xT[:, n],
                                         ALU.mult, ALU.add).then_inc(x_done, 1)
            dve.wait_ge(rstd2_done, 1)
            dve.wait_ge(x_done, KD)
            for k in range(KD):
                if k >= 2:
                    dve.wait_ge(f_done, k - 1)
                dve.scalar_tensor_tensor(scaled[:, k % 2], xT[:, k], mod[:, 4 * KD + k:4 * KD + k + 1], rstd[:, 0],
                                         ALU.mult, ALU.mult).then_inc(sc_done, 1)
                if k >= 1:
                    dve.wait_ge(f_done, k)
                    dve.tensor_tensor(h_lo[:, k - 1], full[:, (k - 1) % 2], h_hi[:, k - 1].bitcast(F32), ALU.subtract).then_inc(lo_done, 1)
            dve.wait_ge(f_done, KD)
            dve.tensor_tensor(h_lo[:, KD - 1], full[:, (KD - 1) % 2], h_hi[:, KD - 1].bitcast(F32), ALU.subtract).then_inc(lo_done, 1)


class BlockProducts:

    def __init__(self, nc, ctx, io, keep, slots):
        sb = lambda n, s, d=F32: ctx.enter_context(nc.sbuf_tensor(f"{n}_early", s, d))
        sem = lambda n: ctx.enter_context(nc.semaphore(f"{n}_early"))
        self.io, self.keep, self.slots = io, keep, slots
        span = range(slots)
        self.raw = [sb(f"u_raw{n}", [P, KD, P]) for n in span]
        self.hi = [sb(f"u_hi{n}", [P, KD, P], F32R) for n in span]
        self.lo = [sb(f"u_lo{n}", [P, KD, P], F32R) for n in span]
        self.act = [sb(f"u_act{n}", [P, T]) for n in span]
        self.ps = [ctx.enter_context(nc.psum_tensor(f"ps_u{n}_early", [P, T], F32)) for n in span]
        self.u_in, self.stored = [sem(f"u_in{n}") for n in span], [sem(f"act_stored{n}") for n in span]
        self.hi_done, self.lo_done, self.mul, self.act_done = sem("u_hi_done"), sem("u_lo_done"), sem("u_mul"), sem("u_act_done")

    def load(self, sp, i, n):
        wait_count(sp, self.lo_done, (i - 1) * self.slots + n + 1)
        sp.dma_start(self.raw[n][:], self.io["u"][ds(i * self.slots + n, 1)].rearrange("o p k e -> (o p) k e"))\
          .then_inc(self.u_in[n], 16)

    def high(self, act, i, n):
        act.wait_ge(self.u_in[n], i * 16 + 16)
        wait_count(act, self.mul, (i - 1) * self.slots + n + 1)
        wait_count(act, self.lo_done, (i - 1) * self.slots + n + 1)
        act.copy(self.hi[n][:], self.raw[n][:]).then_inc(self.hi_done, 1)

    def low(self, eng, i, n):
        eng.wait_ge(self.hi_done, i * self.slots + n + 1)
        wait_count(eng, self.mul, (i - 1) * self.slots + n + 1)
        eng.tensor_tensor(self.lo[n][:], self.raw[n][:], self.hi[n][:].bitcast(F32), ALU.subtract).then_inc(self.lo_done, 1)

    def product(self, pe, i, n):
        h_hi, h_lo = self.keep["h_hi"], self.keep["h_lo"]
        pe.wait_ge(self.lo_done, i * self.slots + n + 1)
        wait_count(pe, self.act_done, (i - 1) * self.slots + n + 1)
        for k in range(KD):
            pe.matmul(self.ps[n][:], self.hi[n][:, k], h_hi[:, k], start=(k == 0), stop=False)
            pe.matmul(self.ps[n][:], self.hi[n][:, k], h_lo[:, k], start=False, stop=False)
            last = pe.matmul(self.ps[n][:], self.lo[n][:, k], h_hi[:, k], start=False, stop=(k == KD - 1))
        last.then_inc(self.mul, 1)

    def gelu(self, act, i, n):
        act.wait_ge(self.mul, i * self.slots + n + 1)
        wait_count(act, self.stored[n], i * 16)
        act.activation(self.act[n][:], self.ps[n][:], ACT.Gelu).then_inc(self.act_done, 1)

    def store(self, sp, i, n, acts):
        sp.wait_ge(self.act_done, i * self.slots + n + 1)
        sp.dma_start(acts[ds(i * self.slots + n, 1)].rearrange("o p t -> (o p) t"), self.act[n][:]).then_inc(self.stored[n], 16)


def retrieval(nc, io, keep, picks, acts, fill):
    with ExitStack() as ctx:
        sb = lambda n, s, d=F32: ctx.enter_context(nc.sbuf_tensor(n, s, d))
        pb = lambda n, s: ctx.enter_context(nc.psum_tensor(n, s, F32))
        sem = lambda n: ctx.enter_context(nc.semaphore(n))
        h_hi, h_lo = keep["h_hi"], keep["h_lo"]
        expert, gate = picks
        w = [sb(f"w_query{s}", [P, KD, P]) for s in range(2)]
        w_hi = [sb(f"w_query_hi{s}", [P, KD, P], F32R) for s in range(2)]
        w_lo = [sb(f"w_query_lo{s}", [P, KD, P], F32R) for s in range(2)]
        keys = [sb(f"keys{s}", [P, N_KEYS]) for s in range(2)]
        q = [sb(f"query{s}", [P, T]) for s in range(2)]
        iota50 = sb("iota_pairs", [P, N_PAIRS])
        turn_mark = sb("turn_mark", [P, 1])
        scores = sb("scores", [P, 2, TB, N_KEYS])
        rest = sb("rest", [P, 2, TB, N_KEYS])
        top = sb("top_keys", [P, 2, TB, TOPK])
        idx = sb("top_idx", [P, 2, TB, TOPK], U32)
        num = sb("top_num", [P, 2, TB, TOPK])
        cand = sb("cand", [P, TB, N_PAIRS])
        cnum = sb("cand_num", [P, TB, N_PAIRS])
        crest = sb("cand_rest", [P, TB, N_PAIRS])
        ctop = sb("cand_top", [P, TB, TOPK])
        cpos = sb("cand_pos", [P, TB, TOPK], U32)
        cposf = sb("cand_posf", [P, TB, TOPK])
        hit = sb("hit", [P, TB, TOPK, N_PAIRS])
        ex = sb("gate_exp", [P, TB, TOPK])
        tot = sb("gate_sum", [P, TB, 1])
        picked = sb("picked", [P, TB, TOPK])
        ps_q = [pb(f"ps_q{s}", [P, T]) for s in range(2)]
        ps_s = [pb(f"ps_s{s}", [P, T]) for s in range(2)]
        iota_done = sem("iota50_done")
        w_in, k_in = [sem(f"wq_in{s}") for s in range(2)], [sem(f"keys_in{s}") for s in range(2)]
        wq_hi, wq_lo, q_done, q_kept, s_done = sem("wq_hi"), sem("wq_lo"), sem("q_done"), sem("q_kept"), sem("s_done")
        s_copied, s_used, s_read = sem("s_copied"), sem("s_used"), sem("s_read")
        chain, gate_chain, e_in, e_done = sem("topk_chain"), sem("gate_chain"), sem("exp_in"), sem("exp_done")
        block = ctx.enter_context(nc.Block())
        LAST = PEER_HEADS - 1

        @block.sync
        def _(sp):
            def loads(h):
                for s in range(2):
                    wait_count(sp, wq_lo, h * 2 + s - 1)
                    sp.dma_start(w[s][:], io["w_q"][ds(h * 2 + s, 1)].rearrange("o p k c -> (o p) k c")).then_inc(w_in[s], 16)
                for n in range(FILL):
                    fill.load(sp, h, n)
                for s in range(2):
                    wait_count(sp, s_done, h)
                    sp.dma_start(keys[s][:], io[("keys_a", "keys_b")[s]][ds(h, 1)].rearrange("o p k -> (o p) k")).then_inc(k_in[s], 16)

            def stores(h):
                for n in range(FILL):
                    fill.store(sp, h, n, acts)

            loads(0)
            with sp.Fori(1, PEER_HEADS) as h:
                loads(h)
                stores(h - 1)
            for n in range(FILL):
                fill.load(sp, PEER_HEADS, n)
            stores(LAST)

        @block.gpsimd
        def _(pool):
            pool.iota(iota50[:], pattern=[[1, N_PAIRS]], base=0, channel_multiplier=0,
                      allow_small_or_imprecise_dtypes=True).then_inc(iota_done, 1)

            def turn(h):
                for s in range(2):
                    pool.wait_ge(wq_hi, h * 2 + s + 1)
                    wait_count(pool, q_done, h * 2 + s - 1)
                    pool.tensor_tensor(w_lo[s][:], w[s][:], w_hi[s][:].bitcast(F32), ALU.subtract).then_inc(wq_lo, 1)
                for n in range(FILL):
                    fill.low(pool, h, n)

            turns(pool, PEER_HEADS, turn)
            for n in range(FILL):
                fill.low(pool, PEER_HEADS, n)

        @block.tensor
        def _(pe):
            def turn(h):
                for s in range(2):
                    pe.wait_ge(wq_lo, h * 2 + s + 1)
                    wait_count(pe, q_kept, h * 2)
                    for k in range(KD):
                        pe.matmul(ps_q[s][:], w_hi[s][:, k], h_hi[:, k], start=(k == 0), stop=False)
                        pe.matmul(ps_q[s][:], w_hi[s][:, k], h_lo[:, k], start=False, stop=False)
                        last = pe.matmul(ps_q[s][:], w_lo[s][:, k], h_hi[:, k], start=False, stop=(k == KD - 1))
                    last.then_inc(q_done, 1)
                wait_count(pe, s_used, h)
                pe.wait_ge(q_kept, h * 2 + 2)
                for s in range(2):
                    pe.wait_ge(k_in[s], h * 16 + 16)
                    for b in range(TB):
                        last = pe.matmul(ps_s[s][:, b * P:(b + 1) * P], q[s][:, b * P:(b + 1) * P], keys[s][:], start=True, stop=True)
                last.then_inc(s_done, 1)
                for n in range(FILL):
                    fill.product(pe, h, n)

            turns(pe, PEER_HEADS, turn)

        @block.scalar
        def _(act):
            def soft(h):
                act.wait_ge(e_in, h + 1)
                act.activation(ex[:], ex[:], ACT.Exp).then_inc(e_done, 1)

            def high(h, s):
                act.wait_ge(w_in[s], h * 16 + 16)
                wait_count(act, q_done, h * 2 + s - 1)
                wait_count(act, wq_lo, h * 2 + s - 1)
                act.copy(w_hi[s][:], w[s][:]).then_inc(wq_hi, 1)

            def turn(h, last=False):
                for s in range(2):
                    act.wait_ge(q_done, h * 2 + s + 1)
                    wait_count(act, s_done, h)
                    act.copy(q[s][:], ps_q[s][:]).then_inc(q_kept, 1)
                for s in range(2):
                    if not last:
                        high(h + 1, s)
                act.wait_ge(s_done, h + 1)
                wait_count(act, s_read, h)
                for s in range(2):
                    act.copy(scores[:, s], ps_s[s][:].rearrange("p (b k) -> p b k", b=TB)).then_inc(s_copied, 1)
                act.wait_ge(s_copied, h * 2 + 2)
                act.sem_inc(s_used, 1)
                if not (isinstance(h, int) and h == 0):
                    soft(h - 1)
                for n in range(FILL):
                    fill.gelu(act, h, n)
                    fill.high(act, h + 1, n)

            for s in range(2):
                high(0, s)
            for n in range(FILL):
                fill.high(act, 0, n)
            turn(0)
            with act.Fori(1, LAST) as h:
                turn(h)
            turn(LAST, last=True)
            soft(LAST)

        @block.vector
        def _(dve):
            dve.wait_ge(iota_done, 1)

            def turn(h):
                steps = [0]

                def stage(instructions):
                    for ins in instructions:
                        ins.then_inc(chain, 1)
                        steps[0] += 1
                    dve.wait_ge(chain, steps[0])

                both = [(s, b) for s in range(2) for b in range(TB)]
                dve.wait_ge(s_used, h + 1)
                dve.memset(turn_mark[:], 0.0)
                dve.sem_clear(chain)
                stage(dve.max(top[:, s, b, 0:8], scores[:, s, b]) for s, b in both)
                stage([f for s, b in both for f in (
                    dve.match_replace(rest[:, s, b], top[:, s, b, 0:8], scores[:, s, b], NEG),
                    dve.max_index(idx[:, s, b, 0:8], top[:, s, b, 0:8], scores[:, s, b]))])
                dve.sem_inc(s_read, 1)
                stage(dve.max(top[:, s, b, 8:16], rest[:, s, b]) for s, b in both)
                stage(dve.max_index(idx[:, s, b, 8:16], top[:, s, b, 8:16], rest[:, s, b]) for s, b in both)

                def pair_sums(out, of):
                    for a in range(8):
                        n = PAIR_ROWS[a][1]
                        yield dve.tensor_tensor(out[:, :, PAIR_START[a]:PAIR_START[a] + n],
                                                of[:, 0, :, a:a + 1].broadcast_to([P, TB, n]), of[:, 1, :, 0:n], ALU.add)
                    yield dve.tensor_tensor(out[:, :, PAIR_START[8]:N_PAIRS], of[:, 0, :, 8:16],
                                            of[:, 1, :, 0:1].broadcast_to([P, TB, 8]), ALU.add)

                stage([*pair_sums(cand, top), dve.tensor_copy(num[:, 1], idx[:, 1]),
                       dve.tensor_scalar(num[:, 0], idx[:, 0], float(N_KEYS), None, ALU.mult)])
                stage([*(dve.max(ctop[:, b, 0:8], cand[:, b]) for b in range(TB)), *pair_sums(cnum, num)])
                stage([f for b in range(TB) for f in (
                    dve.match_replace(crest[:, b], ctop[:, b, 0:8], cand[:, b], NEG),
                    dve.max_index(cpos[:, b, 0:8], ctop[:, b, 0:8], cand[:, b]))])
                stage(dve.max(ctop[:, b, 8:16], crest[:, b]) for b in range(TB))
                if not (isinstance(h, int) and h == 0):
                    gates_of_last(h)
                stage(f for b in range(-1, TB) for f in (
                    [dve.tensor_tensor(ex[:], ctop[:], ctop[:, :, 0:1].broadcast_to([P, TB, TOPK]), ALU.subtract)] if b < 0 else
                    [dve.max_index(cpos[:, b, 8:16], ctop[:, b, 8:16], crest[:, b])]))
                dve.sem_inc(e_in, 1)
                stage([dve.tensor_copy(cposf[:], cpos[:])])
                stage(dve.tensor_tensor(hit[:, b], cposf[:, b].rearrange("p (k o) -> p k o", o=1).broadcast_to([P, TOPK, N_PAIRS]),
                                        iota50[:].rearrange("p (o n) -> p o n", o=1).broadcast_to([P, TOPK, N_PAIRS]), ALU.is_equal)
                      for b in range(TB))
                stage(dve.tensor_tensor(hit[:, b], hit[:, b], cnum[:, b].rearrange("p (o n) -> p o n", o=1).broadcast_to([P, TOPK, N_PAIRS]), ALU.mult)
                      for b in range(TB))
                stage([dve.tensor_reduce(picked[:], hit[:], AX.X, ALU.add)])
                stage([dve.tensor_copy(expert[:, :, ds(h * TOPK, TOPK)], picked[:])])

            def gates_of_last(h):
                dve.wait_ge(e_done, h)
                dve.tensor_reduce(tot[:], ex[:], AX.X, ALU.add).then_inc(gate_chain, 1)
                dve.wait_ge(gate_chain, h * 3 - 2)
                dve.reciprocal(tot[:], tot[:]).then_inc(gate_chain, 1)
                dve.wait_ge(gate_chain, h * 3 - 1)
                dve.tensor_tensor(gate[:, :, ds((h - 1) * TOPK, TOPK)], ex[:], tot[:].broadcast_to([P, TB, TOPK]), ALU.mult)\
                   .then_inc(gate_chain, 1)
                dve.wait_ge(gate_chain, h * 3)

            turns(dve, PEER_HEADS, turn)
            gates_of_last(PEER_HEADS)


def dense_gates(nc, io, keep, picks, g_dram, acts, fill):
    with ExitStack() as ctx:
        sb = lambda n, s, d=F32: ctx.enter_context(nc.sbuf_tensor(n, s, d))
        pb = lambda n, s: ctx.enter_context(nc.psum_tensor(n, s, F32))
        sem = lambda n: ctx.enter_context(nc.semaphore(n))
        expert, gate = picks
        whole = sb("whole", [P, TB, P], I32)
        part = sb("part", [P, 2, TB, P], I32)
        ij = sb("ij", [P, 2, TB, P])
        cols = sb("pick_cols", [P, 3, T])
        BATCH, PB, PER = 8, 4, 4
        HB = 2
        hot_i = [sb(f"hot_i{n}", [P, BATCH, P]) for n in range(HB)]
        hot_j = [sb(f"hot_j{n}", [P, BATCH, P]) for n in range(HB)]
        tile = [sb(f"g_tile{n}", [P, P, G_TOK]) for n in range(2)]
        ps_g = [pb(f"ps_g{n}", [P, PER, P]) for n in range(PB)]
        chain, t_done, c_done = sem("pick_chain"), sem("pick_t"), sem("pick_cols_done")
        hot, g_done, g_kept = sem("hot"), sem("g_done"), sem("g_kept")
        stored = [sem(f"g_stored{n}") for n in range(2)]
        block = ctx.enter_context(nc.Block())
        FILLS = G_TOK // PER
        BATCHES = G_TOK // BATCH
        FPB = BATCH // PER
        cols_of = [ps_g[n][:].rearrange("p t i -> p (t i)") for n in range(3)]
        TURNS = G_TILES // 2
        early = lambda r: PEER_HEADS + r

        REGULAR = [3, 7, 11, 15]
        START, END = [-1, -1, 7, 11], [3, 7, 15, 15]

        def all_turns(eng, body):
            body(0, after=START)
            with eng.Fori(1, TURNS - 1) as r:
                body(r, after=REGULAR)
            body(TURNS - 1, last=True, after=END)

        @block.gpsimd
        def _(pool):
            def turn(r, after, last=False):
                for n in range(0 if last else FILL):
                    fill.low(pool, early(r + 1), n)

            all_turns(pool, turn)

        @block.vector
        def _(dve):
            done = [0]

            def link(ins):
                done[0] += 1
                ins.then_inc(chain, 1)
                dve.wait_ge(chain, done[0])

            link(dve.tensor_copy(whole[:], expert[:]))
            link(dve.tensor_scalar(part[:, 0], whole[:], 7, None, ALU.logical_shift_right))
            link(dve.tensor_scalar(part[:, 1], whole[:], N_KEYS - 1, None, ALU.bitwise_and))
            link(dve.tensor_copy(ij[:], part[:]))
            dve.wait_ge(t_done, 1)
            for n in range(3):
                dve.tensor_copy(cols[:, n], cols_of[n]).then_inc(c_done, 1)
            dve.wait_ge(c_done, 3)

            def turn(r):
                for x in range(2 * BATCHES):
                    n = x % HB
                    t0 = (r * 2 * BATCHES + x) * BATCH
                    wait_count(dve, g_done, (r * 2 * BATCHES + x - HB + 1) * FPB)
                    dve.tensor_tensor(hot_j[n][:], keep["iota"][:].rearrange("p (o j) -> p o j", o=1).broadcast_to([P, BATCH, P]),
                                      cols[:, 1, ds(t0, BATCH)].rearrange("p (t o) -> p t o", o=1).broadcast_to([P, BATCH, P]),
                                      ALU.is_equal).then_inc(hot, 1)
                    for o in range(BATCH):
                        dve.tensor_scalar(hot_i[n][:, o], keep["iota"][:], cols[:, 0, ds(t0 + o, 1)], cols[:, 2, ds(t0 + o, 1)],
                                          ALU.is_equal, ALU.mult).then_inc(hot, 1)

            turns(dve, TURNS, turn)

        @block.tensor
        def _(pe):
            for n in range(START.count(-1)):
                fill.product(pe, early(0), n)
            pe.wait_ge(chain, 4)
            for n in range(3):
                for b in range(TB):
                    src = gate[:, b] if n == 2 else ij[:, n, b]
                    last = pe.transpose(cols_of[n][:, b * P:(b + 1) * P], src, keep["ident"][:])
            last.then_inc(t_done, 1)
            pe.wait_ge(c_done, 3)

            def turn(r, after, last=False):
                for f in range(2 * FILLS):
                    at = r * 2 * FILLS + f
                    x, m = f // FPB, f % PB
                    wait_count(pe, g_kept, at - PB + 1)
                    for o in range(PER):
                        slot = (f % FPB) * PER + o
                        pe.wait_ge(hot, (r * 2 * BATCHES + x) * (BATCH + 1) + slot + 2)
                        last = pe.matmul(ps_g[m][:, o], hot_j[x % HB][:, slot], hot_i[x % HB][:, slot], start=True, stop=True)
                    last.then_inc(g_done, 1)
                    for n in range(FILL):
                        if after[n] == f:
                            fill.product(pe, early(r), n)

            all_turns(pe, turn)

        @block.scalar
        def _(act):
            def block_done(r, n, last):
                fill.gelu(act, early(r), n)
                if not last:
                    fill.high(act, early(r + 1), n)

            def turn(r, after, last=False):
                for f in range(2 * FILLS):
                    n, m = f // FILLS, f % PB
                    if f % FILLS == 0:
                        wait_count(act, stored[n], r * 16)
                    act.wait_ge(g_done, r * 2 * FILLS + f + 1)
                    act.copy(tile[n][:, :, (f % FILLS) * PER:(f % FILLS + 1) * PER], ps_g[m][:].rearrange("p t i -> p i t")).then_inc(g_kept, 1)
                    for j in range(FILL):
                        if after[j] + 2 == f:
                            block_done(r, j, last)
                for j in range(FILL):
                    if after[j] + 2 >= 2 * FILLS:
                        block_done(r, j, last)

            all_turns(act, turn)

        @block.sync
        def _(sp):
            def turn(r, after, last=False):
                for n in range(0 if last else FILL):
                    fill.load(sp, early(r + 1), n)
                for n in range(2):
                    sp.wait_ge(g_kept, (r * 2 + n + 1) * FILLS)
                    sp.dma_start(g_dram[ds(r * 2 + n, 1)].rearrange("o p i t -> (o p) (i t)"),
                                 tile[n][:].rearrange("p i t -> p (i t)")).then_inc(stored[n], 16)
                    for m in range(n * FILL // 2, (n + 1) * FILL // 2):
                        fill.store(sp, early(r), m, acts)

            all_turns(sp, turn)
            for n in range(2):
                sp.wait_ge(stored[n], TURNS * 16)
            for n in range(FILL):
                sp.wait_ge(fill.stored[n], early(TURNS) * 16)


def experts(nc, io, keep, g_dram, acts, yT):
    with ExitStack() as ctx:
        sb = lambda n, s, d=F32: ctx.enter_context(nc.sbuf_tensor(n, s, d))
        pb = lambda n, s: ctx.enter_context(nc.psum_tensor(n, s, F32))
        sem = lambda n: ctx.enter_context(nc.semaphore(n))
        h_hi, h_lo = keep["h_hi"], keep["h_lo"]
        HALF = GROUP // 2
        UR, US, VR, VS = 2, 2, 4, 4
        HC = D // 2
        u_raw = [sb(f"u_raw{n}", [P, KD, P]) for n in range(UR)]
        u_hi = [sb(f"u_hi{n}", [P, KD, P], F32R) for n in range(US)]
        u_lo = [sb(f"u_lo{n}", [P, KD, P], F32R) for n in range(US)]
        v_raw = [sb(f"v_raw{n}", [P, HC]) for n in range(VR)]
        v_hi = [sb(f"v_hi{n}", [P, HC], F32R) for n in range(VS)]
        v_lo = [sb(f"v_lo{n}", [P, HC], F32R) for n in range(VS)]
        gates = [sb(f"gates{n}", [P, G_TILES, HALF, G_TOK]) for n in range(2)]
        wt = [sb(f"act{n}", [P, T]) for n in range(HALF)]
        w_hi = [sb(f"w_hi{n}", [P, T], F32R) for n in range(GROUP)]
        w_lo = [sb(f"w_lo{n}", [P, T], F32R) for n in range(GROUP)]
        ps_a = [pb(f"ps_a{n}", [P, T]) for n in range(HALF)]
        ps_y = [pb(f"ps_y{n}", [P, T]) for n in range(4)]
        u_in = [sem(f"u_in{n}") for n in range(UR)]
        v_in = [sem(f"v_in{n}") for n in range(VR)]
        a_in = [sem(f"a_in{n}") for n in range(HALF)]
        g_in = [sem(f"g_in{n}") for n in range(2)]
        uhi, ulo, vhi, vlo = sem("u_hi_done"), sem("u_lo_done"), sem("v_hi_done"), sem("v_lo_done")
        u_mul, v_mul, act_done, w_done, whi, wlo = sem("u_mul"), sem("v_mul"), sem("act_done"), sem("w_gated"), sem("w_hi_done"), sem("w_lo_done")
        y_kept = sem("y_kept")
        block = ctx.enter_context(nc.Block())
        READY = FILLED // GROUP
        LOADED, MADE = "loaded", "made"
        u_at = lambda g, n: (g - READY) * GROUP + n
        v_at = lambda g, half, n: g * 2 * GROUP + half * GROUP + n

        def y_banks(half, after):
            return ps_a if half == 1 and after is LOADED else ps_y

        def group_loop(eng, body):
            body(0, LOADED, LOADED)
            with eng.Fori(1, READY - 1) as g:
                body(g, LOADED, LOADED)
            body(READY - 1, LOADED, MADE)
            body(READY, MADE, MADE)
            with eng.Fori(READY + 1, N_GROUPS - 1) as g:
                body(g, MADE, MADE)
            body(N_GROUPS - 1, MADE, None)

        def order(lift_u, lift_v, first_step, second_step, add_y, loop):
            for n in range(GROUP - 1):
                first_step(0, n, LOADED)
                if n >= 1:
                    second_step(0, n - 1)
                    if n <= 3:
                        lift_v(0, 0, n - 1)

            def body(g, mine, after):
                lifted = mine is LOADED
                if not lifted:
                    lift_v(g, 0, 0)
                    lift_v(g, 0, 1)
                first_step(g, GROUP - 1, mine)
                second_step(g, GROUP - 2)
                if not lifted:
                    lift_v(g, 0, 2)
                second_step(g, GROUP - 1)
                for n in range(3, GROUP):
                    lift_v(g, 0, n)
                if after is None:
                    add_y(g, 0, after)
                    for n in range(GROUP):
                        lift_v(g, 1, n)
                    add_y(g, 1, after)
                    return
                g1 = g + 1
                if after is MADE:
                    lift_u(g1, 0)
                    lift_u(g1, 1)
                    add_y(g, 0, after)
                    first_step(g1, 0, after)
                    lift_u(g1, 2)
                    first_step(g1, 1, after)
                    lift_u(g1, 3)
                    first_step(g1, 2, after)
                    lift_v(g, 1, 0)
                    lift_v(g, 1, 1)
                    first_step(g1, 3, after)
                    lift_v(g, 1, 2)
                else:
                    lift_v(g, 1, 0)
                    lift_v(g, 1, 1)
                    lift_v(g, 1, 2)
                    add_y(g, 0, after)
                    for n in range(HALF):
                        first_step(g1, n, after)
                for n in range(3, GROUP):
                    lift_v(g, 1, n)
                    if n <= 6:
                        second_step(g1, n - 3)
                if after is LOADED:
                    lift_v(g1, 0, 0)
                    first_step(g1, 4, after)
                    lift_v(g1, 0, 1)
                    first_step(g1, 5, after)
                    second_step(g1, 4)
                    lift_v(g1, 0, 2)
                    add_y(g, 1, after)
                    first_step(g1, 6, after)
                    second_step(g1, 5)
                    return
                lift_u(g1, 4)
                lift_u(g1, 5)
                add_y(g, 1, after)
                first_step(g1, 4, after)
                lift_u(g1, 6)
                first_step(g1, 5, after)
                second_step(g1, 4)
                lift_u(g1, 7)
                first_step(g1, 6, after)
                second_step(g1, 5)

            loop(body)

        @block.sync
        def _(sp):
            def load_u(g, n):
                wait_count(sp, ulo, u_at(g, n) - UR + 1)
                sp.dma_start(u_raw[n % UR][:], io["u"][ds(g * GROUP + n, 1)].rearrange("o p k e -> (o p) k e")).then_inc(u_in[n % UR], 16)

            def load_act(g, n):
                wait_count(sp, wlo, g * GROUP + n - HALF + 1)
                sp.dma_start(wt[n % HALF][:], acts[ds(g * GROUP + n, 1)].rearrange("o p t -> (o p) t")).then_inc(a_in[n % HALF], 16)

            def load_g(g, half):
                wait_count(sp, w_done, g * GROUP + half * HALF - HALF)
                src = g_dram[:].rearrange("a p (q i) t -> q p a i t", i=HALF)[ds(g * 2 + half, 1)]
                sp.dma_start(gates[half][:], src.rearrange("o p a i t -> (o p) a i t")).then_inc(g_in[half], 16)

            def load_v(g, half, n):
                wait_count(sp, vlo, v_at(g, half, n) - VR + 1)
                sp.dma_start(v_raw[n % VR][:], io["v"][ds(g * GROUP + n, 1)].rearrange("o p d -> (o p) d")[:, half * HC:(half + 1) * HC])\
                  .then_inc(v_in[n % VR], 16)

            load_g(0, 0)
            for n in range(HALF):
                load_act(0, n)
            for n in range(VR):
                load_v(0, 0, n)
            load_g(0, 1)
            for n in range(HALF, GROUP):
                load_act(0, n)

            def group(g, mine, after):
                for half in range(2):
                    for n in range(GROUP):
                        if not (isinstance(g, int) and g == 0 and half == 0 and n < VR):
                            load_v(g, half, n)
                        if n == HALF - 1 and after:
                            load_g(g + 1, half)
                    if after:
                        for n in range(half * HALF, half * HALF + HALF):
                            (load_u if after is MADE else load_act)(g + 1, n)

            group_loop(sp, group)

        @block.scalar
        def _(act):
            def split_u(g, n):
                act.wait_ge(u_in[n % UR], ((g - READY) * (GROUP // UR) + n // UR + 1) * 16)
                wait_count(act, u_mul, u_at(g, n) - US + 1)
                wait_count(act, ulo, u_at(g, n) - US + 1)
                act.copy(u_hi[n % US][:], u_raw[n % UR][:]).then_inc(uhi, 1)

            def split_v(g, half, n):
                act.wait_ge(v_in[n % VR], (g * (2 * GROUP // VR) + half * (GROUP // VR) + n // VR + 1) * 16)
                wait_count(act, v_mul, v_at(g, half, n) - VS + 1)
                wait_count(act, vlo, v_at(g, half, n) - VS + 1)
                act.copy(v_hi[n % VS][:], v_raw[n % VR][:]).then_inc(vhi, 1)

            def gelu(g, n, how):
                if how is MADE:
                    act.wait_ge(u_mul, u_at(g, n) + 1)
                    act.wait_ge(wlo, g * GROUP + n - HALF + 1)
                    act.activation(wt[n % HALF][:], ps_a[n % HALF][:], ACT.Gelu).then_inc(act_done, 1)

            def w_high(g, n):
                act.wait_ge(w_done, g * GROUP + n + 1)
                if not (isinstance(g, int) and g == 0):
                    act.wait_ge(v_mul, v_at(g - 1, 1, n) + 1)
                act.copy(w_hi[n][:], wt[n % HALF][:]).then_inc(whi, 1)

            order(split_u, split_v, gelu, w_high, lambda g, half, after: None, lambda body: group_loop(act, body))

        @block.vector
        def _(dve):
            def split_u(g, n):
                dve.wait_ge(uhi, u_at(g, n) + 1)
                wait_count(dve, u_mul, u_at(g, n) - US + 1)
                dve.tensor_tensor(u_lo[n % US][:], u_raw[n % UR][:], u_hi[n % US][:].bitcast(F32), ALU.subtract).then_inc(ulo, 1)

            def split_v(g, half, n):
                dve.wait_ge(vhi, v_at(g, half, n) + 1)
                wait_count(dve, v_mul, v_at(g, half, n) - VS + 1)
                dve.tensor_tensor(v_lo[n % VS][:], v_raw[n % VR][:], v_hi[n % VS][:].bitcast(F32), ALU.subtract).then_inc(vlo, 1)

            def weigh(g, n, how):
                if how is MADE:
                    dve.wait_ge(act_done, u_at(g, n) + 1)
                else:
                    dve.wait_ge(a_in[n % HALF], (g * 2 + n // HALF + 1) * 16)
                dve.wait_ge(g_in[n // HALF], g * 16 + 16)
                w = wt[n % HALF][:].rearrange("p (a t) -> p a t", a=G_TILES)
                dve.tensor_tensor(w, w, gates[n // HALF][:, :, n % HALF], ALU.mult).then_inc(w_done, 1)

            def w_low(g, n):
                dve.wait_ge(whi, g * GROUP + n + 1)
                if not (isinstance(g, int) and g == 0):
                    dve.wait_ge(v_mul, v_at(g - 1, 1, n) + 1)
                dve.tensor_tensor(w_lo[n][:], wt[n % HALF][:], w_hi[n][:].bitcast(F32), ALU.subtract).then_inc(wlo, 1)

            def add_y(g, half, after):
                dve.wait_ge(v_mul, v_at(g, half, GROUP))
                first = isinstance(g, int) and g == 0
                if not first:
                    dve.wait_ge(y_kept, g * 8 + half * 4 - 4)
                for c in range(4):
                    y = yT[:, half * 4 + c]
                    ps = y_banks(half, after)[c][:]
                    if first:
                        dve.tensor_copy(y, ps).then_inc(y_kept, 1)
                    else:
                        dve.tensor_tensor(y, y, ps, ALU.add).then_inc(y_kept, 1)

            order(split_u, split_v, weigh, w_low, add_y, lambda body: group_loop(dve, body))

        @block.tensor
        def _(pe):
            def u_products(g, n):
                pe.wait_ge(ulo, u_at(g, n) + 1)
                wait_count(pe, act_done, u_at(g, n) - HALF + 1)
                for k in range(KD):
                    hi, lo = u_hi[n % US][:, k], u_lo[n % US][:, k]
                    pe.matmul(ps_a[n % HALF][:], hi, h_hi[:, k], start=(k == 0), stop=False)
                    pe.matmul(ps_a[n % HALF][:], hi, h_lo[:, k], start=False, stop=False)
                    last = pe.matmul(ps_a[n % HALF][:], lo, h_hi[:, k], start=False, stop=(k == KD - 1))
                last.then_inc(u_mul, 1)

            def v_products(g, half, n, mine, after):
                pe.wait_ge(vlo, v_at(g, half, n) + 1)
                pe.wait_ge(wlo, g * GROUP + n + 1)
                if n == 0:
                    alone = after is LOADED or (half == 0 and mine is LOADED)
                    wait_count(pe, y_kept, g * 8 + half * 4 - (4 if alone else 0))
                ps_y_of = y_banks(half, after)
                for c in range(4):
                    hi, lo = v_hi[n % VS][:, c * P:(c + 1) * P], v_lo[n % VS][:, c * P:(c + 1) * P]
                    pe.matmul(ps_y_of[c][:], hi, w_hi[n][:], start=(n == 0), stop=False)
                    pe.matmul(ps_y_of[c][:], hi, w_lo[n][:], start=False, stop=False)
                    last = pe.matmul(ps_y_of[c][:], lo, w_hi[n][:], start=False, stop=(n == GROUP - 1))
                last.then_inc(v_mul, 1)

            def group(g, mine, after):
                for half in range(2):
                    for n in range(GROUP):
                        v_products(g, half, n, mine, after)
                    if after is MADE:
                        if half == 0 and mine is LOADED:
                            pe.wait_ge(y_kept, g * 8)
                        for n in range(half * HALF, half * HALF + HALF):
                            u_products(g + 1, n)

            group_loop(pe, group)


def finish(nc, io, keep, yT):
    with ExitStack() as ctx:
        sb = lambda n, s, d=F32: ctx.enter_context(nc.sbuf_tensor(n, s, d))
        sem = lambda n: ctx.enter_context(nc.semaphore(n))
        xT, mod = keep["xT"], keep["mod"]
        sq = sb("sq_y", [P, KD, T])
        g_fin = sb("g_final", [P, KD])
        rstd = sb("rstd_y", [P, T])
        ps = ctx.enter_context(nc.psum_tensor("ps_sum_y", [P, T], F32))
        g_in, x_done, sq_done, sum_done, ln_done, rstd_done, o_done, stored = (
            sem("gf_in"), sem("x2_done"), sem("sq_y_done"), sem("sum_y_done"), sem("ln_y_done"), sem("rstd_y_done"), sem("out_done"), sem("stored"))
        block = ctx.enter_context(nc.Block())

        @block.sync
        def _(sp):
            sp.dma_start(g_fin[:], io["g_final"]).then_inc(g_in, 16)
            for k in range(KD):
                sp.wait_ge(o_done, k + 1)
                sp.dma_start(io["out"][:, k], yT[:, k]).then_inc(stored, 16)
            sp.wait_ge(stored, 16 * KD)

        @block.vector
        def _(dve):
            for k in range(KD):
                dve.scalar_tensor_tensor(xT[:, k], yT[:, k], mod[:, 5 * KD + k:5 * KD + k + 1], xT[:, k], ALU.mult, ALU.add)\
                   .then_inc(x_done, 1)
            dve.wait_ge(rstd_done, 1)
            dve.wait_ge(g_in, 16)
            dve.wait_ge(x_done, KD)
            for k in range(KD):
                dve.scalar_tensor_tensor(yT[:, k], xT[:, k], g_fin[:, k:k + 1], rstd[:], ALU.mult, ALU.mult).then_inc(o_done, 1)

        @block.scalar
        def _(act):
            act.preload_act_table_set("natural_log_exp_and_others")
            for k in range(KD):
                act.wait_ge(x_done, k + 1)
                act.activation(sq[:, k], xT[:, k], ACT.Square).then_inc(sq_done, 1)
            act.wait_ge(sum_done, 1)
            act.activation(rstd[:], ps[:], ACT.Ln, bias=keep["eps"][:], scale=1.0 / D).then_inc(ln_done, 1)
            act.wait_ge(ln_done, 1)
            act.activation(rstd[:], rstd[:], ACT.Exp, scale=-0.5).then_inc(rstd_done, 1)

        @block.tensor
        def _(pe):
            for k in range(KD):
                pe.wait_ge(sq_done, k + 1)
                last = pe.matmul(ps[:], keep["ones"][:], sq[:, k], start=(k == 0), stop=(k == KD - 1))
            last.then_inc(sum_done, 1)


def program(nc, io):
    with ExitStack() as top:
        sb = lambda n, s, d=F32: top.enter_context(nc.sbuf_tensor(n, s, d))
        keep = {
            "xT": sb("xT", [P, KD, T]), "mod": sb("mod", [P, 6 * KD]), "gains": sb("gains", [P, KD]),
            "ones": sb("ones", [P, P]), "neg_ones": sb("neg_ones", [P, P]), "pair_ones": sb("pair_ones", [P, P]),
            "ident": sb("ident", [P, P]), "neg_tri": sb("neg_tri", [P, P]), "iota": sb("iota", [P, P]), "eps": sb("eps", [P, 1]),
        }
        g_dram = nc.dram_tensor("gate_tiles", [G_TILES, P, N_KEYS, G_TOK], F32, kind="Internal").ap()
        keep["w_out_in"] = top.enter_context(nc.semaphore("w_out_in"))
        with ExitStack() as mix:
            msb = lambda n, s: mix.enter_context(nc.sbuf_tensor(n, s, F32, side="right"))
            t16, v8, gx = msb("t16", [P, N_PROJ, T]), msb("v8", [P, 2, TB, T]), msb("gate_x", [P, GLA_PAIRS, T])
            with ExitStack() as front:
                for n in ("h_hi", "h_lo"):
                    keep[n] = front.enter_context(nc.sbuf_tensor(f"{n}_mixer", [P, KD, T], F32R))
                front_stage(nc, io, keep, t16, v8, gx)
            keep["w_out"] = sb("w_out_raw", [P, KD, KD, P])
            catT = msb("catT", [P, KD, T])
            stick_breaking(nc, io, keep, t16, v8, catT)
            gated_linear(nc, io, keep, t16, v8, gx, catT)
            for n in ("h_hi", "h_lo"):
                keep[n] = sb(n, [P, KD, T], F32R)
            mixer_back(nc, io, keep, t16, v8, catT)
        with ExitStack() as front:
            fsb = lambda n, s, d=F32: front.enter_context(nc.sbuf_tensor(n, s, d))
            picks = (fsb("expert", [P, TB, P]), fsb("gate", [P, TB, P]))
            acts = nc.dram_tensor("activations", [FILLED, P, T], F32, kind="Internal").ap()
            fill = BlockProducts(nc, front, io, keep, FILL)
            retrieval(nc, io, keep, picks, acts, fill)
            dense_gates(nc, io, keep, picks, g_dram, acts, fill)
        with ExitStack() as back:
            yT = back.enter_context(nc.sbuf_tensor("yT", [P, KD, T], F32))
            experts(nc, io, keep, g_dram, acts, yT)
            finish(nc, io, keep, yT)


def kernel(**inputs):
    import numpy as np
    import concourse.bacc as bacc
    from concourse.bass_utils import run_bass_kernel_spmd

    nc = bacc.Bacc("TRN2", target_bir_lowering=False, num_devices=1)
    arrays = laid_out(np, inputs)
    io = {n: nc.dram_tensor(f"in_{n}", a.shape, mybir.dt.from_np(a.dtype), kind="ExternalInput").ap() for n, a in arrays.items()}
    io["out"] = nc.dram_tensor("out_0", (P, KD, T), F32, kind="ExternalOutput").ap()
    program(nc, io)
    r = run_bass_kernel_spmd(nc, [{f"in_{n}": a for n, a in arrays.items()}], core_ids=[0])
    out = r.results[0]["out_0"]
    return np.ascontiguousarray(out.transpose(2, 1, 0)).reshape(1, T, D)


def laid_out(np, inputs):
    get = lambda n: np.asarray(inputs[n])
    chunks = lambda w, n: w.reshape(KD, P, w.shape[1] // n, n).transpose(2, 1, 0, 3)
    cols = lambda v: v.reshape(-1, P).T
    w_in = get("w_in")[0]
    at = np.cumsum([0, 512, 512, 512, 256, 256, 512, GLA_RANK, 512])
    part = [w_in[:, a:b] for a, b in zip(at[:-1], at[1:])]
    sq, sk, sv, gq, gk, gv, lr, gr = part
    arrays = {
        "xT": get("x")[0].T.reshape(KD, P, T).transpose(1, 0, 2),
        "cT": cols(get("c")[0]),
        "w_ada": chunks(get("w_ada")[0], 512),
        "b_ada": cols(get("b_ada")[0]),
        "gains": np.concatenate([cols(get("g_sb_norm")[0]), cols(get("g_gla_norm")[0])], axis=1),
        "w_proj": chunks(np.concatenate([sq, sk, gq, gk, gr], axis=1), P),
        "w_lr": chunks(lr, GLA_RANK)[0],
        "w_values": np.concatenate([sv.reshape(KD, P, T), gv.reshape(KD, P, T)]),
        "gate_up": get("w_gla_gate_up")[0],
        "b_gate": cols(get("b_gla_gate")[0]),
        "w_out": chunks(get("w_out")[0], P).transpose(1, 0, 2, 3),
        "w_q": chunks(get("w_peer_q")[0], P),
        "keys_a": get("peer_keys_a")[0].transpose(0, 2, 1),
        "keys_b": get("peer_keys_b")[0].transpose(0, 2, 1),
        "u": get("peer_u")[0].reshape(N_KEYS, P, KD, P).transpose(0, 3, 2, 1),
        "v": get("peer_v")[0].reshape(N_KEYS, P, D),
        "g_final": cols(get("g_final")),
    }
    return {n: np.ascontiguousarray(a) for n, a in arrays.items()}
```

```python
from contextlib import ExitStack

import concourse.bass as bass
from concourse import mybir
from concourse.bass import ds

F32 = mybir.dt.float32
F32R = mybir.dt.float32r
U32 = mybir.dt.uint32
I32 = mybir.dt.int32
ALU = mybir.AluOpType
ACT = mybir.ActivationFunctionType
AX = mybir.AxisListType

P = 128
D, T = 1024, 512
KD = D // P
TB = T // P
EPS = 1e-6
SB_HEADS, SB_DH = 8, 64
GLA_HEADS, GLA_DK, GLA_DV, GLA_CHUNK, GLA_RANK, GLA_TAU = 4, 64, 128, 64, 16, 16.0
GLA_PAIRS = GLA_HEADS // 2
N_CHUNKS = T // GLA_CHUNK
PEER_HEADS, N_KEYS, TOPK = 8, 128, 16
SBQ, SBK, GLQ, GLK, GLR, N_PROJ = 0, 4, 8, 10, 12, 16
NEG = -3.0e38
PAIR_ROWS = [(a, TOPK // (a + 1)) for a in range(TOPK)]
PAIR_START = [sum(n for _, n in PAIR_ROWS[:a]) for a in range(TOPK)]
N_PAIRS = sum(n for _, n in PAIR_ROWS)
G_TOK = 32
G_TILES = T // G_TOK
FILL = 4
EARLY_BLOCKS = 2
FILLED = FILL * (PEER_HEADS + G_TILES // 2)
GROUP = 8
N_GROUPS = N_KEYS // GROUP


def turns(eng, n, body):
    body(0)
    with eng.Fori(1, n) as i:
        body(i)


def wait_count(eng, sem, count):
    if not isinstance(count, int) or count > 0:
        eng.wait_ge(sem, count)


def front_stage(nc, io, keep, t16, v8, gx):
    with ExitStack() as ctx:
        sb = lambda n, s, d=F32: ctx.enter_context(nc.sbuf_tensor(n, s, d))
        pb = lambda n, s: ctx.enter_context(nc.psum_tensor(n, s, F32))
        sem = lambda n: ctx.enter_context(nc.semaphore(n))
        xT, mod, h_hi, h_lo = keep["xT"], keep["mod"], keep["h_hi"], keep["h_lo"]
        COLS = 512
        N_ADA, EARLY, TURNS, PAIR = 6 * D // COLS, 2 * D // COLS, N_PROJ // 2, 2
        PER = COLS // P
        assert N_ADA - EARLY == TURNS
        cT = sb("cT", [P, KD])
        c_act = sb("c_act", [P, KD])
        b_cols = sb("b_cols", [P, 6 * KD])
        w_ada = [sb(f"w_ada{n}", [P, KD, COLS]) for n in range(3)]
        ada = [sb(f"ada_sum{n}", [P, COLS]) for n in range(2)]
        sq = sb("sq_x", [P, 2, T])
        rstd = sb("rstd_x", [P, T])
        scaled = sq
        full = sb("full_h", [P, 2, T])
        w = [sb(f"w_proj{n}", [P, KD, P]) for n in range(PAIR)]
        w_hi = [sb(f"w_proj_hi{n}", [P, KD, P], F32R) for n in range(PAIR)]
        w_lo = [sb(f"w_proj_lo{n}", [P, KD, P], F32R) for n in range(PAIR)]
        wv = [sb(f"w_val{n}", [P, T]) for n in range(2)]
        wv_hi = [sb(f"w_val_hi{n}", [P, T], F32R) for n in range(2)]
        wv_lo = [sb(f"w_val_lo{n}", [P, T], F32R) for n in range(2)]
        wl = sb("w_lr", [P, KD, GLA_RANK])
        wl_hi = sb("w_lr_hi", [P, KD, GLA_RANK], F32R)
        wl_lo = sb("w_lr_lo", [P, KD, GLA_RANK], F32R)
        lrT = sb("lrT", [GLA_RANK, T])
        up = sb("gate_up", [GLA_RANK, GLA_PAIRS * P])
        b_gate = sb("b_gate", [P, GLA_PAIRS])
        ps_sum = pb("ps_sum_x", [P, T])
        ps_mod = pb("ps_mod", [P, 6 * KD])
        ps = [pb(f"ps_proj{n}", [P, T]) for n in range(PAIR)]
        ps_v = [pb(f"ps_val{n}", [P, T]) for n in range(TB)]
        small_in, x_in, late_in = sem("small_in"), sem("x_in"), sem("late_in")
        ada_in = [sem(f"ada_in{n}") for n in range(3)]
        w_in = [sem(f"w_proj_in{n}") for n in range(PAIR)]
        wv_in = [sem(f"wv_in{n}") for n in range(2)]
        consts, silu_done, sq_done, sum_done = sem("consts"), sem("silu_done"), sem("sq_done"), sem("sum_done")
        ln_done, rstd_done, chain, ada_read = sem("ln_done"), sem("rstd_done"), sem("ada_chain"), sem("ada_read")
        mod_done, mod_kept = sem("mod_done"), sem("mod_kept")
        scaled_done, full_done, hhi, hlo = sem("scaled_done"), sem("full_done"), sem("h_hi_done"), sem("h_lo_done")
        whi, wlo, prod, kept = sem("w_hi_done"), sem("w_lo_done"), sem("proj_done"), sem("proj_kept")
        lhi, llo, l_done, l_kept, g_done = sem("lr_hi"), sem("lr_lo"), sem("lr_done"), sem("lr_kept"), sem("gate_done")
        vhi, vlo, v_mul, v_kept = sem("wv_hi_done"), sem("wv_lo_done"), sem("v_mul"), sem("v_kept")
        block = ctx.enter_context(nc.Block())
        N_VAL = 2 * KD

        def projection_turns(eng, turn):
            with eng.Fori(0, (TURNS - 1) // 2) as i:
                turn(i, 0)
                turn(i, 1)
            turn((TURNS - 1) // 2, 0)

        @block.sync
        def _(sp):
            def load_ada(m, slot):
                sp.dma_start(w_ada[slot][:], io["w_ada"][ds(m, 1)].rearrange("o p k c -> (o p) k c")).then_inc(ada_in[slot], 16)

            def load_w(i, n):
                wait_count(sp, wlo, i * PAIR + n - PAIR + 1)
                sp.dma_start(w[n][:], io["w_proj"][ds(i * PAIR + n, 1)].rearrange("o p k c -> (o p) k c")).then_inc(w_in[n], 16)

            sp.dma_start(cT[:], io["cT"]).then_inc(small_in, 16)
            sp.dma_start(b_cols[:], io["b_ada"]).then_inc(small_in, 16)
            load_ada(0, 0)
            sp.dma_start(xT[:], io["xT"]).then_inc(x_in, 16)
            for m in range(1, 3):
                load_ada(m, m)
            sp.wait_ge(ada_read, 1)
            load_ada(3, 0)
            for n in range(PAIR):
                load_w(0, n)
            sp.dma_start(keep["gains"][:], io["gains"]).then_inc(late_in, 16)
            sp.dma_start(wl[:], io["w_lr"]).then_inc(late_in, 16)
            sp.dma_start(up[:], io["gate_up"]).then_inc(late_in, 16)
            sp.dma_start(b_gate[:], io["b_gate"]).then_inc(late_in, 16)

            def late_ada(i, e):
                m = EARLY + 2 * i + e
                sp.wait_ge(ada_read, m - 1)
                load_ada(m, 1 + e)

            def turn(i, e):
                late_ada(i, e)
                for n in range(PAIR):
                    load_w(2 * i + e + 1, n)

            projection_turns(sp, turn)
            late_ada((TURNS - 1) // 2, 1)
            for v in range(N_VAL):
                if v >= 2:
                    sp.wait_ge(vlo, v - 1)
                sp.dma_start(wv[v % 2][:], io["w_values"][v]).then_inc(wv_in[v % 2], 16)

        @block.gpsimd
        def _(pool):
            pool.memset(keep["ones"][:], 1.0).then_inc(consts, 1)
            pool.memset(keep["pair_ones"][:], 0.0).then_inc(consts, 1)
            pool.memset(keep["neg_ones"][:], -1.0).then_inc(consts, 1)
            pool.wait_ge(consts, 3)
            for e in range(2):
                pool.memset(keep["pair_ones"][64 * e:64 * e + 64, 64 * e:64 * e + 64], 1.0).then_inc(consts, 1)
                pool.wait_ge(consts, 4 + e)
            pool.affine_select(out=keep["ident"][:], in_=keep["ones"][:], compare_op=ALU.is_equal, fill=0.0, base=0,
                               pattern=[[-1, P]], channel_multiplier=1).then_inc(consts, 1)
            pool.affine_select(out=keep["neg_tri"][:], in_=keep["neg_ones"][:], compare_op=ALU.is_ge, fill=0.0, base=0,
                               pattern=[[-1, P]], channel_multiplier=1).then_inc(consts, 1)
            pool.iota(keep["iota"][:], pattern=[[1, P]], base=0, channel_multiplier=0,
                      allow_small_or_imprecise_dtypes=True).then_inc(consts, 1)
            pool.memset(keep["eps"][:], EPS).then_inc(consts, 1)

            def low(j, n):
                pool.wait_ge(whi, j * PAIR + n + 1)
                wait_count(pool, prod, j * PAIR + n - PAIR + 1)
                pool.tensor_tensor(w_lo[n][:], w[n][:], w_hi[n][:].bitcast(F32), ALU.subtract).then_inc(wlo, 1)

            def turn(i, e):
                for n in range(PAIR):
                    low(2 * i + e + 1, n)

            for n in range(PAIR):
                low(0, n)
            projection_turns(pool, turn)

        @block.scalar
        def _(act):
            def high(i, n):
                act.wait_ge(w_in[n], i * 16 + 16)
                wait_count(act, prod, i * PAIR + n - PAIR + 1)
                wait_count(act, wlo, i * PAIR + n - PAIR + 1)
                act.copy(w_hi[n][:], w[n][:]).then_inc(whi, 1)

            def keep_chunk(i, n):
                act.wait_ge(prod, i * PAIR + n + 1)
                act.copy(t16[:, ds(i * PAIR + n, 1)], ps[n][:].rearrange("p (o t) -> p o t", o=1)).then_inc(kept, 1)

            act.wait_ge(small_in, 32)
            act.activation(c_act[:], cT[:], ACT.Silu).then_inc(silu_done, 1)
            act.wait_ge(x_in, 16)
            for k in range(KD):
                if k >= 2:
                    act.wait_ge(sum_done, k - 1)
                act.activation(sq[:, k % 2], xT[:, k], ACT.Square).then_inc(sq_done, 1)
            act.wait_ge(sum_done, KD)
            act.wait_ge(consts, 9)
            act.activation(rstd[:], ps_sum[:], ACT.Ln, bias=keep["eps"][:], scale=1.0 / D).then_inc(ln_done, 1)
            act.wait_ge(ln_done, 1)
            act.activation(rstd[:], rstd[:], ACT.Exp, scale=-0.5).then_inc(rstd_done, 1)
            for n in range(PAIR):
                high(0, n)
            act.wait_ge(mod_kept, 2)
            for k in range(KD):
                shift = mod[:, k:k + 1]
                act.wait_ge(scaled_done, k + 1)
                act.activation(h_hi[:, k], scaled[:, k % 2], ACT.Identity, bias=shift).then_inc(hhi, 1)
                if k >= 2:
                    act.wait_ge(hlo, k - 1)
                act.activation(full[:, k % 2], scaled[:, k % 2], ACT.Identity, bias=shift).then_inc(full_done, 1)

            def turn(i, e):
                for n in range(PAIR):
                    keep_chunk(2 * i + e, n)
                    high(2 * i + e + 1, n)

            projection_turns(act, turn)
            act.wait_ge(late_in, 64)
            act.copy(wl_hi[:], wl[:]).then_inc(lhi, 1)

            def values_high(v):
                act.wait_ge(wv_in[v % 2], 16 * (v // 2 + 1))
                if v >= 2:
                    act.wait_ge(v_mul, v - 1)
                    act.wait_ge(vlo, v - 1)
                act.copy(wv_hi[v % 2][:], wv[v % 2][:]).then_inc(vhi, 1)

            for n in range(PAIR):
                keep_chunk(TURNS - 1, n)
                values_high(n)
            act.wait_ge(kept, N_PROJ)
            act.activation(t16[:, GLR:GLR + 4], t16[:, GLR:GLR + 4], ACT.Silu)
            act.wait_ge(l_done, 1)
            act.copy(lrT[:], ps_sum[0:GLA_RANK, :]).then_inc(l_kept, 1)
            for v in range(PAIR, N_VAL):
                values_high(v)
                if v == 3:
                    for p in range(GLA_PAIRS):
                        act.wait_ge(g_done, p + 1)
                        act.activation(gx[:, p], ps[p][:], ACT.Identity, bias=b_gate[:, p:p + 1])

        def keep_values(dve, g):
            dve.wait_ge(v_mul, (g + 1) * KD)
            for b in range(TB):
                dve.tensor_copy(v8[:, g, b], ps_v[b][:]).then_inc(v_kept, 1)

        @block.vector
        def _(dve):
            def sum_rows(m, slot, uses, at):
                dve.wait_ge(ada_in[slot], uses * 16)
                wait_count(dve, mod_done, m - 1)
                for k in range(KD):
                    col = c_act[:, k:k + 1]
                    if k == 0:
                        last = dve.tensor_scalar(ada[at][:], w_ada[slot][:, 0], col, None, ALU.mult)
                    else:
                        dve.wait_ge(chain, m * KD + k)
                        last = dve.scalar_tensor_tensor(ada[at][:], w_ada[slot][:, k], col, ada[at][:], ALU.mult, ALU.add)
                    last.then_inc(chain, 1)
                dve.wait_ge(chain, m * KD + KD)
                dve.sem_inc(ada_read, 1)

            dve.wait_ge(silu_done, 1)
            for m in range(EARLY):
                sum_rows(m, m % 3, m // 3 + 1, m % 2)
            n_early = EARLY * PER
            dve.wait_ge(mod_done, EARLY)
            dve.tensor_tensor(mod[:, 0:n_early], ps_mod[:, 0:n_early], b_cols[:, 0:n_early], ALU.add).then_inc(mod_kept, 1)
            dve.wait_ge(mod_kept, 1)
            dve.tensor_scalar(mod[:, KD:2 * KD], mod[:, KD:2 * KD], 1.0, None, ALU.add).then_inc(mod_kept, 1)
            dve.wait_ge(mod_kept, 2)
            dve.wait_ge(rstd_done, 1)
            for k in range(KD + 1):
                if k < KD:
                    if k >= 2:
                        dve.wait_ge(full_done, k - 1)
                    dve.scalar_tensor_tensor(scaled[:, k % 2], xT[:, k], mod[:, KD + k:KD + k + 1], rstd[:], ALU.mult, ALU.mult)\
                       .then_inc(scaled_done, 1)
                if k >= 1:
                    dve.wait_ge(full_done, k)
                    dve.tensor_tensor(h_lo[:, k - 1], full[:, (k - 1) % 2], h_hi[:, k - 1].bitcast(F32), ALU.subtract).then_inc(hlo, 1)

            def turn(i, e):
                sum_rows(EARLY + 2 * i + e, 1 + e, i + 2, e)

            projection_turns(dve, turn)
            turn((TURNS - 1) // 2, 1)
            dve.wait_ge(lhi, 1)
            dve.tensor_tensor(wl_lo[:], wl[:], wl_hi[:].bitcast(F32), ALU.subtract).then_inc(llo, 1)
            for v in range(N_VAL):
                dve.wait_ge(vhi, v + 1)
                if v >= 2:
                    dve.wait_ge(v_mul, v - 1)
                dve.tensor_tensor(wv_lo[v % 2][:], wv[v % 2][:], wv_hi[v % 2][:].bitcast(F32), ALU.subtract).then_inc(vlo, 1)
                if v == KD:
                    keep_values(dve, 0)
                if v == KD + 2:
                    dve.wait_ge(kept, N_PROJ)
                    for n in range(SBK - SBQ):
                        dve.tensor_scalar(t16[:, SBQ + n], t16[:, SBQ + n], SB_DH ** -0.5, None, ALU.mult)
            dve.wait_ge(mod_done, N_ADA)
            dve.tensor_tensor(mod[:, n_early:], ps_mod[:, n_early:], b_cols[:, n_early:], ALU.add).then_inc(mod_kept, 1)
            dve.wait_ge(mod_kept, 3)
            dve.tensor_scalar(mod[:, 4 * KD:5 * KD], mod[:, 4 * KD:5 * KD], 1.0, None, ALU.add)
            keep_values(dve, 1)

        @block.tensor
        def _(pe):
            def mod_columns(m, at):
                pe.wait_ge(chain, m * KD + KD)
                for c in range(PER):
                    col = m * PER + c
                    last = pe.matmul(ps_mod[:, ds(col, 1)], ada[at][:, c * P:(c + 1) * P], keep["ones"][:, 0:1], start=True, stop=True)
                last.then_inc(mod_done, 1)

            def three_passes(n, k):
                hi, lo = w_hi[n][:, k], w_lo[n][:, k]
                pe.matmul(ps[n][:], hi, h_hi[:, k], start=(k == 0), stop=False)
                pe.matmul(ps[n][:], hi, h_lo[:, k], start=False, stop=False)
                return pe.matmul(ps[n][:], lo, h_hi[:, k], start=False, stop=(k == KD - 1))

            def product(i, n):
                pe.wait_ge(wlo, i * PAIR + n + 1)
                wait_count(pe, kept, i * PAIR + n - PAIR + 1)
                for k in range(KD):
                    last = three_passes(n, k)
                last.then_inc(prod, 1)

            pe.wait_ge(consts, 1)
            for k in range(KD):
                pe.wait_ge(sq_done, k + 1)
                pe.matmul(ps_sum[:], keep["ones"][:], sq[:, k % 2], start=(k == 0), stop=(k == KD - 1)).then_inc(sum_done, 1)
            for m in range(EARLY):
                mod_columns(m, m % 2)
            for n in range(PAIR):
                pe.wait_ge(wlo, n + 1)
            for k in range(KD):
                pe.wait_ge(hlo, k + 1)
                for n in range(PAIR):
                    last = three_passes(n, k)
                    if k == KD - 1:
                        last.then_inc(prod, 1)
            pe.wait_ge(mod_kept, 1)

            def turn(i, e):
                mod_columns(EARLY + 2 * i + e, e)
                for n in range(PAIR):
                    product(2 * i + e + 1, n)

            projection_turns(pe, turn)
            mod_columns(N_ADA - 1, 1)
            pe.wait_ge(llo, 1)
            for k in range(KD):
                for a, b in ((wl_hi, h_hi), (wl_hi, h_lo), (wl_lo, h_hi)):
                    last = pe.matmul(ps_sum[0:GLA_RANK, :], a[:, k], b[:, k], start=(k == 0 and b is h_hi and a is wl_hi),
                                     stop=(k == KD - 1 and a is wl_lo))
            last.then_inc(l_done, 1)
            for v in range(N_VAL):
                k = v % KD
                pe.wait_ge(vlo, v + 1)
                for b in range(TB):
                    t = slice(b * P, (b + 1) * P)
                    if v == KD:
                        pe.wait_ge(v_kept, b + 1)
                    pe.matmul(ps_v[b][:], h_hi[:, k, t], wv_hi[v % 2][:], start=(k == 0), stop=False)
                    pe.matmul(ps_v[b][:], h_hi[:, k, t], wv_lo[v % 2][:], start=False, stop=False)
                    last = pe.matmul(ps_v[b][:], h_lo[:, k, t], wv_hi[v % 2][:], start=False, stop=(k == KD - 1))
                last.then_inc(v_mul, 1)
                if v == 2:
                    pe.wait_ge(l_kept, 1)
                    pe.wait_ge(kept, N_PROJ)
                    for p in range(GLA_PAIRS):
                        pe.matmul(ps[p][:], up[:, p * P:(p + 1) * P], lrT[:], start=True, stop=True).then_inc(g_done, 1)


class LinearOperands:
    SCALAR_STEPS, VECTOR_STEPS = 8, 8 + 5 * GLA_PAIRS

    def __init__(self, nc, ctx, t16, gx):
        sb = lambda n, s: ctx.enter_context(nc.sbuf_tensor(n, s, F32, side="right"))
        sem = lambda n: ctx.enter_context(nc.semaphore(n))
        self.t16, self.x = t16, gx
        self.restart = sb("restart", [P, T])
        self.mag = sb("gate_mag", [P, GLA_PAIRS, T])
        self.bc = sb("b_cum16", [P, GLA_PAIRS, T])
        self.k_mid = sb("from_mid", [P, GLA_PAIRS, T])
        self.k_dec = sb("to_last", [P, GLA_PAIRS, T])
        self.q_in = sb("q_intra", [P, GLA_PAIRS, T])
        self.q_st = sb("q_state", [P, GLA_PAIRS, T])
        self.carry = sb("chunk_decay", [P, GLA_PAIRS, N_CHUNKS])
        self.k_in = sb("k_intra", [P, GLA_HEADS, T])
        self.zeros, self.log, self.chain, self.exps = sem("gla_zeros"), sem("gla_log"), sem("gla_decays"), sem("gla_exps")

    def constants(self, pool):
        pool.memset(self.k_in[:], 0.0).then_inc(self.zeros, 1)
        pool.memset(self.restart[:], 1.0).then_inc(self.zeros, 1)
        pool.wait_ge(self.zeros, 2)
        pool.memset(self.restart[:].rearrange("p (c t) -> p c t", c=N_CHUNKS)[:, :, 0:1], 0.0).then_inc(self.zeros, 1)

    def scalar_step(self, act, n):
        if n == 0:
            act.activation(self.mag[:], self.x[:], ACT.Abs).then_inc(self.log, 1)
        elif n == 1:
            act.wait_ge(self.log, 1)
            act.activation(self.mag[:], self.mag[:], ACT.Exp, scale=-1.0).then_inc(self.log, 1)
        elif n == 2:
            act.wait_ge(self.log, 2)
            act.activation(self.mag[:], self.mag[:], ACT.Ln, bias=1.0).then_inc(self.log, 1)
        elif n == 3:
            act.wait_ge(self.chain, 8)
            act.activation(self.q_in[:], self.k_mid[:], ACT.Exp, scale=1.0 / GLA_TAU).then_inc(self.exps, 1)
        elif n == 4:
            act.wait_ge(self.exps, 1)
            act.activation(self.k_mid[:], self.k_mid[:], ACT.Exp, scale=-1.0 / GLA_TAU).then_inc(self.exps, 1)
        elif n == 5:
            act.activation(self.q_st[:], self.bc[:], ACT.Exp, scale=1.0 / GLA_TAU).then_inc(self.exps, 1)
        elif n == 6:
            act.activation(self.k_dec[:], self.k_dec[:], ACT.Exp, scale=1.0 / GLA_TAU).then_inc(self.exps, 1)
        elif n == 7:
            last_row = self.bc[:].rearrange("p a (c t) -> p a c t", c=N_CHUNKS)[:, :, :, GLA_CHUNK - 1]
            act.activation(self.carry[:], last_row, ACT.Exp, scale=1.0 / GLA_TAU).then_inc(self.exps, 1)

    def vector_step(self, dve, n):
        view = lambda tile, p: tile[:, p].rearrange("p (c t) -> p c t", c=N_CHUNKS)
        C = GLA_CHUNK
        if n == 0:
            dve.wait_ge(self.log, 3)
            dve.tensor_scalar(self.x[:], self.x[:], 0.0, None, ALU.min).then_inc(self.chain, 1)
        elif n == 1:
            dve.wait_ge(self.chain, 1)
            dve.tensor_tensor(self.x[:], self.x[:], self.mag[:], ALU.subtract).then_inc(self.chain, 1)
        elif n < 4:
            p = n - 2
            dve.wait_ge(self.chain, 2)
            dve.wait_ge(self.zeros, 3)
            dve.tensor_tensor_scan(self.bc[:, p], self.restart[:], self.x[:, p], 0.0, ALU.mult, ALU.add).then_inc(self.chain, 1)
        elif n < 8:
            p = (n - 4) // 2
            b = view(self.bc, p)
            dve.wait_ge(self.chain, 4)
            if n % 2 == 0:
                mid = b[:, :, C // 2 - 1:C // 2].broadcast_to([P, N_CHUNKS, C])
                dve.tensor_tensor(view(self.k_mid, p), b, mid, ALU.subtract).then_inc(self.chain, 1)
            else:
                end = b[:, :, C - 1:C].broadcast_to([P, N_CHUNKS, C])
                dve.tensor_tensor(view(self.k_dec, p), end, b, ALU.subtract).then_inc(self.chain, 1)
        else:
            p, kind = (n - 8) // 5, (n - 8) % 5
            dve.wait_ge(self.exps, 5)
            k, q = self.t16[:, GLK + p], self.t16[:, GLQ + p]
            if kind == 0:
                dve.tensor_tensor(self.k_dec[:, p], k, self.k_dec[:, p], ALU.mult)
            elif kind < 3:
                out = (self.q_in, self.q_st)[kind - 1][:, p]
                dve.scalar_tensor_tensor(out, q, GLA_DK ** -0.5, out, ALU.mult, ALU.mult)
            else:
                e = kind - 3
                r = slice(64 * e, 64 * e + 64)
                dve.tensor_tensor(self.k_in[r, 2 * p + e], self.t16[r, GLK + p], self.k_mid[r, p], ALU.mult)


def stick_breaking(nc, io, keep, t16, v8, catT, operands):
    with ExitStack() as ctx:
        sb = lambda n, s, d=F32: ctx.enter_context(nc.sbuf_tensor(n, s, d))
        pb = lambda n, s: ctx.enter_context(nc.psum_tensor(n, s, F32))
        sem = lambda n: ctx.enter_context(nc.semaphore(n))
        NU, ZB = SB_HEADS * TB, 6
        mag = sb("z_mag", [P, 2, T])
        ez = sb("z_exp", [P, 2, T])
        lz = sb("z_log", [P, 2, T])
        soft = sb("softplus", [P, 2, TB, T])
        w = sb("sb_weights", [P, 2, TB, T])
        ps_z = [pb(f"ps_z{n}", [P, T]) for n in range(ZB)]
        ps_o = [pb(f"ps_o{n}", [P, T]) for n in range(2)]
        z_done, mag_done, ez_done, lz_done = sem("z_done"), sem("mag_done"), sem("ez_done"), sem("lz_done")
        soft_done, soft_masked, suffix_done = sem("soft_done"), sem("soft_masked"), sem("suffix_done")
        w_done, w_masked, o_done, o_kept = sem("w_done"), sem("w_masked"), sem("o_done"), sem("o_kept")
        block = ctx.enter_context(nc.Block())
        place = lambda u: (u // TB, TB - 1 - u % TB)
        LAG_SUM, LAG_OUT = 2, 6
        SCALAR_AT = [3, 4, 5, 16, 17, 18, 19, 20]
        VECTOR_AT = [*range(6, 14), *range(NU - 10, NU)]
        assert len(SCALAR_AT) == operands.SCALAR_STEPS and len(VECTOR_AT) == operands.VECTOR_STEPS

        @block.sync
        def _(sp):
            sp.dma_start(keep["w_out"][:], io["w_out"]).then_inc(keep["w_out_in"], 16)

        @block.tensor
        def _(pe):
            def scores(u):
                h, s = place(u)
                r, c = 64 * (h % 2), h // 2
                if u >= ZB:
                    pe.wait_ge(w_done, u - ZB + 1)
                pe.matmul(ps_z[u % ZB][:, s * P:T], t16[r:r + 64, SBK + c, s * P:(s + 1) * P], t16[r:r + 64, SBQ + c, s * P:T],
                          start=True, stop=True).then_inc(z_done, 1)

            def outputs(h):
                pe.wait_ge(w_masked, TB * h + TB)
                if h >= 4 and h % 2 == 0:
                    pe.wait_ge(o_kept, h // 2 - 1)
                for s in range(TB):
                    last = pe.matmul(ps_o[h // 2 % 2][64 * (h % 2):64 * (h % 2) + 64, s * P:T], v8[:, 0, s, h * 64:h * 64 + 64],
                                     w[:, h % 2, s, s * P:T], start=(s == 0), stop=(s == TB - 1))
                last.then_inc(o_done, 1)

            for u in range(NU + LAG_OUT):
                if u < NU:
                    scores(u)
                if LAG_SUM <= u < NU + LAG_SUM:
                    v = u - LAG_SUM
                    h, s = place(v)
                    pe.wait_ge(soft_masked, v + 1)
                    for s2 in range(s, TB):
                        last = pe.matmul(ps_z[v % ZB][:, s2 * P:T], keep["neg_tri" if s2 == s else "neg_ones"][:],
                                         soft[:, h % 2, s2, s2 * P:T], start=False, stop=(s2 == TB - 1), skip_group_check=True)
                    last.then_inc(suffix_done, 1)
                if u >= LAG_OUT and (u - LAG_OUT) % TB == TB - 1:
                    outputs((u - LAG_OUT) // TB)

        @block.scalar
        def _(act):
            def weights(u):
                h, s = place(u)
                act.wait_ge(suffix_done, u + 1)
                if h >= 2:
                    act.wait_ge(o_done, h - 1)
                act.activation(w[:, h % 2, s, s * P:T], ps_z[u % ZB][:, s * P:T], ACT.Exp).then_inc(w_done, 1)

            act.preload_act_table_set("natural_log_exp_and_others")
            for u in range(NU + 3):
                if u < NU:
                    h, s = place(u)
                    n = T - s * P
                    act.wait_ge(z_done, u + 1)
                    if u >= 2:
                        act.wait_ge(ez_done, u - 1)
                    act.activation(mag[:, u % 2, 0:n], ps_z[u % ZB][:, s * P:T], ACT.Abs).then_inc(mag_done, 1)
                    act.wait_ge(mag_done, u + 1)
                    if u >= 2:
                        act.wait_ge(lz_done, u - 1)
                    act.activation(ez[:, u % 2, 0:n], mag[:, u % 2, 0:n], ACT.Exp, scale=-1.0).then_inc(ez_done, 1)
                    act.wait_ge(ez_done, u + 1)
                    if u >= 2:
                        act.wait_ge(soft_done, u - 1)
                    act.activation(lz[:, u % 2, 0:n], ez[:, u % 2, 0:n], ACT.Ln, bias=1.0).then_inc(lz_done, 1)
                if u >= 3:
                    weights(u - 3)
                if u in SCALAR_AT:
                    operands.scalar_step(act, SCALAR_AT.index(u))

        @block.vector
        def _(dve):
            def keep_outputs(p):
                dve.wait_ge(o_done, 2 * p + 2)
                dve.tensor_copy(catT[:, p], ps_o[p % 2][:]).then_inc(o_kept, 1)

            for u in range(NU):
                h, s = place(u)
                n = T - s * P
                dve.wait_ge(lz_done, u + 1)
                if h >= 2 and s == TB - 1:
                    dve.wait_ge(suffix_done, TB * (h - 1))
                dve.scalar_tensor_tensor(soft[:, h % 2, s, s * P:T], ps_z[u % ZB][:, s * P:T], 0.0, lz[:, u % 2, 0:n],
                                         ALU.max, ALU.add).then_inc(soft_done, 1)
                if h >= 3 and h % 2 == 1 and s == 0:
                    keep_outputs((h - 3) // 2)
                if u in VECTOR_AT:
                    operands.vector_step(dve, VECTOR_AT.index(u))
            keep_outputs(SB_HEADS // 2 - 1)

        @block.gpsimd
        def _(pool):
            def mask(tile, h, s, done):
                diag = tile[:, h % 2, s, s * P:(s + 1) * P]
                pool.affine_select(out=diag, in_=diag, compare_op=ALU.is_gt, fill=0.0, base=0, pattern=[[1, P]],
                                   channel_multiplier=-1).then_inc(done, 1)

            operands.constants(pool)
            for u in range(NU + 3):
                if u < NU:
                    pool.wait_ge(soft_done, u + 1)
                    mask(soft, *place(u), soft_masked)
                if u >= 3:
                    pool.wait_ge(w_done, u - 2)
                    mask(w, *place(u - 3), w_masked)


def gated_linear(nc, keep, v8, catT, operands):
    with ExitStack() as ctx:
        sb = lambda n, s, d=F32: ctx.enter_context(nc.sbuf_tensor(n, s, d))
        pb = lambda n, s: ctx.enter_context(nc.psum_tensor(n, s, F32))
        sem = lambda n: ctx.enter_context(nc.semaphore(n))
        C, NC = GLA_CHUNK, N_CHUNKS
        causal = sb("gla_causal", [P, C])
        carry, q_in, q_st, k_in, k_dec = operands.carry, operands.q_in, operands.q_st, operands.k_in, operands.k_dec
        kt = sb("k_decayed_t", [P, GLA_PAIRS, NC, P])
        sc = sb("gla_scores", [P, GLA_HEADS, TB, P])
        st = sb("gla_state", [P, GLA_HEADS, 2, GLA_DV])
        sq = sb("sq_sb", [P, TB, T])
        rstd = sb("rstd_sb", [P, TB, T])
        ps_g = [pb(f"ps_gate{n}", [P, T]) for n in range(2)]
        ps_u = [pb(f"ps_upd{n}", [P, T]) for n in range(2)]
        ps_o = [pb(f"ps_gla_o{h}", [P, T]) for h in range(GLA_HEADS)]
        zeros = sem("gla_block_zeros")
        t_done, kt_done, s_done, sc_done = sem("kt_ps"), sem("kt_done"), sem("sc_ps"), sem("sc_done")
        sq_done, sum_done, ln_done, rstd_done = sem("sq_sb_done"), sem("sum_sb_done"), sem("ln_sb_done"), sem("rstd_sb_done")
        u_done, st_done, inter, o_done = sem("upd_done"), sem("state_done"), sem("inter_done"), sem("gla_o_done")
        block = ctx.enter_context(nc.Block())
        upd_bank = lambda p, c: (ps_u, ps_g)[c % 2][p]

        @block.gpsimd
        def _(pool):
            pool.memset(causal[:], 1.0).then_inc(zeros, 1)
            for o in range(2):
                pool.wait_ge(zeros, 1 + o)
                half = causal[64 * o:64 * o + 64, :]
                pool.affine_select(out=half, in_=half, compare_op=ALU.is_ge, fill=0.0, base=0, pattern=[[1, C]],
                                   channel_multiplier=-1).then_inc(zeros, 1)
            pool.wait_ge(zeros, 3)
            for tile in (kt, sc, st):
                pool.memset(tile[:], 0.0).then_inc(zeros, 1)

        @block.scalar
        def _(act):
            for c in range(TB):
                act.activation(sq[:, c], catT[:, c], ACT.Square).then_inc(sq_done, 1)
            for c in range(TB):
                act.wait_ge(sum_done, c + 1)
                act.activation(rstd[:, c], ps_u[c % 2][:], ACT.Ln, bias=keep["eps"][:], scale=1.0 / SB_DH).then_inc(ln_done, 1)
            for c in range(TB):
                act.wait_ge(ln_done, c + 1)
                act.activation(rstd[:, c], rstd[:, c], ACT.Exp, scale=-0.5).then_inc(rstd_done, 1)

        @block.vector
        def _(dve):
            dve.wait_ge(zeros, 6)
            for p in range(GLA_PAIRS):
                dve.wait_ge(t_done, p + 1)
                for o in range(2):
                    r = slice(64 * o, 64 * o + 64)
                    src = ps_g[p][:].rearrange("p (b d) -> p b d", b=TB)
                    dst = kt[:, p].rearrange("p (b o) d -> p b o d", o=2)
                    dve.tensor_copy(dst[r, :, o, :], src[r]).then_inc(kt_done, 1)
            for h in range(GLA_HEADS):
                dve.wait_ge(s_done, h + 1)
                for o in range(2):
                    r = slice(64 * o, 64 * o + 64)
                    src = ps_o[h][:].rearrange("p (b t) -> p b t", b=TB)
                    m = causal[r].rearrange("p (o t) -> p o t", o=1).broadcast_to([64, TB, C])
                    dve.tensor_tensor(sc[r, h, :, o * C:(o + 1) * C], src[r, :, o * C:(o + 1) * C], m, ALU.mult).then_inc(sc_done, 1)
            for c in range(NC - 1):
                dve.wait_ge(u_done, 2 * c + 2)
                if c >= 2:
                    dve.wait_ge(inter, c - 1)
                if c >= 1:
                    dve.wait_ge(st_done, GLA_HEADS * c)
                for h in range(GLA_HEADS):
                    p, e = h // 2, h % 2
                    r = slice(64 * e, 64 * e + 64)
                    new, old = st[r, h, (c + 1) % 2], st[r, h, c % 2]
                    u = upd_bank(p, c)[r, e * P:(e + 1) * P]
                    if c == 0:
                        dve.tensor_copy(new, u).then_inc(st_done, 1)
                    else:
                        dve.scalar_tensor_tensor(new, old, carry[r, p, c:c + 1], u, ALU.mult, ALU.add).then_inc(st_done, 1)
                if 1 <= c <= TB:
                    n = c - 1
                    dve.wait_ge(rstd_done, n + 1)
                    dve.scalar_tensor_tensor(catT[:, n], catT[:, n], keep["gains"][:, n:n + 1], rstd[:, n], ALU.mult, ALU.mult)
            for h in range(GLA_HEADS):
                dve.wait_ge(o_done, 1)
                dve.tensor_copy(catT[:, TB + h], ps_o[h][:])

        @block.tensor
        def _(pe):
            def head_sums(c):
                pe.wait_ge(sq_done, c + 1)
                if c >= 2:
                    pe.wait_ge(ln_done, c - 1)
                pe.matmul(ps_u[c % 2][:], keep["pair_ones"][:], sq[:, c], start=True, stop=True).then_inc(sum_done, 1)

            for p in range(GLA_PAIRS):
                for b in range(TB):
                    last = pe.transpose(ps_g[p][:, b * P:(b + 1) * P], k_dec[:, p, b * P:(b + 1) * P], keep["ident"][:])
                last.then_inc(t_done, 1)
            head_sums(0)
            head_sums(1)
            for h in range(GLA_HEADS):
                for b in range(TB):
                    last = pe.matmul(ps_o[h][:, b * P:(b + 1) * P], k_in[:, h, b * P:(b + 1) * P],
                                     q_in[:, h // 2, b * P:(b + 1) * P], start=True, stop=True)
                last.then_inc(s_done, 1)
            head_sums(2)
            head_sums(3)
            pe.wait_ge(ln_done, TB)
            pe.wait_ge(kt_done, 2 * GLA_PAIRS)
            pe.wait_ge(sc_done, 2 * GLA_HEADS)

            def update(c):
                if c >= 2:
                    pe.wait_ge(st_done, GLA_HEADS * (c - 1))
                for p in range(GLA_PAIRS):
                    pe.matmul(upd_bank(p, c)[:, 0:2 * P], kt[:, p, c], v8[:, 1, c // 2, p * 256:(p + 1) * 256],
                              start=True, stop=True).then_inc(u_done, 1)

            update(0)
            for c in range(NC):
                if c + 1 < NC - 1:
                    update(c + 1)
                if c % 2 == 0:
                    for h in range(GLA_HEADS):
                        pe.matmul(ps_o[h][:, c * C:(c + 2) * C], v8[:, 1, c // 2, h * P:(h + 1) * P], sc[:, h, c // 2],
                                  start=True, stop=False, skip_group_check=True)
                if c >= 1:
                    pe.wait_ge(st_done, GLA_HEADS * c)
                    for h in range(GLA_HEADS):
                        last = pe.matmul(ps_o[h][:, c * C:(c + 1) * C], st[:, h, c % 2], q_st[:, h // 2, c * C:(c + 1) * C],
                                         start=False, stop=(c % 2 == 1), skip_group_check=True)
                    last.then_inc(inter, 1)
            pe.wait_ge(inter, NC - 1)
            pe.nop().then_inc(o_done, 1)


def mixer_back(nc, io, keep, t16, v8, gx, catT, query):
    with ExitStack() as ctx:
        sb = lambda n, s, d=F32: ctx.enter_context(nc.sbuf_tensor(n, s, d))
        pb = lambda n, s: ctx.enter_context(nc.psum_tensor(n, s, F32))
        sem = lambda n: ctx.enter_context(nc.semaphore(n))
        xT, mod, gains = keep["xT"], keep["mod"], keep["gains"]
        h_hi, h_lo = keep["h_hi"], keep["h_lo"]
        WS = 3
        NG = KD - TB
        cat_hi, cat_lo = sb("cat_hi", [P, KD, T], F32R), sb("cat_lo", [P, KD, T], F32R)
        w_hi = [sb(f"w_out_hi{n}", [P, KD, P], F32R) for n in range(WS)]
        w_lo = [sb(f"w_out_lo{n}", [P, KD, P], F32R) for n in range(WS)]
        sq, rstd = v8[:, 0], v8[:, 1]
        halves = lambda tile: [tile[:, 2 * s:2 * s + 2].rearrange("p a (b c) -> p (a b) c", c=P) for s in range(2)]
        wq, wq_hi, wq_lo = halves(catT), halves(cat_hi), halves(cat_lo)
        scaled, full = rstd[:, 2:4], sq[:, 2:4]
        ps_s = [*(pb(f"ps_hs{n}", [P, T]) for n in range(2)), *query["ps"]]
        ps_p = [pb(f"ps_mix{n}", [P, T]) for n in range(3)]
        ps_x = pb("ps_sum_2", [P, T])
        sq_done, sum_done, ln_done, rstd_done = sem("hsq"), sem("hsum"), sem("hln"), sem("hrstd")
        normed, cat_done, chi, clo = sem("normed"), sem("cat_done"), sem("cat_hi_done"), sem("cat_lo_done")
        whi, wlo, mix_done, x_done = sem("w_out_hi_done"), sem("w_out_lo_done"), sem("mix_done"), sem("x1_done")
        sq2_done, sum2_done, ln2_done, rstd2_done = sem("sq2"), sem("sum2"), sem("ln2"), sem("rstd2")
        sc_done, f_done, hi_done, lo_done = sem("scaled2"), sem("full2"), sem("hi_done"), sem("lo_done")
        total = gx[:, 0]
        wq_in, added = sem("wq_first_in"), sem("squares_added")
        block = ctx.enter_context(nc.Block())

        @block.sync
        def _(sp):
            sp.wait_ge(clo, KD)
            for s in range(2):
                sp.dma_start(wq[s], io["w_q"][s]).then_inc(wq_in, 16)

        @block.scalar
        def _(act):
            def w_high(n):
                if n == 0:
                    act.wait_ge(keep["w_out_in"], 16)
                if n >= WS:
                    act.wait_ge(mix_done, n - WS + 1)
                    act.wait_ge(wlo, n - WS + 1)
                act.copy(w_hi[n % WS][:], keep["w_out"][:, n]).then_inc(whi, 1)

            for c in range(NG):
                act.activation(sq[:, c], catT[:, TB + c], ACT.Square).then_inc(sq_done, 1)
                if c == 1:
                    w_high(0)
                    act.copy(cat_hi[:, 0:2], catT[:, 0:2]).then_inc(chi, 2)
            for c in range(NG):
                act.wait_ge(sum_done, c + 1)
                act.activation(rstd[:, c], ps_s[c][:], ACT.Ln, bias=keep["eps"][:], scale=1.0 / GLA_DV).then_inc(ln_done, 1)
                act.wait_ge(ln_done, c + 1)
                act.activation(rstd[:, c], rstd[:, c], ACT.Exp, scale=-0.5).then_inc(rstd_done, 1)
                if c == 0:
                    act.copy(cat_hi[:, 2:4], catT[:, 2:4]).then_inc(chi, 2)
                    w_high(1)
            for c in range(NG):
                act.wait_ge(cat_done, c + 1)
                act.copy(cat_hi[:, TB + c], catT[:, TB + c]).then_inc(chi, 1)
            for n in range(KD):
                if n + 2 < KD:
                    w_high(n + 2)
                act.wait_ge(x_done, n + 1)
                if n >= 2:
                    act.wait_ge(added, n - 1)
                else:
                    act.wait_ge(sum_done, NG)
                act.activation(sq[:, n % 2], xT[:, n], ACT.Square).then_inc(sq2_done, 1)
            act.wait_ge(wq_in, 32)
            act.wait_ge(mix_done, KD)
            act.copy(wq_hi[0], wq[0]).then_inc(query["hi"], 1)
            act.wait_ge(sum2_done, 1)
            act.activation(rstd[:, 0], ps_x[:], ACT.Ln, bias=keep["eps"][:], scale=1.0 / D).then_inc(ln2_done, 1)
            act.wait_ge(ln2_done, 1)
            act.activation(rstd[:, 0], rstd[:, 0], ACT.Exp, scale=-0.5).then_inc(rstd2_done, 1)
            act.copy(wq_hi[1], wq[1]).then_inc(query["hi"], 1)
            for k in range(KD):
                shift = mod[:, 3 * KD + k:3 * KD + k + 1]
                act.wait_ge(sc_done, k + 1)
                act.activation(h_hi[:, k], scaled[:, k % 2], ACT.Identity, bias=shift).then_inc(hi_done, 1)
                if k >= 2:
                    act.wait_ge(lo_done, k - 1)
                act.activation(full[:, k % 2], scaled[:, k % 2], ACT.Identity, bias=shift).then_inc(f_done, 1)

        @block.gpsimd
        def _(pool):
            for n in range(KD):
                pool.wait_ge(whi, n + 1)
                if n >= WS:
                    pool.wait_ge(mix_done, n - WS + 1)
                pool.tensor_tensor(w_lo[n % WS][:], keep["w_out"][:, n], w_hi[n % WS][:].bitcast(F32), ALU.subtract).then_inc(wlo, 1)
            for s in range(2):
                pool.wait_ge(query["hi"], s + 1)
                pool.tensor_tensor(wq_lo[s], wq[s], wq_hi[s].bitcast(F32), ALU.subtract).then_inc(query["lo"], 1)

        @block.tensor
        def _(pe):
            for c in range(NG):
                pe.wait_ge(sq_done, c + 1)
                pe.matmul(ps_s[c][:], keep["ones"][:], sq[:, c], start=True, stop=True).then_inc(sum_done, 1)
            spans = [(0, 0, TB), (1, 0, TB), (0, TB, KD), (1, TB, KD), *((n, 0, KD) for n in range(2, KD))]
            for n, k0, k1 in spans:
                pe.wait_ge(wlo, n + 1)
                if n >= 3:
                    pe.wait_ge(x_done, n - 2)
                for k in range(k0, k1):
                    if n == 0:
                        pe.wait_ge(clo, k + 1)
                    hi, lo = w_hi[n % WS][:, k], w_lo[n % WS][:, k]
                    pe.matmul(ps_p[n % 3][:], hi, cat_hi[:, k], start=(k == 0), stop=False)
                    pe.matmul(ps_p[n % 3][:], hi, cat_lo[:, k], start=False, stop=False)
                    last = pe.matmul(ps_p[n % 3][:], lo, cat_hi[:, k], start=False, stop=(k == KD - 1))
                if k1 == KD:
                    last.then_inc(mix_done, 1)
            pe.wait_ge(added, KD - 1)
            pe.matmul(ps_x[:], keep["ones"][:], total, start=True, stop=False)
            pe.wait_ge(sq2_done, KD)
            pe.matmul(ps_x[:], keep["ones"][:], sq[:, (KD - 1) % 2], start=False, stop=True).then_inc(sum2_done, 1)
            pe.wait_ge(query["lo"], 2)
            for k in range(KD):
                pe.wait_ge(lo_done, k + 1)
                for s in range(2):
                    bank = query["ps"][s]
                    pe.matmul(bank[:], wq_hi[s][:, k], h_hi[:, k], start=(k == 0), stop=False)
                    pe.matmul(bank[:], wq_hi[s][:, k], h_lo[:, k], start=False, stop=False)
                    last = pe.matmul(bank[:], wq_lo[s][:, k], h_hi[:, k], start=False, stop=(k == KD - 1))
                    if k == KD - 1:
                        last.then_inc(query["done"], 1)

        @block.vector
        def _(dve):
            def cat_low(c0, c1):
                dve.wait_ge(chi, c1)
                dve.tensor_tensor(cat_lo[:, c0:c1], catT[:, c0:c1], cat_hi[:, c0:c1].bitcast(F32), ALU.subtract).then_inc(clo, c1 - c0)

            cat_low(0, 2)
            cat_low(2, 4)
            for c in range(NG):
                dve.wait_ge(rstd_done, c + 1)
                at = TB + c
                dve.scalar_tensor_tensor(catT[:, at], catT[:, at], gains[:, at:at + 1], rstd[:, c], ALU.mult, ALU.mult).then_inc(normed, 1)
                dve.wait_ge(normed, c + 1)
                dve.tensor_tensor(catT[:, at], catT[:, at], t16[:, GLR + c], ALU.mult).then_inc(cat_done, 1)
                if c >= 1:
                    cat_low(at - 1, at)
            cat_low(KD - 1, KD)
            for n in range(KD):
                dve.wait_ge(mix_done, n + 1)
                dve.scalar_tensor_tensor(xT[:, n], ps_p[n % 3][:], mod[:, 2 * KD + n:2 * KD + n + 1], xT[:, n],
                                         ALU.mult, ALU.add).then_inc(x_done, 1)
                if n == KD - 1:
                    break
                dve.wait_ge(sq2_done, n + 1)
                if n == 0:
                    dve.tensor_copy(total, sq[:, 0]).then_inc(added, 1)
                else:
                    dve.wait_ge(added, n)
                    dve.tensor_tensor(total, total, sq[:, n % 2], ALU.add).then_inc(added, 1)
            dve.wait_ge(rstd2_done, 1)
            dve.wait_ge(x_done, KD)
            for k in range(KD):
                if k >= 2:
                    dve.wait_ge(f_done, k - 1)
                dve.scalar_tensor_tensor(scaled[:, k % 2], xT[:, k], mod[:, 4 * KD + k:4 * KD + k + 1], rstd[:, 0],
                                         ALU.mult, ALU.mult).then_inc(sc_done, 1)
                if k >= 1:
                    dve.wait_ge(f_done, k)
                    dve.tensor_tensor(h_lo[:, k - 1], full[:, (k - 1) % 2], h_hi[:, k - 1].bitcast(F32), ALU.subtract).then_inc(lo_done, 1)
            dve.wait_ge(f_done, KD)
            dve.tensor_tensor(h_lo[:, KD - 1], full[:, (KD - 1) % 2], h_hi[:, KD - 1].bitcast(F32), ALU.subtract).then_inc(lo_done, 1)


class BlockProducts:

    def __init__(self, nc, ctx, io, keep, slots):
        sb = lambda n, s, d=F32: ctx.enter_context(nc.sbuf_tensor(f"{n}_early", s, d))
        sem = lambda n: ctx.enter_context(nc.semaphore(f"{n}_early"))
        self.io, self.keep, self.slots = io, keep, slots
        span = range(slots)
        self.raw = [sb(f"u_raw{n}", [P, KD, P]) for n in span]
        self.hi = [sb(f"u_hi{n}", [P, KD, P], F32R) for n in span]
        self.lo = [sb(f"u_lo{n}", [P, KD, P], F32R) for n in span]
        self.act = [sb(f"u_act{n}", [P, T]) for n in span]
        self.ps = [ctx.enter_context(nc.psum_tensor(f"ps_u{n}_early", [P, T], F32)) for n in span]
        self.u_in, self.stored = [sem(f"u_in{n}") for n in span], [sem(f"act_stored{n}") for n in span]
        self.hi_done, self.lo_done, self.mul, self.act_done = sem("u_hi_done"), sem("u_lo_done"), sem("u_mul"), sem("u_act_done")

    def load(self, sp, i, n):
        wait_count(sp, self.lo_done, (i - 1) * self.slots + n + 1)
        sp.dma_start(self.raw[n][:], self.io["u"][ds(i * self.slots + n, 1)].rearrange("o p k e -> (o p) k e"))\
          .then_inc(self.u_in[n], 16)

    def high(self, act, i, n):
        act.wait_ge(self.u_in[n], i * 16 + 16)
        wait_count(act, self.mul, (i - 1) * self.slots + n + 1)
        wait_count(act, self.lo_done, (i - 1) * self.slots + n + 1)
        act.copy(self.hi[n][:], self.raw[n][:]).then_inc(self.hi_done, 1)

    def low(self, eng, i, n):
        eng.wait_ge(self.hi_done, i * self.slots + n + 1)
        wait_count(eng, self.mul, (i - 1) * self.slots + n + 1)
        eng.tensor_tensor(self.lo[n][:], self.raw[n][:], self.hi[n][:].bitcast(F32), ALU.subtract).then_inc(self.lo_done, 1)

    def product(self, pe, i, n):
        h_hi, h_lo = self.keep["h_hi"], self.keep["h_lo"]
        pe.wait_ge(self.lo_done, i * self.slots + n + 1)
        wait_count(pe, self.act_done, (i - 1) * self.slots + n + 1)
        for k in range(KD):
            pe.matmul(self.ps[n][:], self.hi[n][:, k], h_hi[:, k], start=(k == 0), stop=False)
            pe.matmul(self.ps[n][:], self.hi[n][:, k], h_lo[:, k], start=False, stop=False)
            last = pe.matmul(self.ps[n][:], self.lo[n][:, k], h_hi[:, k], start=False, stop=(k == KD - 1))
        last.then_inc(self.mul, 1)

    def gelu(self, act, i, n):
        act.wait_ge(self.mul, i * self.slots + n + 1)
        wait_count(act, self.stored[n], i * 16)
        act.activation(self.act[n][:], self.ps[n][:], ACT.Gelu).then_inc(self.act_done, 1)

    def store(self, sp, i, n, acts):
        sp.wait_ge(self.act_done, i * self.slots + n + 1)
        sp.dma_start(acts[ds(i * self.slots + n, 1)].rearrange("o p t -> (o p) t"), self.act[n][:]).then_inc(self.stored[n], 16)


def retrieval(nc, io, keep, picks, acts, fill, query):
    with ExitStack() as ctx:
        sb = lambda n, s, d=F32: ctx.enter_context(nc.sbuf_tensor(n, s, d))
        pb = lambda n, s: ctx.enter_context(nc.psum_tensor(n, s, F32))
        sem = lambda n: ctx.enter_context(nc.semaphore(n))
        h_hi, h_lo = keep["h_hi"], keep["h_lo"]
        expert, gate = picks
        w = [sb(f"w_query{s}", [P, KD, P]) for s in range(2)]
        w_hi = [sb(f"w_query_hi{s}", [P, KD, P], F32R) for s in range(2)]
        w_lo = [sb(f"w_query_lo{s}", [P, KD, P], F32R) for s in range(2)]
        keys = [sb(f"keys{s}", [P, N_KEYS]) for s in range(2)]
        q = [sb(f"query{s}", [P, T]) for s in range(2)]
        iota50 = sb("iota_pairs", [P, N_PAIRS])
        turn_mark = sb("turn_mark", [P, 1])
        scores = sb("scores", [P, 2, TB, N_KEYS])
        rest = sb("rest", [P, 2, TB, N_KEYS])
        top = sb("top_keys", [P, 2, TB, TOPK])
        idx = sb("top_idx", [P, 2, TB, TOPK], U32)
        num = sb("top_num", [P, 2, TB, TOPK])
        cand = sb("cand", [P, TB, N_PAIRS])
        cnum = sb("cand_num", [P, TB, N_PAIRS])
        crest = sb("cand_rest", [P, TB, N_PAIRS])
        ctop = sb("cand_top", [P, TB, TOPK])
        cpos = sb("cand_pos", [P, TB, TOPK], U32)
        cposf = sb("cand_posf", [P, TB, TOPK])
        hit = sb("hit", [P, TB, TOPK, N_PAIRS])
        ex = sb("gate_exp", [P, TB, TOPK])
        tot = sb("gate_sum", [P, TB, 1])
        picked = sb("picked", [P, TB, TOPK])
        ps_q = query["ps"]
        ps_s = [pb(f"ps_s{s}", [P, T]) for s in range(2)]
        iota_done = sem("iota50_done")
        w_in, k_in = [sem(f"wq_in{s}") for s in range(2)], [sem(f"keys_in{s}") for s in range(2)]
        wq_hi, wq_lo, q_done = query["hi"], query["lo"], query["done"]
        q_kept, s_done = sem("q_kept"), sem("s_done")
        s_copied, s_used, s_read = sem("s_copied"), sem("s_used"), sem("s_read")
        chain, gate_chain, e_in, e_done = sem("topk_chain"), sem("gate_chain"), sem("exp_in"), sem("exp_done")
        block = ctx.enter_context(nc.Block())
        LAST = PEER_HEADS - 1
        first = lambda h: isinstance(h, int) and h == 0

        @block.sync
        def _(sp):
            def loads(h):
                for s in range(0 if first(h) else 2):
                    sp.wait_ge(wq_lo, h * 2 + s - 1)
                    sp.dma_start(w[s][:], io["w_q"][ds(h * 2 + s, 1)].rearrange("o p k c -> (o p) k c")).then_inc(w_in[s], 16)
                for s in range(2):
                    wait_count(sp, s_done, h)
                    sp.dma_start(keys[s][:], io[("keys_a", "keys_b")[s]][ds(h, 1)].rearrange("o p k -> (o p) k")).then_inc(k_in[s], 16)
                for n in range(FILL):
                    fill.load(sp, h, n)

            def stores(h):
                for n in range(FILL):
                    fill.store(sp, h, n, acts)

            loads(0)
            with sp.Fori(1, PEER_HEADS) as h:
                loads(h)
                stores(h - 1)
            for n in range(FILL):
                fill.load(sp, PEER_HEADS, n)
            stores(LAST)

        @block.gpsimd
        def _(pool):
            pool.iota(iota50[:], pattern=[[1, N_PAIRS]], base=0, channel_multiplier=0,
                      allow_small_or_imprecise_dtypes=True).then_inc(iota_done, 1)

            def turn(h):
                for s in range(0 if first(h) else 2):
                    pool.wait_ge(wq_hi, h * 2 + s + 1)
                    wait_count(pool, q_done, h * 2 + s - 1)
                    pool.tensor_tensor(w_lo[s][:], w[s][:], w_hi[s][:].bitcast(F32), ALU.subtract).then_inc(wq_lo, 1)
                for n in range(FILL):
                    fill.low(pool, h, n)

            turns(pool, PEER_HEADS, turn)
            for n in range(FILL):
                fill.low(pool, PEER_HEADS, n)

        @block.tensor
        def _(pe):
            def turn(h):
                for s in range(0 if first(h) else 2):
                    pe.wait_ge(wq_lo, h * 2 + s + 1)
                    wait_count(pe, q_kept, h * 2)
                    for k in range(KD):
                        pe.matmul(ps_q[s][:], w_hi[s][:, k], h_hi[:, k], start=(k == 0), stop=False)
                        pe.matmul(ps_q[s][:], w_hi[s][:, k], h_lo[:, k], start=False, stop=False)
                        last = pe.matmul(ps_q[s][:], w_lo[s][:, k], h_hi[:, k], start=False, stop=(k == KD - 1))
                    last.then_inc(q_done, 1)
                wait_count(pe, s_used, h)
                pe.wait_ge(q_kept, h * 2 + 2)
                for s in range(2):
                    pe.wait_ge(k_in[s], h * 16 + 16)
                    for b in range(TB):
                        last = pe.matmul(ps_s[s][:, b * P:(b + 1) * P], q[s][:, b * P:(b + 1) * P], keys[s][:], start=True, stop=True)
                last.then_inc(s_done, 1)
                for n in range(FILL):
                    fill.product(pe, h, n)

            turns(pe, PEER_HEADS, turn)
            for n in range(EARLY_BLOCKS):
                fill.product(pe, PEER_HEADS, n)

        @block.scalar
        def _(act):
            def soft(h):
                act.wait_ge(e_in, h + 1)
                act.activation(ex[:], ex[:], ACT.Exp).then_inc(e_done, 1)

            def high(h, s):
                act.wait_ge(w_in[s], h * 16)
                wait_count(act, q_done, h * 2 + s - 1)
                wait_count(act, wq_lo, h * 2 + s - 1)
                act.copy(w_hi[s][:], w[s][:]).then_inc(wq_hi, 1)

            def turn(h, last=False):
                for s in range(2):
                    act.wait_ge(q_done, h * 2 + s + 1)
                    wait_count(act, s_done, h)
                    act.copy(q[s][:], ps_q[s][:]).then_inc(q_kept, 1)
                for s in range(0 if first(h) or last else 2):
                    high(h + 1, s)
                act.wait_ge(s_done, h + 1)
                wait_count(act, s_read, h)
                for s in range(2):
                    act.copy(scores[:, s], ps_s[s][:].rearrange("p (b k) -> p b k", b=TB)).then_inc(s_copied, 1)
                act.wait_ge(s_copied, h * 2 + 2)
                act.sem_inc(s_used, 1)
                if first(h):
                    for n in range(FILL):
                        fill.high(act, 0, n)
                    for s in range(2):
                        high(1, s)
                else:
                    soft(h - 1)
                for n in range(FILL):
                    fill.gelu(act, h, n)
                    fill.high(act, h + 1, n)

            turn(0)
            with act.Fori(1, LAST) as h:
                turn(h)
            turn(LAST, last=True)
            soft(LAST)

        @block.vector
        def _(dve):
            dve.wait_ge(iota_done, 1)

            def turn(h):
                steps = [0]

                def stage(instructions):
                    for ins in instructions:
                        ins.then_inc(chain, 1)
                        steps[0] += 1
                    dve.wait_ge(chain, steps[0])

                both = [(s, b) for s in range(2) for b in range(TB)]
                dve.wait_ge(s_used, h + 1)
                dve.memset(turn_mark[:], 0.0)
                dve.sem_clear(chain)
                stage(dve.max(top[:, s, b, 0:8], scores[:, s, b]) for s, b in both)
                stage([f for s, b in both for f in (
                    dve.match_replace(rest[:, s, b], top[:, s, b, 0:8], scores[:, s, b], NEG),
                    dve.max_index(idx[:, s, b, 0:8], top[:, s, b, 0:8], scores[:, s, b]))])
                dve.sem_inc(s_read, 1)
                stage(dve.max(top[:, s, b, 8:16], rest[:, s, b]) for s, b in both)
                stage(dve.max_index(idx[:, s, b, 8:16], top[:, s, b, 8:16], rest[:, s, b]) for s, b in both)

                def pair_sums(out, of):
                    for a in range(8):
                        n = PAIR_ROWS[a][1]
                        yield dve.tensor_tensor(out[:, :, PAIR_START[a]:PAIR_START[a] + n],
                                                of[:, 0, :, a:a + 1].broadcast_to([P, TB, n]), of[:, 1, :, 0:n], ALU.add)
                    yield dve.tensor_tensor(out[:, :, PAIR_START[8]:N_PAIRS], of[:, 0, :, 8:16],
                                            of[:, 1, :, 0:1].broadcast_to([P, TB, 8]), ALU.add)

                stage([*pair_sums(cand, top), dve.tensor_copy(num[:, 1], idx[:, 1]),
                       dve.tensor_scalar(num[:, 0], idx[:, 0], float(N_KEYS), None, ALU.mult)])
                stage([*(dve.max(ctop[:, b, 0:8], cand[:, b]) for b in range(TB)), *pair_sums(cnum, num)])
                stage([f for b in range(TB) for f in (
                    dve.match_replace(crest[:, b], ctop[:, b, 0:8], cand[:, b], NEG),
                    dve.max_index(cpos[:, b, 0:8], ctop[:, b, 0:8], cand[:, b]))])
                stage(dve.max(ctop[:, b, 8:16], crest[:, b]) for b in range(TB))
                if not (isinstance(h, int) and h == 0):
                    gates_of_last(h)
                stage(f for b in range(-1, TB) for f in (
                    [dve.tensor_tensor(ex[:], ctop[:], ctop[:, :, 0:1].broadcast_to([P, TB, TOPK]), ALU.subtract)] if b < 0 else
                    [dve.max_index(cpos[:, b, 8:16], ctop[:, b, 8:16], crest[:, b])]))
                dve.sem_inc(e_in, 1)
                stage([dve.tensor_copy(cposf[:], cpos[:])])
                stage(dve.tensor_tensor(hit[:, b], cposf[:, b].rearrange("p (k o) -> p k o", o=1).broadcast_to([P, TOPK, N_PAIRS]),
                                        iota50[:].rearrange("p (o n) -> p o n", o=1).broadcast_to([P, TOPK, N_PAIRS]), ALU.is_equal)
                      for b in range(TB))
                stage(dve.tensor_tensor(hit[:, b], hit[:, b], cnum[:, b].rearrange("p (o n) -> p o n", o=1).broadcast_to([P, TOPK, N_PAIRS]), ALU.mult)
                      for b in range(TB))
                stage([dve.tensor_reduce(picked[:], hit[:], AX.X, ALU.add)])
                stage([dve.tensor_copy(expert[:, :, ds(h * TOPK, TOPK)], picked[:])])

            def gates_of_last(h):
                dve.wait_ge(e_done, h)
                dve.tensor_reduce(tot[:], ex[:], AX.X, ALU.add).then_inc(gate_chain, 1)
                dve.wait_ge(gate_chain, h * 3 - 2)
                dve.reciprocal(tot[:], tot[:]).then_inc(gate_chain, 1)
                dve.wait_ge(gate_chain, h * 3 - 1)
                dve.tensor_tensor(gate[:, :, ds((h - 1) * TOPK, TOPK)], ex[:], tot[:].broadcast_to([P, TB, TOPK]), ALU.mult)\
                   .then_inc(gate_chain, 1)
                dve.wait_ge(gate_chain, h * 3)

            turns(dve, PEER_HEADS, turn)
            gates_of_last(PEER_HEADS)


def dense_gates(nc, keep, picks, g_dram, acts, fill):
    with ExitStack() as ctx:
        sb = lambda n, s, d=F32: ctx.enter_context(nc.sbuf_tensor(n, s, d))
        pb = lambda n, s: ctx.enter_context(nc.psum_tensor(n, s, F32))
        sem = lambda n: ctx.enter_context(nc.semaphore(n))
        expert, gate = picks
        whole = sb("whole", [P, TB, P], I32)
        part = sb("part", [P, 2, TB, P], I32)
        ij = sb("ij", [P, 2, TB, P])
        cols = sb("pick_cols", [P, 3, T])
        BATCH, PB, PER = 8, 4, 4
        HB = 2
        hot_i = [sb(f"hot_i{n}", [P, BATCH, P]) for n in range(HB)]
        hot_j = [sb(f"hot_j{n}", [P, BATCH, P]) for n in range(HB)]
        tile = [sb(f"g_tile{n}", [P, P, G_TOK]) for n in range(2)]
        ps_g = [pb(f"ps_g{n}", [P, PER, P]) for n in range(PB)]
        chain, t_done, c_done = sem("pick_chain"), sem("pick_t"), sem("pick_cols_done")
        hot, g_done, g_kept = sem("hot"), sem("g_done"), sem("g_kept")
        stored = [sem(f"g_stored{n}") for n in range(2)]
        block = ctx.enter_context(nc.Block())
        FILLS = G_TOK // PER
        BATCHES = G_TOK // BATCH
        FPB = BATCH // PER
        cols_of = [ps_g[n][:].rearrange("p t i -> p (t i)") for n in range(3)]
        TURNS = G_TILES // 2
        early = lambda r: PEER_HEADS + r

        REGULAR = [3, 7, 11, 15]
        START, END = [-1, -1, -1, 9], [3, 9, 15, 15]

        def all_turns(eng, body):
            body(0, after=START)
            with eng.Fori(1, TURNS - 1) as r:
                body(r, after=REGULAR)
            body(TURNS - 1, last=True, after=END)

        @block.gpsimd
        def _(pool):
            def turn(r, after, last=False):
                for n in range(0 if last else FILL):
                    fill.low(pool, early(r + 1), n)

            all_turns(pool, turn)

        @block.vector
        def _(dve):
            done = [0]

            def link(ins):
                done[0] += 1
                ins.then_inc(chain, 1)
                dve.wait_ge(chain, done[0])

            link(dve.tensor_copy(whole[:], expert[:]))
            link(dve.tensor_scalar(part[:, 0], whole[:], 7, None, ALU.logical_shift_right))
            link(dve.tensor_scalar(part[:, 1], whole[:], N_KEYS - 1, None, ALU.bitwise_and))
            link(dve.tensor_copy(ij[:], part[:]))
            dve.wait_ge(t_done, 1)
            for n in range(3):
                dve.tensor_copy(cols[:, n], cols_of[n]).then_inc(c_done, 1)
            dve.wait_ge(c_done, 3)

            def turn(r):
                for x in range(2 * BATCHES):
                    n = x % HB
                    t0 = (r * 2 * BATCHES + x) * BATCH
                    wait_count(dve, g_done, (r * 2 * BATCHES + x - HB + 1) * FPB)
                    dve.tensor_tensor(hot_j[n][:], keep["iota"][:].rearrange("p (o j) -> p o j", o=1).broadcast_to([P, BATCH, P]),
                                      cols[:, 1, ds(t0, BATCH)].rearrange("p (t o) -> p t o", o=1).broadcast_to([P, BATCH, P]),
                                      ALU.is_equal).then_inc(hot, 1)
                    for o in range(BATCH):
                        dve.tensor_scalar(hot_i[n][:, o], keep["iota"][:], cols[:, 0, ds(t0 + o, 1)], cols[:, 2, ds(t0 + o, 1)],
                                          ALU.is_equal, ALU.mult).then_inc(hot, 1)

            turns(dve, TURNS, turn)

        @block.tensor
        def _(pe):
            for n in range(EARLY_BLOCKS, START.count(-1)):
                fill.product(pe, early(0), n)
            pe.wait_ge(chain, 4)
            for n in range(3):
                for b in range(TB):
                    src = gate[:, b] if n == 2 else ij[:, n, b]
                    last = pe.transpose(cols_of[n][:, b * P:(b + 1) * P], src, keep["ident"][:])
            last.then_inc(t_done, 1)
            pe.wait_ge(c_done, 3)

            def turn(r, after, last=False):
                for f in range(2 * FILLS):
                    at = r * 2 * FILLS + f
                    x, m = f // FPB, f % PB
                    wait_count(pe, g_kept, at - PB + 1)
                    for o in range(PER):
                        slot = (f % FPB) * PER + o
                        pe.wait_ge(hot, (r * 2 * BATCHES + x) * (BATCH + 1) + slot + 2)
                        last = pe.matmul(ps_g[m][:, o], hot_j[x % HB][:, slot], hot_i[x % HB][:, slot], start=True, stop=True)
                    last.then_inc(g_done, 1)
                    for n in range(FILL):
                        if after[n] == f:
                            fill.product(pe, early(r), n)

            all_turns(pe, turn)

        @block.scalar
        def _(act):
            def block_done(r, n, last):
                fill.gelu(act, early(r), n)
                if not last:
                    fill.high(act, early(r + 1), n)

            def turn(r, after, last=False):
                for f in range(2 * FILLS):
                    n, m = f // FILLS, f % PB
                    if f % FILLS == 0:
                        wait_count(act, stored[n], r * 16)
                    act.wait_ge(g_done, r * 2 * FILLS + f + 1)
                    act.copy(tile[n][:, :, (f % FILLS) * PER:(f % FILLS + 1) * PER], ps_g[m][:].rearrange("p t i -> p i t")).then_inc(g_kept, 1)
                    for j in range(FILL):
                        if after[j] + 2 == f:
                            block_done(r, j, last)
                for j in range(FILL):
                    if after[j] + 2 >= 2 * FILLS:
                        block_done(r, j, last)

            all_turns(act, turn)

        @block.sync
        def _(sp):
            def turn(r, after, last=False):
                for n in range(0 if last else FILL):
                    fill.load(sp, early(r + 1), n)
                for n in range(2):
                    sp.wait_ge(g_kept, (r * 2 + n + 1) * FILLS)
                    sp.dma_start(g_dram[ds(r * 2 + n, 1)].rearrange("o p i t -> (o p) (i t)"),
                                 tile[n][:].rearrange("p i t -> p (i t)")).then_inc(stored[n], 16)
                    for m in range(n * FILL // 2, (n + 1) * FILL // 2):
                        fill.store(sp, early(r), m, acts)

            all_turns(sp, turn)
            for n in range(2):
                sp.wait_ge(stored[n], TURNS * 16)
            for n in range(FILL):
                sp.wait_ge(fill.stored[n], early(TURNS) * 16)


def experts(nc, io, keep, g_dram, acts, yT, sq, x_done, sq_done):
    with ExitStack() as ctx:
        sb = lambda n, s, d=F32: ctx.enter_context(nc.sbuf_tensor(n, s, d))
        pb = lambda n, s: ctx.enter_context(nc.psum_tensor(n, s, F32))
        sem = lambda n: ctx.enter_context(nc.semaphore(n))
        h_hi, h_lo = keep["h_hi"], keep["h_lo"]
        HALF = GROUP // 2
        UR, US, VR, VS = 2, 2, 4, 4
        HC = D // 2
        u_raw = [sb(f"u_raw{n}", [P, KD, P]) for n in range(UR)]
        u_hi = [sb(f"u_hi{n}", [P, KD, P], F32R) for n in range(US)]
        u_lo = [sb(f"u_lo{n}", [P, KD, P], F32R) for n in range(US)]
        v_raw = [sb(f"v_raw{n}", [P, HC]) for n in range(VR)]
        v_hi = [sb(f"v_hi{n}", [P, HC], F32R) for n in range(VS)]
        v_lo = [sb(f"v_lo{n}", [P, HC], F32R) for n in range(VS)]
        gates = [sb(f"gates{n}", [P, G_TILES, HALF, G_TOK]) for n in range(2)]
        wt = [sb(f"act{n}", [P, T]) for n in range(HALF)]
        w_hi = [sb(f"w_hi{n}", [P, T], F32R) for n in range(GROUP)]
        w_lo = [sb(f"w_lo{n}", [P, T], F32R) for n in range(GROUP)]
        ps_a = [pb(f"ps_a{n}", [P, T]) for n in range(HALF)]
        ps_y = [pb(f"ps_y{n}", [P, T]) for n in range(4)]
        u_in = [sem(f"u_in{n}") for n in range(UR)]
        v_in = [sem(f"v_in{n}") for n in range(VR)]
        a_in = [sem(f"a_in{n}") for n in range(HALF)]
        g_in = [sem(f"g_in{n}") for n in range(2)]
        uhi, ulo, vhi, vlo = sem("u_hi_done"), sem("u_lo_done"), sem("v_hi_done"), sem("v_lo_done")
        u_mul, v_mul, act_done, w_done, whi, wlo = sem("u_mul"), sem("v_mul"), sem("act_done"), sem("w_gated"), sem("w_hi_done"), sem("w_lo_done")
        y_kept = sem("y_kept")
        block = ctx.enter_context(nc.Block())
        READY = FILLED // GROUP
        LOADED, MADE = "loaded", "made"
        u_at = lambda g, n: (g - READY) * GROUP + n
        v_at = lambda g, half, n: g * 2 * GROUP + half * GROUP + n

        def y_banks(half, after):
            return ps_a if half == 1 and after is LOADED else ps_y

        def group_loop(eng, body):
            body(0, LOADED, LOADED)
            with eng.Fori(1, READY - 1) as g:
                body(g, LOADED, LOADED)
            body(READY - 1, LOADED, MADE)
            body(READY, MADE, MADE)
            with eng.Fori(READY + 1, N_GROUPS - 1) as g:
                body(g, MADE, MADE)
            body(N_GROUPS - 1, MADE, None)

        def order(lift_u, lift_v, first_step, second_step, add_y, half_done, loop):
            lift_v(0, 0, 0)
            first_step(0, 0, LOADED)
            second_step(0, 0)
            for n in range(1, GROUP - 1):
                if n <= 2:
                    lift_v(0, 0, n)
                first_step(0, n, LOADED)
                if n >= 2:
                    second_step(0, n - 1)

            def body(g, mine, after):
                lifted = mine is LOADED
                if not lifted:
                    lift_v(g, 0, 0)
                    lift_v(g, 0, 1)
                first_step(g, GROUP - 1, mine)
                second_step(g, GROUP - 2)
                if not lifted:
                    lift_v(g, 0, 2)
                second_step(g, GROUP - 1)
                for n in range(3, GROUP):
                    lift_v(g, 0, n)
                if after is None:
                    add_y(g, 0, after)
                    for n in range(GROUP):
                        lift_v(g, 1, n)
                        if n == HALF:
                            half_done()
                    add_y(g, 1, after)
                    return
                g1 = g + 1
                if after is MADE:
                    lift_u(g1, 0)
                    lift_u(g1, 1)
                    add_y(g, 0, after)
                    first_step(g1, 0, after)
                    lift_u(g1, 2)
                    first_step(g1, 1, after)
                    lift_u(g1, 3)
                    first_step(g1, 2, after)
                    lift_v(g, 1, 0)
                    lift_v(g, 1, 1)
                    first_step(g1, 3, after)
                    lift_v(g, 1, 2)
                else:
                    lift_v(g, 1, 0)
                    lift_v(g, 1, 1)
                    lift_v(g, 1, 2)
                    add_y(g, 0, after)
                    for n in range(HALF):
                        first_step(g1, n, after)
                for n in range(3, GROUP):
                    lift_v(g, 1, n)
                    if n <= 6:
                        second_step(g1, n - 3)
                if after is LOADED:
                    lift_v(g1, 0, 0)
                    first_step(g1, 4, after)
                    lift_v(g1, 0, 1)
                    first_step(g1, 5, after)
                    second_step(g1, 4)
                    lift_v(g1, 0, 2)
                    add_y(g, 1, after)
                    first_step(g1, 6, after)
                    second_step(g1, 5)
                    return
                lift_u(g1, 4)
                lift_u(g1, 5)
                add_y(g, 1, after)
                first_step(g1, 4, after)
                lift_u(g1, 6)
                first_step(g1, 5, after)
                second_step(g1, 4)
                lift_u(g1, 7)
                first_step(g1, 6, after)
                second_step(g1, 5)

            loop(body)

        @block.sync
        def _(sp):
            def load_u(g, n):
                wait_count(sp, ulo, u_at(g, n) - UR + 1)
                sp.dma_start(u_raw[n % UR][:], io["u"][ds(g * GROUP + n, 1)].rearrange("o p k e -> (o p) k e")).then_inc(u_in[n % UR], 16)

            def load_act(g, n):
                wait_count(sp, wlo, g * GROUP + n - HALF + 1)
                sp.dma_start(wt[n % HALF][:], acts[ds(g * GROUP + n, 1)].rearrange("o p t -> (o p) t")).then_inc(a_in[n % HALF], 16)

            def load_g(g, half):
                wait_count(sp, w_done, g * GROUP + half * HALF - HALF)
                src = g_dram[:].rearrange("a p (q i) t -> q p a i t", i=HALF)[ds(g * 2 + half, 1)]
                sp.dma_start(gates[half][:], src.rearrange("o p a i t -> (o p) a i t")).then_inc(g_in[half], 16)

            def load_v(g, half, n):
                wait_count(sp, vlo, v_at(g, half, n) - VR + 1)
                sp.dma_start(v_raw[n % VR][:], io["v"][ds(g * GROUP + n, 1)].rearrange("o p d -> (o p) d")[:, half * HC:(half + 1) * HC])\
                  .then_inc(v_in[n % VR], 16)

            load_v(0, 0, 0)
            load_g(0, 0)
            load_act(0, 0)
            load_v(0, 0, 1)
            for n in range(1, HALF):
                load_act(0, n)
            for n in range(2, VR):
                load_v(0, 0, n)
            load_g(0, 1)
            for n in range(HALF, GROUP):
                load_act(0, n)

            def group(g, mine, after):
                for half in range(2):
                    for n in range(GROUP):
                        if not (isinstance(g, int) and g == 0 and half == 0 and n < VR):
                            load_v(g, half, n)
                        if n == HALF - 1 and after:
                            load_g(g + 1, half)
                    if after:
                        for n in range(half * HALF, half * HALF + HALF):
                            (load_u if after is MADE else load_act)(g + 1, n)

            group_loop(sp, group)

        @block.scalar
        def _(act):
            def split_u(g, n):
                act.wait_ge(u_in[n % UR], ((g - READY) * (GROUP // UR) + n // UR + 1) * 16)
                wait_count(act, u_mul, u_at(g, n) - US + 1)
                wait_count(act, ulo, u_at(g, n) - US + 1)
                act.copy(u_hi[n % US][:], u_raw[n % UR][:]).then_inc(uhi, 1)

            def split_v(g, half, n):
                act.wait_ge(v_in[n % VR], (g * (2 * GROUP // VR) + half * (GROUP // VR) + n // VR + 1) * 16)
                wait_count(act, v_mul, v_at(g, half, n) - VS + 1)
                wait_count(act, vlo, v_at(g, half, n) - VS + 1)
                act.copy(v_hi[n % VS][:], v_raw[n % VR][:]).then_inc(vhi, 1)

            def gelu(g, n, how):
                if how is MADE:
                    act.wait_ge(u_mul, u_at(g, n) + 1)
                    act.wait_ge(wlo, g * GROUP + n - HALF + 1)
                    act.activation(wt[n % HALF][:], ps_a[n % HALF][:], ACT.Gelu).then_inc(act_done, 1)

            def w_high(g, n):
                act.wait_ge(w_done, g * GROUP + n + 1)
                if not (isinstance(g, int) and g == 0):
                    act.wait_ge(v_mul, v_at(g - 1, 1, n) + 1)
                act.copy(w_hi[n][:], wt[n % HALF][:]).then_inc(whi, 1)

            def squares():
                for k in range(HALF):
                    act.wait_ge(x_done, k + 1)
                    act.activation(sq[:, k], keep["xT"][:, k], ACT.Square).then_inc(sq_done, 1)

            order(split_u, split_v, gelu, w_high, lambda g, half, after: None, squares, lambda body: group_loop(act, body))

        @block.vector
        def _(dve):
            def split_u(g, n):
                dve.wait_ge(uhi, u_at(g, n) + 1)
                wait_count(dve, u_mul, u_at(g, n) - US + 1)
                dve.tensor_tensor(u_lo[n % US][:], u_raw[n % UR][:], u_hi[n % US][:].bitcast(F32), ALU.subtract).then_inc(ulo, 1)

            def split_v(g, half, n):
                dve.wait_ge(vhi, v_at(g, half, n) + 1)
                wait_count(dve, v_mul, v_at(g, half, n) - VS + 1)
                dve.tensor_tensor(v_lo[n % VS][:], v_raw[n % VR][:], v_hi[n % VS][:].bitcast(F32), ALU.subtract).then_inc(vlo, 1)

            def weigh(g, n, how):
                if how is MADE:
                    dve.wait_ge(act_done, u_at(g, n) + 1)
                else:
                    dve.wait_ge(a_in[n % HALF], (g * 2 + n // HALF + 1) * 16)
                dve.wait_ge(g_in[n // HALF], g * 16 + 16)
                w = wt[n % HALF][:].rearrange("p (a t) -> p a t", a=G_TILES)
                dve.tensor_tensor(w, w, gates[n // HALF][:, :, n % HALF], ALU.mult).then_inc(w_done, 1)

            def w_low(g, n):
                dve.wait_ge(whi, g * GROUP + n + 1)
                if not (isinstance(g, int) and g == 0):
                    dve.wait_ge(v_mul, v_at(g - 1, 1, n) + 1)
                dve.tensor_tensor(w_lo[n][:], wt[n % HALF][:], w_hi[n][:].bitcast(F32), ALU.subtract).then_inc(wlo, 1)

            def add_y(g, half, after):
                dve.wait_ge(v_mul, v_at(g, half, GROUP))
                first = isinstance(g, int) and g == 0
                if not first:
                    dve.wait_ge(y_kept, g * 8 + half * 4 - 4)
                for c in range(4):
                    y = yT[:, half * 4 + c]
                    ps = y_banks(half, after)[c][:]
                    if first:
                        dve.tensor_copy(y, ps).then_inc(y_kept, 1)
                    else:
                        dve.tensor_tensor(y, y, ps, ALU.add).then_inc(y_kept, 1)

            def residual():
                for k in range(HALF):
                    gate = keep["mod"][:, 5 * KD + k:5 * KD + k + 1]
                    dve.wait_ge(y_kept, (N_GROUPS - 1) * 8 + k + 1)
                    dve.scalar_tensor_tensor(keep["xT"][:, k], yT[:, k], gate, keep["xT"][:, k], ALU.mult, ALU.add).then_inc(x_done, 1)

            order(split_u, split_v, weigh, w_low, add_y, residual, lambda body: group_loop(dve, body))

        @block.tensor
        def _(pe):
            def u_products(g, n):
                pe.wait_ge(ulo, u_at(g, n) + 1)
                wait_count(pe, act_done, u_at(g, n) - HALF + 1)
                for k in range(KD):
                    hi, lo = u_hi[n % US][:, k], u_lo[n % US][:, k]
                    pe.matmul(ps_a[n % HALF][:], hi, h_hi[:, k], start=(k == 0), stop=False)
                    pe.matmul(ps_a[n % HALF][:], hi, h_lo[:, k], start=False, stop=False)
                    last = pe.matmul(ps_a[n % HALF][:], lo, h_hi[:, k], start=False, stop=(k == KD - 1))
                last.then_inc(u_mul, 1)

            def v_products(g, half, n, mine, after):
                pe.wait_ge(vlo, v_at(g, half, n) + 1)
                pe.wait_ge(wlo, g * GROUP + n + 1)
                if n == 0:
                    alone = after is LOADED or (half == 0 and mine is LOADED)
                    wait_count(pe, y_kept, g * 8 + half * 4 - (4 if alone else 0))
                ps_y_of = y_banks(half, after)
                for c in range(4):
                    hi, lo = v_hi[n % VS][:, c * P:(c + 1) * P], v_lo[n % VS][:, c * P:(c + 1) * P]
                    pe.matmul(ps_y_of[c][:], hi, w_hi[n][:], start=(n == 0), stop=False)
                    pe.matmul(ps_y_of[c][:], hi, w_lo[n][:], start=False, stop=False)
                    last = pe.matmul(ps_y_of[c][:], lo, w_hi[n][:], start=False, stop=(n == GROUP - 1))
                last.then_inc(v_mul, 1)

            def group(g, mine, after):
                for half in range(2):
                    for n in range(GROUP):
                        v_products(g, half, n, mine, after)
                    if after is MADE:
                        if half == 0 and mine is LOADED:
                            pe.wait_ge(y_kept, g * 8)
                        for n in range(half * HALF, half * HALF + HALF):
                            u_products(g + 1, n)

            group_loop(pe, group)


def finish(nc, io, keep, yT, sq, x_done, sq_done):
    with ExitStack() as ctx:
        sb = lambda n, s, d=F32: ctx.enter_context(nc.sbuf_tensor(n, s, d))
        sem = lambda n: ctx.enter_context(nc.semaphore(n))
        xT, mod = keep["xT"], keep["mod"]
        g_fin = sb("g_final", [P, KD])
        rstd = sb("rstd_y", [P, T])
        ps = ctx.enter_context(nc.psum_tensor("ps_sum_y", [P, T], F32))
        g_in, sum_done, ln_done, rstd_done, o_done, stored = (
            sem("gf_in"), sem("sum_y_done"), sem("ln_y_done"), sem("rstd_y_done"), sem("out_done"), sem("stored"))
        READY = KD // 2
        block = ctx.enter_context(nc.Block())

        @block.sync
        def _(sp):
            sp.dma_start(g_fin[:], io["g_final"]).then_inc(g_in, 16)
            for k in range(KD):
                sp.wait_ge(o_done, k + 1)
                sp.dma_start(io["out"][:, k], yT[:, k]).then_inc(stored, 16)
            sp.wait_ge(stored, 16 * KD)

        @block.vector
        def _(dve):
            for k in range(READY, KD):
                dve.scalar_tensor_tensor(xT[:, k], yT[:, k], mod[:, 5 * KD + k:5 * KD + k + 1], xT[:, k], ALU.mult, ALU.add)\
                   .then_inc(x_done, 1)
            dve.wait_ge(rstd_done, 1)
            dve.wait_ge(g_in, 16)
            dve.wait_ge(x_done, KD)
            for k in range(KD):
                dve.scalar_tensor_tensor(yT[:, k], xT[:, k], g_fin[:, k:k + 1], rstd[:], ALU.mult, ALU.mult).then_inc(o_done, 1)

        @block.scalar
        def _(act):
            act.preload_act_table_set("natural_log_exp_and_others")
            for k in range(READY, KD):
                act.wait_ge(x_done, k + 1)
                act.activation(sq[:, k], xT[:, k], ACT.Square).then_inc(sq_done, 1)
            act.wait_ge(sum_done, 1)
            act.activation(rstd[:], ps[:], ACT.Ln, bias=keep["eps"][:], scale=1.0 / D).then_inc(ln_done, 1)
            act.wait_ge(ln_done, 1)
            act.activation(rstd[:], rstd[:], ACT.Exp, scale=-0.5).then_inc(rstd_done, 1)

        @block.tensor
        def _(pe):
            for k in range(KD):
                pe.wait_ge(sq_done, k + 1)
                last = pe.matmul(ps[:], keep["ones"][:], sq[:, k], start=(k == 0), stop=(k == KD - 1))
            last.then_inc(sum_done, 1)


def program(nc, io):
    with ExitStack() as top:
        sb = lambda n, s, d=F32: top.enter_context(nc.sbuf_tensor(n, s, d))
        keep = {
            "xT": sb("xT", [P, KD, T]), "mod": sb("mod", [P, 6 * KD]), "gains": sb("gains", [P, KD]),
            "ones": sb("ones", [P, P]), "neg_ones": sb("neg_ones", [P, P]), "pair_ones": sb("pair_ones", [P, P]),
            "ident": sb("ident", [P, P]), "neg_tri": sb("neg_tri", [P, P]), "iota": sb("iota", [P, P]), "eps": sb("eps", [P, 1]),
        }
        g_dram = nc.dram_tensor("gate_tiles", [G_TILES, P, N_KEYS, G_TOK], F32, kind="Internal").ap()
        keep["w_out_in"] = top.enter_context(nc.semaphore("w_out_in"))
        with ExitStack() as mix:
            msb = lambda n, s: mix.enter_context(nc.sbuf_tensor(n, s, F32, side="right"))
            t16, v8, gx = msb("t16", [P, N_PROJ, T]), msb("v8", [P, 2, TB, T]), msb("gate_x", [P, GLA_PAIRS, T])
            with ExitStack() as front:
                for n in ("h_hi", "h_lo"):
                    keep[n] = front.enter_context(nc.sbuf_tensor(f"{n}_mixer", [P, KD, T], F32R))
                front_stage(nc, io, keep, t16, v8, gx)
            keep["w_out"] = sb("w_out_raw", [P, KD, KD, P])
            catT = msb("catT", [P, KD, T])
            with ExitStack() as linear:
                operands = LinearOperands(nc, linear, t16, gx)
                stick_breaking(nc, io, keep, t16, v8, catT, operands)
                gated_linear(nc, keep, v8, catT, operands)
            for n in ("h_hi", "h_lo"):
                keep[n] = sb(n, [P, KD, T], F32R)
            query_banks = top.enter_context(ExitStack())
            query = {
                "ps": [query_banks.enter_context(nc.psum_tensor(f"ps_q{s}", [P, T], F32, side="right")) for s in range(2)],
                **{n: top.enter_context(nc.semaphore(f"query_{n}")) for n in ("hi", "lo", "done")},
            }
            mixer_back(nc, io, keep, t16, v8, gx, catT, query)
        with ExitStack() as front:
            fsb = lambda n, s, d=F32: front.enter_context(nc.sbuf_tensor(n, s, d))
            picks = (fsb("expert", [P, TB, P]), fsb("gate", [P, TB, P]))
            acts = nc.dram_tensor("activations", [FILLED, P, T], F32, kind="Internal").ap()
            fill = BlockProducts(nc, front, io, keep, FILL)
            retrieval(nc, io, keep, picks, acts, fill, query)
            query_banks.close()
            dense_gates(nc, keep, picks, g_dram, acts, fill)
        with ExitStack() as back:
            yT = back.enter_context(nc.sbuf_tensor("yT", [P, KD, T], F32))
            sq = keep["w_out"][:, 0:KD // 2].rearrange("p n k c -> p (n k c)").rearrange("p (k t) -> p k t", k=KD)
            x_done, sq_done = back.enter_context(nc.semaphore("x2_done")), back.enter_context(nc.semaphore("sq_y_done"))
            experts(nc, io, keep, g_dram, acts, yT, sq, x_done, sq_done)
            finish(nc, io, keep, yT, sq, x_done, sq_done)


def kernel(**inputs):
    import numpy as np
    import concourse.bacc as bacc
    from concourse.bass_utils import run_bass_kernel_spmd

    nc = bacc.Bacc("TRN2", target_bir_lowering=False, num_devices=1)
    arrays = laid_out(np, inputs)
    io = {n: nc.dram_tensor(f"in_{n}", a.shape, mybir.dt.from_np(a.dtype), kind="ExternalInput").ap() for n, a in arrays.items()}
    io["out"] = nc.dram_tensor("out_0", (P, KD, T), F32, kind="ExternalOutput").ap()
    program(nc, io)
    r = run_bass_kernel_spmd(nc, [{f"in_{n}": a for n, a in arrays.items()}], core_ids=[0])
    out = r.results[0]["out_0"]
    return np.ascontiguousarray(out.transpose(2, 1, 0)).reshape(1, T, D)


def laid_out(np, inputs):
    get = lambda n: np.asarray(inputs[n])
    chunks = lambda w, n: w.reshape(KD, P, w.shape[1] // n, n).transpose(2, 1, 0, 3)
    cols = lambda v: v.reshape(-1, P).T
    w_in = get("w_in")[0]
    at = np.cumsum([0, 512, 512, 512, 256, 256, 512, GLA_RANK, 512])
    part = [w_in[:, a:b] for a, b in zip(at[:-1], at[1:])]
    sq, sk, sv, gq, gk, gv, lr, gr = part
    arrays = {
        "xT": get("x")[0].T.reshape(KD, P, T).transpose(1, 0, 2),
        "cT": cols(get("c")[0]),
        "w_ada": chunks(get("w_ada")[0], 512),
        "b_ada": cols(get("b_ada")[0]),
        "gains": np.concatenate([cols(get("g_sb_norm")[0]), cols(get("g_gla_norm")[0])], axis=1),
        "w_proj": chunks(np.concatenate([sq, sk, gq, gk, gr], axis=1), P),
        "w_lr": chunks(lr, GLA_RANK)[0],
        "w_values": np.concatenate([sv.reshape(KD, P, T), gv.reshape(KD, P, T)]),
        "gate_up": get("w_gla_gate_up")[0],
        "b_gate": cols(get("b_gla_gate")[0]),
        "w_out": chunks(get("w_out")[0], P).transpose(1, 0, 2, 3),
        "w_q": chunks(get("w_peer_q")[0], P),
        "keys_a": get("peer_keys_a")[0].transpose(0, 2, 1),
        "keys_b": get("peer_keys_b")[0].transpose(0, 2, 1),
        "u": get("peer_u")[0].reshape(N_KEYS, P, KD, P).transpose(0, 3, 2, 1),
        "v": get("peer_v")[0].reshape(N_KEYS, P, D),
        "g_final": cols(get("g_final")),
    }
    return {n: np.ascontiguousarray(a) for n, a in arrays.items()}
```
